# Optimizing a Trainium2 kernel written in Bass

```python
import jax, jax.numpy as jnp
from jax import lax
import numpy as np

D_MODEL = 1024
BATCH = 1
SEQ = 1024
DEPTH = 1
DEC_BATCH = 8
DEC_SEQ = 8
PAST_LEN = 1024
PAGE_SIZE = 128

C_CONV = D_MODEL // 2
HEAD_DIM = 64
N_HEADS = D_MODEL // (2 * HEAD_DIM)
N_KV_HEADS = N_HEADS // 2
GROUP = N_HEADS // N_KV_HEADS
N_IDX_HEADS = 16
IDX_DIM = 64
TOPK_MAX = 256
Q_BLOCK = 128
CONV_WIDTH = 31
ROPE_THETA = 500000.0
ROPE_FRACTION = 4
D_MIX = C_CONV + N_HEADS * HEAD_DIM
D_FF = -(-(8 * D_MODEL) // (3 * 256)) * 256
IN_SPLIT_SIZES = (C_CONV, C_CONV, N_HEADS * HEAD_DIM, N_KV_HEADS * HEAD_DIM,
                  N_KV_HEADS * HEAD_DIM, N_IDX_HEADS * IDX_DIM, IDX_DIM)
D_IN = sum(IN_SPLIT_SIZES) + N_IDX_HEADS

kernel_name = 'hymba_conformer_dsa_decoder_step'

def rms_norm(x, g, eps=1e-6):
    xf = x.astype(jnp.float32)
    y = xf * lax.rsqrt(jnp.mean(xf * xf, axis=-1, keepdims=True) + eps)
    return (y * g.astype(jnp.float32)).astype(x.dtype)

def layer_norm(x, g, b, eps=1e-5):
    xf = x.astype(jnp.float32)
    mu = jnp.mean(xf, axis=-1, keepdims=True)
    xc = xf - mu
    y = xc * lax.rsqrt(jnp.mean(xc * xc, axis=-1, keepdims=True) + eps)
    return (y * g.astype(jnp.float32) + b.astype(jnp.float32)).astype(x.dtype)

def rope_partial(x, pos):
    rd = x.shape[-1] // ROPE_FRACTION
    half = rd // 2
    inv_freq = ROPE_THETA ** (-jnp.arange(half, dtype=jnp.float32) / half)
    ang = pos.astype(jnp.float32)[:, None] * inv_freq[None, :]
    cos = jnp.cos(ang)[:, None, :]
    sin = jnp.sin(ang)[:, None, :]
    xr = x[..., :rd].astype(jnp.float32)
    x1, x2 = xr[..., :half], xr[..., half:]
    rot = jnp.concatenate([x1 * cos - x2 * sin, x2 * cos + x1 * sin], axis=-1)
    return jnp.concatenate([rot.astype(x.dtype), x[..., rd:]], axis=-1)

def mixer_inputs(x, pos, norm_g, w_in, q_norm_g, k_norm_g):
    B, T, _ = x.shape
    h = rms_norm(x, norm_g)
    z = jnp.einsum('btd,de->bte', h, w_in)
    offs = np.cumsum(IN_SPLIT_SIZES).tolist()
    u_val, u_gate, q, k, v, qi, ki, wi = jnp.split(z, offs, axis=-1)
    u = u_val * jax.nn.sigmoid(u_gate)
    q = rope_partial(rms_norm(q.reshape(B, T, N_HEADS, HEAD_DIM), q_norm_g), pos)
    k = rope_partial(rms_norm(k.reshape(B, T, N_KV_HEADS, HEAD_DIM), k_norm_g), pos)
    v = v.reshape(B, T, N_KV_HEADS, HEAD_DIM)
    qi = rope_partial(qi.reshape(B, T, N_IDX_HEADS, IDX_DIM), pos)
    ki = rope_partial(ki[:, :, None, :], pos)[:, :, 0, :]
    wi = wi * ((N_IDX_HEADS * IDX_DIM) ** -0.5)
    return u, q, k, v, qi, ki, wi

def conv_mixer(u, past_u, dw_w, dw_b, ln_g, ln_b):
    full = jnp.concatenate([past_u, u], axis=1)
    y = lax.conv_general_dilated(full, dw_w[:, None, :], window_strides=(1,), padding='VALID',
                                 dimension_numbers=('NWC', 'WIO', 'NWC'),
                                 feature_group_count=C_CONV) + dw_b
    y = jax.nn.silu(layer_norm(y, ln_g, ln_b))
    return y, full[:, -(CONV_WIDTH - 1):]

def indexer_topk(qi, wi, ki, q_pos, topk):
    s = jnp.einsum('bthd,bsd->bths', qi.astype(jnp.float32), ki.astype(jnp.float32))
    score = jnp.einsum('bths,bth->bts', jax.nn.relu(s), wi.astype(jnp.float32))
    key_pos = jnp.arange(ki.shape[1], dtype=jnp.int32)
    causal = key_pos[None, :] <= q_pos[:, None]
    score = jnp.where(causal[None], score, -jnp.inf)
    _, sel = lax.top_k(score, topk)
    valid = sel <= q_pos[None, :, None]
    return sel, valid

def sparse_attend(q, k_sel, v_sel, valid):
    B, T = q.shape[:2]
    qg = q.reshape(B, T, N_KV_HEADS, GROUP, HEAD_DIM).astype(jnp.float32)
    s = jnp.einsum('btgrd,btkgd->btgrk', qg, k_sel.astype(jnp.float32)) * (HEAD_DIM ** -0.5)
    s = jnp.where(valid[:, :, None, None, :], s, -jnp.inf)
    p = jax.nn.softmax(s, axis=-1)
    o = jnp.einsum('btgrk,btkgd->btgrd', p, v_sel.astype(jnp.float32))
    return o.reshape(B, T, N_HEADS * HEAD_DIM).astype(q.dtype)

def prompt_attention(q, k, v, qi, wi, ki, topk):
    B, S = q.shape[:2]
    nb = S // Q_BLOCK
    bidx = jnp.arange(B)[:, None, None]

    def to_blocks(a):
        return jnp.moveaxis(a.reshape(B, nb, Q_BLOCK, *a.shape[2:]), 1, 0)

    def one_block(args):
        qb, qib, wib, pos_b = args
        sel, valid = indexer_topk(qib, wib, ki, pos_b, topk)
        return sparse_attend(qb, k[bidx, sel], v[bidx, sel], valid)

    pos = jnp.arange(S, dtype=jnp.int32).reshape(nb, Q_BLOCK)
    out = lax.map(one_block, (to_blocks(q), to_blocks(qi), to_blocks(wi), pos))
    return jnp.moveaxis(out, 0, 1).reshape(B, S, N_HEADS * HEAD_DIM)

def sample_attention(layer, q, k_new, v_new, qi, wi, ki_new, q_pos,
                     cache_k, cache_v, cache_idx_k, page_table, topk):
    DB, T = q.shape[:2]
    past = page_table.shape[1] * PAGE_SIZE
    bidx = jnp.arange(DB)[:, None, None]
    ki_past = cache_idx_k[layer, page_table].reshape(DB, past, IDX_DIM)
    ki_all = jnp.concatenate([ki_past, ki_new.astype(ki_past.dtype)], axis=1)
    sel, valid = indexer_topk(qi, wi, ki_all, q_pos, topk)
    in_past = (sel < past)[..., None, None]
    sp = jnp.minimum(sel, past - 1)
    phys = page_table[bidx, sp // PAGE_SIZE]
    off = sp % PAGE_SIZE
    sn = jnp.clip(sel - past, 0, T - 1)
    k_sel = jnp.where(in_past, cache_k[layer, phys, off], k_new[bidx, sn])
    v_sel = jnp.where(in_past, cache_v[layer, phys, off], v_new[bidx, sn])
    return sparse_attend(q, k_sel, v_sel, valid)

def merge_and_ffn(x, conv_out, attn_out, w_out, ffn_norm_g, w_gate, w_up, w_down):
    mix = jnp.concatenate([conv_out, attn_out.astype(conv_out.dtype)], axis=-1)
    x = x + jnp.einsum('bte,ed->btd', mix, w_out)
    h = rms_norm(x, ffn_norm_g)
    f = jax.nn.silu(jnp.einsum('btd,df->btf', h, w_gate)) * jnp.einsum('btd,df->btf', h, w_up)
    return x + jnp.einsum('btf,fd->btd', f, w_down)

def setup_inputs(seed: int = 0) -> dict:
    key = jax.random.key(seed)
    ks = jax.random.split(key, 24)
    f32 = jnp.float32
    n_pages = PAST_LEN // PAGE_SIZE
    n_used = DEC_BATCH * n_pages
    n_pool = n_used + n_used // 4

    def nrm(k, shape, scale=1.0):
        return jax.random.normal(k, shape, f32) * scale

    page_table = jax.random.permutation(ks[0], n_pool)[:n_used].reshape(DEC_BATCH, n_pages).astype(jnp.int32)
    return {
        'x_prompt': nrm(ks[1], (BATCH, SEQ, D_MODEL)),
        'x_sample': nrm(ks[2], (DEC_BATCH, DEC_SEQ, D_MODEL)),
        'cache_k': nrm(ks[3], (DEPTH, n_pool, PAGE_SIZE, N_KV_HEADS, HEAD_DIM)),
        'cache_v': nrm(ks[4], (DEPTH, n_pool, PAGE_SIZE, N_KV_HEADS, HEAD_DIM)),
        'cache_idx_k': nrm(ks[5], (DEPTH, n_pool, PAGE_SIZE, IDX_DIM)),
        'state_conv': nrm(ks[6], (DEPTH, DEC_BATCH, CONV_WIDTH - 1, C_CONV), 0.5),
        'page_table': page_table,
        'attn_norm_g': 1.0 + nrm(ks[7], (DEPTH, D_MODEL), 0.1),
        'w_in': nrm(ks[8], (DEPTH, D_MODEL, D_IN), D_MODEL ** -0.5),
        'q_norm_g': 1.0 + nrm(ks[9], (DEPTH, HEAD_DIM), 0.1),
        'k_norm_g': 1.0 + nrm(ks[10], (DEPTH, HEAD_DIM), 0.1),
        'conv_dw_w': nrm(ks[11], (DEPTH, CONV_WIDTH, C_CONV), CONV_WIDTH ** -0.5),
        'conv_dw_b': nrm(ks[12], (DEPTH, C_CONV), 0.01),
        'conv_ln_g': 1.0 + nrm(ks[13], (DEPTH, C_CONV), 0.1),
        'conv_ln_b': nrm(ks[14], (DEPTH, C_CONV), 0.01),
        'w_out': nrm(ks[15], (DEPTH, D_MIX, D_MODEL), D_MIX ** -0.5),
        'ffn_norm_g': 1.0 + nrm(ks[16], (DEPTH, D_MODEL), 0.1),
        'w_gate': nrm(ks[17], (DEPTH, D_MODEL, D_FF), D_MODEL ** -0.5),
        'w_up': nrm(ks[18], (DEPTH, D_MODEL, D_FF), D_MODEL ** -0.5),
        'w_down': nrm(ks[19], (DEPTH, D_FF, D_MODEL), D_FF ** -0.5),
    }

def reference(x_prompt, x_sample, cache_k, cache_v, cache_idx_k, state_conv, page_table,
              attn_norm_g, w_in, q_norm_g, k_norm_g, conv_dw_w, conv_dw_b, conv_ln_g, conv_ln_b,
              w_out, ffn_norm_g, w_gate, w_up, w_down):
    B, S = x_prompt.shape[:2]
    DB, T = x_sample.shape[:2]
    past = page_table.shape[1] * PAGE_SIZE
    topk_p = min(TOPK_MAX, S // 4)
    topk_s = min(TOPK_MAX, (past + T) // 4)
    pos_p = jnp.arange(S, dtype=jnp.int32)
    pos_s = past + jnp.arange(T, dtype=jnp.int32)

    xp, xs = x_prompt, x_sample
    kp_l, vp_l, ip_l, cp_l, ks_l, vs_l, is_l, cs_l = [], [], [], [], [], [], [], []
    for l in range(DEPTH):
        u, q, k, v, qi, ki, wi = mixer_inputs(xp, pos_p, attn_norm_g[l], w_in[l], q_norm_g[l], k_norm_g[l])
        zero_buf = jnp.zeros((B, CONV_WIDTH - 1, C_CONV), u.dtype)
        conv_out, conv_state = conv_mixer(u, zero_buf, conv_dw_w[l], conv_dw_b[l], conv_ln_g[l], conv_ln_b[l])
        attn_out = prompt_attention(q, k, v, qi, wi, ki, topk_p)
        xp = merge_and_ffn(xp, conv_out, attn_out, w_out[l], ffn_norm_g[l], w_gate[l], w_up[l], w_down[l])
        kp_l.append(k); vp_l.append(v); ip_l.append(ki); cp_l.append(conv_state)

        u, q, k, v, qi, ki, wi = mixer_inputs(xs, pos_s, attn_norm_g[l], w_in[l], q_norm_g[l], k_norm_g[l])
        conv_out, conv_state = conv_mixer(u, state_conv[l].astype(u.dtype), conv_dw_w[l], conv_dw_b[l],
                                          conv_ln_g[l], conv_ln_b[l])
        attn_out = sample_attention(l, q, k, v, qi, wi, ki, pos_s, cache_k, cache_v, cache_idx_k,
                                    page_table, topk_s)
        xs = merge_and_ffn(xs, conv_out, attn_out, w_out[l], ffn_norm_g[l], w_gate[l], w_up[l], w_down[l])
        ks_l.append(k); vs_l.append(v); is_l.append(ki); cs_l.append(conv_state)

    return (xp, xs,
            jnp.stack(kp_l), jnp.stack(vp_l), jnp.stack(ip_l), jnp.stack(cp_l),
            jnp.stack(ks_l), jnp.stack(vs_l), jnp.stack(is_l), jnp.stack(cs_l))


_drawn_inputs = setup_inputs


def setup_inputs(seed=0):
    import zlib

    import numpy as np

    out = dict(_drawn_inputs(seed))
    spreads = {}
    factors = {'q_norm_g': 5.734, 'conv_dw_b': 6.399, 'conv_ln_b': 8.0}
    for name, (base, spread) in spreads.items():
        noise = np.random.default_rng([zlib.crc32(name.encode()), seed]).standard_normal(out[name].shape)
        drawn = base * np.exp(spread * noise) if base else spread * noise
        out[name] = __import__('jax').numpy.asarray(drawn.astype(out[name].dtype))
    for name, factor in factors.items():
        out[name] = (out[name] * factor).astype(out[name].dtype)
    return out
```

```python
from contextlib import ExitStack

import numpy as np

import concourse.bass as bass
from concourse import mybir

F32 = mybir.dt.float32
F32R = mybir.dt.float32r
BF16 = mybir.dt.bfloat16
I32 = mybir.dt.int32
ALU = mybir.AluOpType
ACT = mybir.ActivationFunctionType
AX_X = mybir.AxisListType.X

P = 128
D = 1024
S = 1024
NS, TS = 8, 8
PAST, PAGE = 1024, 128
NPG = PAST // PAGE
C = 512
NH, NKV, HD = 8, 4, 64
NI, ID = 16, 64
TOPK = 256
W = 31
F = 2816
KT = D // P
CT = C // P
SR = NS * TS
ROWS = S + SR
NT = S // P + 1
SAMPLE = NT - 1
SKEYS = PAST + TS
FIRST = TOPK // P
NSEL = S // P - FIRST

U_VAL, U_GATE, Q_AT, KV_AT = 0, C, 2 * C, 2 * C + NH * HD
QI_AT = KV_AT + 2 * NKV * HD
KI_AT = QI_AT + NI * ID
KIW = ID + NI

FAR = -2.0e38
TAKEN = -3.0e38
DROP = -1.0e30
RMS_EPS, LN_EPS = 1e-6, 1e-5

RAW, SLOTS = 2, 6
N_KIW, N_QI, N_KV, N_Q, N_U, N_OUT, N_FFN = 0, 1, 9, 13, 17, 25, 33
FG = F // P // 2
BLOCKS = [(0, 384), (384, 768), (768, ROWS)]

ALL = [SAMPLE] + list(range(S // P))
SEL = [SAMPLE] + list(range(FIRST, S // P))
CHUNKS = [ALL, SEL, SEL, ALL, ALL, ALL, ALL]
BASE = [sum(len(c) for c in CHUNKS[:i]) for i in range(8)]

def rows_of(t):
    return SR if t == SAMPLE else P

def cols_of(t):
    return slice(t * P, t * P + rows_of(t))

def acc_at(t):
    return sum((j + 1) * P for j in range(FIRST, t))

def dve_parts(n):
    return max(0, n + 1 - 4 * NH)

def mask_at(t):
    return sum((j + 1) * P for j in range(t))

K_ID, K_TRI, K_COS, K_SIN = 0, P, 2 * P, 2 * P + NT * 16
K_M = K_SIN + NT * 16
K_E = K_M + SR
K_NEW = K_E + P
K_GQ = K_NEW + TS
K_GK = K_GQ + HD
K_CW = K_GK + HD
K_CB = K_CW + CT * W
K_LG = K_CB + CT
K_LB = K_LG + CT
K_END = K_LB + CT

def shape_constants():
    f = np.zeros((P, K_END), np.float32)
    f[:, K_ID:K_ID + P] = np.eye(P)
    after = np.arange(P)[None, :] > np.arange(P)[:, None]
    f[:, K_TRI:K_TRI + P] = np.where(after, FAR, 0.0)
    half = HD // 8
    inv = (500000.0 ** (-np.arange(half, dtype=np.float32) / half)).astype(np.float32)
    pos = np.arange(S, dtype=np.float32).reshape(S // P, P).T
    pos = np.concatenate([pos, np.zeros((P, 1), np.float32)], 1)
    pos[:SR, SAMPLE] = PAST + np.arange(SR) % TS
    ang = (pos[:, :, None] * inv).astype(np.float32).astype(np.float64)
    cos, sin = np.cos(ang), np.sin(ang)
    f[:, K_COS:K_SIN] = np.concatenate([cos, cos], 2).reshape(P, -1)
    f[:, K_SIN:K_M] = np.concatenate([-sin, sin], 2).reshape(P, -1)
    r, c = np.arange(P)[:, None], np.arange(SR)[None, :]
    f[:, K_M:K_M + SR] = r % TS == c % TS
    f[:NI, K_E:K_E + P] = np.arange(NI)[:, None] == np.arange(P)[None, :] // TS
    f[:SR, K_NEW:K_NEW + TS] = np.where(np.arange(TS)[None, :] > np.arange(SR)[:, None] % TS, FAR, 0.0)
    b = np.zeros((P, P + NS * SR), np.float32)
    b[:, 0:P] = np.where(after, DROP, 0.0)
    bt, s, gt = np.arange(SR)[:, None, None], np.arange(NS)[None, :, None], np.arange(SR)[None, None, :]
    b[:SR, P:] = ((bt // TS == s) & (bt % TS == gt % TS)).reshape(SR, -1)
    return f, b

def decoder_program(nc, A, O):
    ctx = ExitStack()
    with ctx:
        def sb(name, shape, dt=F32):
            return ctx.enter_context(nc.sbuf_tensor(name, shape, dt))

        def sem(name):
            return ctx.enter_context(nc.semaphore(name))

        hi_t = sb("hi_t", [P, KT, ROWS], F32R)
        lo_t = sb("lo_t", [P, KT, ROWS], F32R)
        w_hi = sb("w_hi", [P, SLOTS, D], F32R)
        w_lo = sb("w_lo", [P, SLOTS, D], F32R)
        w_raw = sb("w_raw", [P, RAW, D])
        kf = sb("kf", [P, K_END])
        kb = sb("kb", [P, P + NS * SR], BF16)
        half_neg = sb("half_neg", [P, 384])
        ms = sb("ms", [P, 2 * NT])
        rs = sb("rs", [P, 2 * NT])
        hs = sb("hs", [P, 4, 8])
        rt = sb("rt", [P, 2, NT * 16])
        wi_tok = sb("wi_tok", [P, NT, NI])
        wts = sb("wts", [NI, SR])
        kin_t = sb("kin_t", [ID, SR])
        m8 = sb("m8", [P, 8])
        ones = sb("ones", [P, P])
        stat = sb("stat", [P, 2, 16])
        mx = sb("mx", [P, 2])
        rinv = sb("rinv", [P, 8])
        pages = sb("pages", [1, NS * NPG], I32)

        arena = (nc.sbuf_base + 31) // 32 * 32
        room = nc.sbuf_usable_end - arena

        def at(name, off, shape, dt=F32):
            return nc.alloc_sbuf_tensor_at(name, shape, dt, offset=arena + off)

        xin = at("xin", 0, [P, 3, D])
        xn = at("xn", 12288, [P, 2, D])
        sq = at("sq", 20480, [P, D])
        gbc = at("gbc", 24576, [P, D])
        qi_tok = at("qi_tok", 0, [P, NSEL + 1, D])
        qi_t = at("qi_t", 28672, [P, 2, 8, P])
        ki_t = at("ki_t", 36864, [P, S])
        acc = at("acc", 40960, [P, acc_at(S // P)])
        sacc = at("sacc", 57856, [SR, SKEYS])
        w_all = at("w_all", 57856, [P, NS, SR])
        rl = at("rl", 61984, [P, 2, SKEYS])
        kiw = at("kiw", 71200, [P, NT, KIW])
        kis_t = [at(f"kis_t{i}", 4128 * i, [ID, SKEYS]) for i in range(2)]
        qis_t = at("qis_t", 8256, [ID, NS, NI, TS])
        mneg = at("mneg", 0, [P, mask_at(S // P)], BF16)
        smneg = at("smneg", 9216, [SR, SKEYS], BF16)
        v_tok = at("v_tok", 11296, [P, NT, NKV * HD])
        k_t = at("k_t", 20512, [P, 2, ROWS])
        qst = at("qst", 29216, [P, 3, NH * HD])
        hsq = at("hsq", 35360, [P, NH * HD])
        sig = at("sig", 37408, [P, 2, 384])
        k_tok = at("k_tok", 61984, [P, NT, NKV * HD])
        PU = W - 1
        UC = PU + S + NS * (PU + TS)
        u = at("u", 61984, [P, 2, UC])
        y = at("y", 40960, [P, CT, ROWS])
        u_last = at("u_last", 29216, [P, CT, PU + SR])
        cst = at("cst", 30720, [SR, 2, C])
        ysq = at("ysq", 61984, [P, CT, 384])
        lnr = at("lnr", 68128, [P, 384])
        sm = at("sm", 40960, [P, 3, S])
        pt = at("pt", 53248, [P, 2, S])
        q_ld = at("q_ld", 61440, [P, 2, NH * HD])
        q_t = at("q_t", 65536, [P, 2, 4, P])
        o_tok = at("o_tok", 69632, [P, NH * HD])
        kt_b = [at("kt_b0", 29216, [P, 2, SKEYS]), at("kt_b1", 37472, [P, 2, SKEYS])]
        v_b = [at("v_b0", 45728, [P, NPG, NKV * HD]), at("v_b1", 53920, [P, NPG, NKV * HD])]
        p_s = at("p_s", 62112, [P, SKEYS])
        pt_s = at("pt_s", 66240, [P, NPG + 1, P])
        o_s = at("o_s", 70848, [P, NKV * HD])
        v_new = at("v_new", 0, [TS, NS, NKV * HD])
        q_blk = at("q_blk", 11296, [P, NS, 2, SR])
        o_st = at("o_st", 15392, [P, 2, 4, P])
        mix_s = at("mix_s", 19488, [P, CT, SR])
        x1 = at("x1", 0, [P, NT, D])
        xn1 = at("xn1", 36864, [P, 2, D])
        sq1 = at("sq1", 45056, [P, D])
        gbc1 = at("gbc1", 49152, [P, D])
        f_hi = at("f_hi", 36864, [P, 2, ROWS], F32R)
        f_lo = at("f_lo", 45568, [P, 2, ROWS], F32R)
        sg = at("sg", 54272, [P, 2, 384])
        ff = at("ff", 57344, [P, 2, 384])
        assert 71200 + NT * KIW * 4 <= room, room

        q_scr = nc.dram_tensor("q_scratch", [NT, P, NH * HD], F32, kind="Internal").ap()

        ps = ctx.enter_context(nc.psum_tensor("ps", [P, 8, 512], F32))

        def wide(b, n, r=slice(0, P)):
            return ps[r, b:b + -(-n // 512), :].rearrange("p a b -> p (a b)")[:, 0:n]

        consts_in = sem("consts_in")
        consts_made = sem("consts_made")
        x_in = [sem(f"x_in{i}") for i in range(3)]
        g_in = sem("g_in")
        x1_in = sem("x1_in")
        ms_ready = sem("ms_ready")
        rs_ready = sem("rs_ready")
        xn_ready = sem("xn_ready")
        xt_done = sem("xt_done")
        hi_ready = sem("hi_ready")
        lo_ready = sem("lo_ready")
        raw_in = [sem(f"raw_in{i}") for i in range(RAW)]
        split_hi = sem("split_hi")
        split_lo = sem("split_lo")
        w_used = sem("w_used")
        proj_done = sem("proj_done")
        proj_evac = sem("proj_evac")
        dve_step = sem("dve_step")
        act_step = sem("act_step")
        pool_step = sem("pool_step")
        kiw_ready = sem("kiw_ready")
        qi_ready = sem("qi_ready")
        kit_ps = sem("kit_ps")
        kit_ready = sem("kit_ready")
        wx_done = sem("wx_done")
        wall_ready = sem("wall_ready")
        qit_ps = sem("qit_ps")
        qit_ready = sem("qit_ready")
        idx_mm = sem("idx_mm")
        relu_done = sem("relu_done")
        acc_done = sem("acc_done")
        kis_in = [sem(f"kis_in{i}") for i in range(2)]
        kin_done = sem("kin_done")
        qist_ps = sem("qist_ps")
        qist_ready = sem("qist_ready")
        sidx_mm = sem("sidx_mm")
        srelu_done = sem("srelu_done")
        sw_mm = sem("sw_mm")
        head_ms = sem("head_ms")
        head_rs = sem("head_rs")
        head_sq = sem("head_sq")
        k_ready = sem("k_ready")
        q_ready = sem("q_ready")
        q_out = [sem(f"q_out{i}") for i in range(3)]
        kt_ps = sem("kt_ps")
        kt_ready = sem("kt_ready")
        masks_ready = sem("masks_ready")
        u_mm = sem("u_mm")
        glu_sig = sem("glu_sig")
        glu_mul = sem("glu_mul")
        u_state = [sem(f"u_state{i}") for i in range(2)]
        ut_ps = sem("ut_ps")
        ulast_ready = sem("ulast_ready")
        cst_ready = sem("cst_ready")
        cst_out = sem("cst_out")
        conv_done = sem("conv_done")
        mean_mm = sem("mean_mm")
        yc_ready = sem("yc_ready")
        ysq_ready = sem("ysq_ready")
        var_mm = sem("var_mm")
        lnv_ready = sem("lnv_ready")
        lnr_ready = sem("lnr_ready")
        yn_ready = sem("yn_ready")
        silu_done = sem("silu_done")
        mixc_hi = sem("mixc_hi")
        mixc_lo = sem("mixc_lo")
        q_in = [sem(f"q_in{i}") for i in range(2)]
        qt_ps = sem("qt_ps")
        qt_ready = sem("qt_ready")
        qk_done = sem("qk_done")
        sm_done = sem("sm_done")
        nmax = sem("nmax")
        exp_done = sem("exp_done")
        pt_ps = sem("pt_ps")
        pt_act = sem("pt_act")
        pt_dve = sem("pt_dve")
        pv_done = sem("pv_done")
        o_ready = sem("o_ready")
        ot_ps = sem("ot_ps")
        mixa_hi = sem("mixa_hi")
        mixa_lo = sem("mixa_lo")
        kv_in = [sem(f"kv_in{i}") for i in range(2)]
        vn_in = sem("vn_in")
        qblk_ready = sem("qblk_ready")
        sqt_ps = sem("sqt_ps")
        ktn_ready = sem("ktn_ready")
        sqk_done = sem("sqk_done")
        smax = sem("smax")
        sexp_done = sem("sexp_done")
        spt_ps = sem("spt_ps")
        spt_ready = sem("spt_ready")
        spv_done = sem("spv_done")
        so_ready = sem("so_ready")
        sot_ps = sem("sot_ps")
        sot_ready = sem("sot_ready")
        mixs_ready = sem("mixs_ready")
        mixs_hi = sem("mixs_hi")
        mixs_lo = sem("mixs_lo")
        x1_ready = sem("x1_ready")
        gate_mm = sem("gate_mm")
        up_mm = sem("up_mm")
        silu_f = sem("silu_f")
        f_ready = sem("f_ready")
        f_hi_ready = sem("f_hi_ready")
        f_lo_ready = sem("f_lo_ready")
        down_mm = sem("down_mm")
        y_added = sem("y_added")
        stores = sem("stores")
        fence_pool = sem("fence_pool")
        fence_dve = sem("fence_dve")

        ident = kf[:, K_ID:K_ID + P]
        nsteps = NSEL * NI
        ck = A["cache_kt"]
        SQ = SR // 2

        block = ctx.enter_context(nc.Block())

        @block.sync
        def _(sp):
            def unit_source(n):
                if n < N_QI:
                    return A["w_in"][:, KI_AT:KI_AT + KIW].rearrange("(k p) n -> p k n", p=P)
                if n < N_U:
                    c, pair = divmod(n - N_QI, 4)
                    col = [QI_AT, QI_AT + 512, KV_AT, Q_AT][c]
                    return A["w_in"][pair * 256:pair * 256 + 256, col:col + 512].rearrange("(k p) n -> p k n", p=P)
                if n < N_OUT:
                    ct, g = divmod(n - N_U, 2)
                    col = (U_GATE if g else U_VAL) + ct * P
                    return A["w_in"][:, col:col + P].rearrange("(k p) n -> p k n", p=P)
                c, pair = divmod(n - N_OUT, 4)
                return A["w_out"][pair * 256:pair * 256 + 256, c * 512:c * 512 + 512].rearrange(
                    "(k p) n -> p k n", p=P)

            def load_unit(n):
                if n >= RAW:
                    sp.wait_ge(split_lo, n - RAW + 1)
                dst = w_raw[:, n % RAW, :]
                if n < N_QI:
                    dst = dst[:, 0:KT * KIW].rearrange("p (k n) -> p k n", k=KT)
                elif N_U <= n < N_OUT:
                    dst = dst.rearrange("p (k n) -> p k n", k=KT)
                else:
                    dst = dst.rearrange("p (k n) -> p k n", k=2)
                sp.dma_start(dst, unit_source(n)).then_inc(raw_in[n % RAW], 16)

            def load_x(o):
                t = ALL[o]
                if o >= 3:
                    sp.wait_ge(xn_ready, o - 2)
                src = A["x_sample"] if t == SAMPLE else A["x_prompt"][cols_of(t), :]
                sp.dma_start(xin[0:rows_of(t), o % 3, :], src).then_inc(x_in[o % 3], 16)

            load_x(0)
            sp.dma_start(gbc[:, :], A["attn_norm_g"].broadcast_to([P, D])).then_inc(g_in, 16)
            load_x(1)
            load_x(2)
            sp.dma_start(kf[:, :], A["kf"]).then_inc(consts_in, 16)
            sp.dma_start(pages[:, :], A["page_table"]).then_inc(consts_in, 16)
            sp.dma_start(kb[:, :], A["kb"]).then_inc(consts_in, 16)
            load_unit(0)
            load_unit(1)
            for o in range(3, NT):
                load_x(o)
            sp.dma_start(O["conv_sample"][:, 0:PU - TS, :], A["state"][:, TS:PU, :]).then_inc(cst_out, 16)
            for n in range(2, 17):
                load_unit(n)
            sp.wait_ge(consts_in, 48)
            sp.wait_ge(qit_ps, NSEL)
            for b in range(NS):
                if b >= 2:
                    sp.wait_ge(sidx_mm, b - 1)
                for j in range(NPG):
                    pg = sp.value_load(pages[0:1, b * NPG + j:b * NPG + j + 1], min_val=0,
                                       max_val=ck.shape[0] - 1)
                    sp.dma_start(kis_t[b % 2][:, j * PAGE:(j + 1) * PAGE],
                                 A["cache_it"][bass.ds(pg, 1)].rearrange("o d s -> d (o s)")
                                 ).then_inc(kis_in[b % 2], 16)
            def load_states(ct):
                if ct == 0:
                    sp.wait_ge(kt_ready, 3)
                    sp.wait_ge(stores, 16 * 6)
                if ct >= 2:
                    sp.wait_ge(conv_done, 2 * (ct - 1))
                dst = u[:, ct % 2, PU + S:].rearrange("p (b w) -> p b w", b=NS)[:, :, 0:PU]
                sp.dma_start(dst, A["state_t"][ct * P:(ct + 1) * P]).then_inc(u_state[ct % 2], 16)

            for n in range(17, 21):
                load_unit(n)
            load_states(0)
            load_states(1)
            for n in range(21, 25):
                load_unit(n)
            load_states(2)
            load_states(3)
            def load_q(i):
                if i == 0:
                    sp.wait_ge(mixc_lo, len(BLOCKS))
                    sp.wait_ge(mixc_hi, len(BLOCKS))
                    for r in range(3):
                        sp.wait_ge(q_out[r], 48)
                if i >= 2:
                    sp.wait_ge(qt_ps, i - 1)
                r = rows_of(i)
                sp.dma_start(q_ld[0:r, i % 2, :], q_scr[i, 0:r, :]).then_inc(q_in[i % 2], 16)

            for n in range(25, 33):
                load_unit(n)
            for i in range(S // P + 1):
                load_q(i)
            sp.wait_ge(mixa_lo, S // P)
            sp.wait_ge(mixa_hi, S // P)
            sp.wait_ge(cst_out, 16 * 3)
            sp.dma_start(v_new[:, :, :], O["v_sample"].rearrange("b t c -> t b c")).then_inc(vn_in, 16)
            for b in range(NS):
                if b >= 2:
                    sp.wait_ge(spv_done, b - 1)
                for j in range(NPG):
                    pg = sp.value_load(pages[0:1, b * NPG + j:b * NPG + j + 1], min_val=0,
                                       max_val=ck.shape[0] - 1)
                    sp.dma_start(kt_b[b % 2][:, :, j * PAGE:(j + 1) * PAGE],
                                 ck[bass.ds(pg, 1)].rearrange("o (a p) s -> p (o a) s", a=2)
                                 ).then_inc(kv_in[b % 2], 16)
                    sp.dma_start(v_b[b % 2][:, j, :],
                                 A["cache_v"][bass.ds(pg, 1)].rearrange("o s c -> s (o c)")
                                 ).then_inc(kv_in[b % 2], 16)
            sp.wait_ge(mixs_lo, 1)
            sp.wait_ge(mixs_hi, 1)
            sp.dma_start(x1[:, 0:SAMPLE, :], A["x_prompt"].rearrange("(t p) d -> p t d", p=P)).then_inc(x1_in, 16)
            sp.dma_start(x1[0:SR, SAMPLE, :], A["x_sample"]).then_inc(x1_in, 16)
            sp.dma_start(gbc1[:, :], A["ffn_norm_g"].broadcast_to([P, D])).then_inc(g_in, 16)
            gv = A["w_gate"].rearrange("(k p) f -> p k f", p=P)
            uv = A["w_up"].rearrange("(k p) f -> p k f", p=P)
            with sp.Fori(0, FG) as g:
                for j in range(6):
                    sp.wait_ge(split_lo, g * 6 + (N_FFN + j - RAW + 1))
                    slot = (N_FFN + j) % RAW
                    c = 2 * g + (j // 2 if j < 4 else j - 4)
                    if j < 4:
                        sp.dma_start(w_raw[:, slot, :].rearrange("p (k n) -> p k n", k=KT),
                                     (gv, uv)[j % 2][:, :, bass.ds(c * P, P)]).then_inc(raw_in[slot], 16)
                    else:
                        sp.dma_start(w_raw[:, slot, :], A["w_down"][bass.ds(c * P, P), :]).then_inc(raw_in[slot], 16)
            for o in range(NT):
                t = ALL[o]
                sp.wait_ge(y_added, 1 + 2 * NT * (FG - 1) + 2 * o + 2)
                dst = O["y_sample"] if t == SAMPLE else O["y_prompt"][cols_of(t), :]
                sp.dma_start(dst, x1[0:rows_of(t), t, :]).then_inc(stores, 16)
            sp.wait_ge(stores, 16 * (6 + NT))

        @block.gpsimd
        def _(pool):
            pool.memset(half_neg[:, :], -0.5).then_inc(pool_step, 1)
            pool.memset(w_all[:, :, :], 0.0).then_inc(consts_made, 1)
            pool.memset(ones[:, :], 1.0 / C).then_inc(consts_made, 1)

            def width(n):
                return KT * KIW if n == 0 else D

            def used(n):
                if n == 0:
                    return proj_done, BASE[1]
                if N_U <= n < N_OUT:
                    return u_mm, 3 * (n - N_U + 1)
                c, i = divmod(n - N_QI, 4) if n < N_U else divmod(n - N_OUT, 4)
                late = 0 if n < N_U else 4
                return (w_used, 3 * (c + late) + i + 1) if i < 3 else (proj_done, BASE[c + late + 2])

            def split(n):
                w = width(n)
                pool.wait_ge(raw_in[n % RAW], 16 * (n // RAW + 1))
                if n >= SLOTS:
                    pool.wait_ge(*used(n - SLOTS))
                pool.tensor_copy(w_hi[:, n % SLOTS, 0:w], w_raw[:, n % RAW, 0:w]).then_inc(split_hi, 1)
                pool.wait_ge(split_hi, n + 1)
                pool.tensor_tensor(w_lo[:, n % SLOTS, 0:w], w_raw[:, n % RAW, 0:w],
                                   w_hi[:, n % SLOTS, 0:w].bitcast(F32), ALU.subtract).then_inc(split_lo, 1)

            def row_rs(q, r, width_):
                pool.wait_ge(ms_ready, q + 1)
                pool.tensor_scalar(rs[0:r, q:q + 1], ms[0:r, q:q + 1], 1.0 / width_, RMS_EPS,
                                   ALU.mult, ALU.add).then_inc(pool_step, 1)
                pool.wait_ge(pool_step, q + 2)
                pool.tensor_tensor(rs[0:r, q:q + 1], rs[0:r, q:q + 1], half_neg[0:r, 0:1],
                                   ALU.pow).then_inc(rs_ready, 1)

            def head_inverse(n, r, heads):
                pool.wait_ge(head_ms, n + 1)
                pool.tensor_tensor(hs[0:r, 2 + n % 2, 0:heads], hs[0:r, n % 2, 0:heads],
                                   half_neg[0:r, 0:heads], ALU.pow).then_inc(head_rs, 1)

            for o in range(NT):
                row_rs(o, rows_of(ALL[o]), D)
                if o % 3 == 1:
                    split(o // 3)
            for n in range(3, 15):
                split(n)
            for n in range(2 * NT):
                if n % NT == 5:
                    for m in (range(15, 19) if n < NT else range(19, 21)):
                        split(m)
                head_inverse(n, rows_of(ALL[n % NT]), NKV if n < NT else NH)
            for n in range(21, 25):
                split(n)
            for n in range(25, 31):
                split(n)
            for k in range(len(BLOCKS)):
                a, b = BLOCKS[k]
                pool.wait_ge(lnv_ready, k + 1)
                pool.tensor_tensor(lnr[:, 0:b - a], lnr[:, 0:b - a], half_neg[:, 0:b - a],
                                   ALU.pow).then_inc(lnr_ready, 1)
            for n in range(31, 33):
                split(n)
            for o in range(NT):
                row_rs(NT + o, rows_of(ALL[o]), D)
            for j in range(6):
                split(N_FFN + j)
            with pool.Fori(0, FG - 1) as g:
                for j in range(6):
                    n = N_FFN + 6 + j
                    slot, raw = n % SLOTS, n % RAW
                    pool.wait_ge(raw_in[raw], g * 48 + 16 * (n // RAW + 1))
                    if j < 4:
                        pool.wait_ge((gate_mm, up_mm)[j % 2], g * 6 + 3 * (j // 2 + 1))
                    elif j == 4:
                        pool.wait_ge(w_used, g + (3 * 6 + 1))
                    else:
                        pool.wait_ge(down_mm, g * (2 * NT) + (2 * NT + 1))
                    pool.sem_inc(fence_pool, 1)
                    pool.tensor_copy(w_hi[:, slot, :], w_raw[:, raw, :]).then_inc(split_hi, 1)
                    pool.wait_ge(split_hi, g * 6 + (n + 1))
                    pool.tensor_tensor(w_lo[:, slot, :], w_raw[:, raw, :], w_hi[:, slot, :].bitcast(F32),
                                       ALU.subtract).then_inc(split_lo, 1)

        @block.tensor
        def _(pe):
            def unit(n, k, width_):
                s = slice(k * width_, (k + 1) * width_)
                return w_hi[:, n % SLOTS, s], w_lo[:, n % SLOTS, s]

            def three(out, a_hi, a_lo, b_hi, b_lo, first, last):
                pe.matmul(out, a_hi, b_hi, start=first, stop=False)
                pe.matmul(out, a_hi, b_lo, start=False, stop=False)
                return pe.matmul(out, a_lo, b_hi, start=False, stop=last)

            def transpose_rows(q, src, r):
                pe.wait_ge(xn_ready, q + 1)
                if q % NT >= 4:
                    pe.wait_ge(hi_ready, q - 3)
                    pe.wait_ge(lo_ready, q - 3)
                for k in range(KT):
                    b = 2 * (q % NT % 4) + k // 4
                    mm = pe.transpose(ps[:, b, (k % 4) * P:(k % 4) * P + r], src[:, k * P:(k + 1) * P],
                                      ident[0:r, 0:r])
                mm.then_inc(xt_done, 1)

            def last_in_bank(c, t):
                first = 5 if c >= 5 else 0
                if t == 4:
                    return BASE[c] - BASE[first] + 1
                b = 4 if t == SAMPLE else t
                if c == first or b not in CHUNKS[c - 1]:
                    return None
                return BASE[c - 1] - BASE[first] + CHUNKS[c - 1].index(b) + 1

            def project(c, n0, width_, evac):
                tiles = CHUNKS[c]
                groups = [tiles[0:1], [t for t in tiles[1:] if t < 4], [t for t in tiles[1:] if t >= 4]]
                units = 1 if n0 == 0 else 4
                per = KT // units
                for gi, group in enumerate(groups):
                    for t in group:
                        before = last_in_bank(c, t)
                        if before is not None:
                            pe.wait_ge(evac, before)
                    for k in range(KT):
                        n = n0 + k // per
                        if gi == 0 and k % per == 0:
                            pe.wait_ge(split_lo, n + 1)
                        w = unit(n, k % per, width_)
                        for t in group:
                            r = rows_of(t)
                            out = ps[0:r, 4 if t == SAMPLE else t, 0:width_]
                            mm = three(out, hi_t[:, k, cols_of(t)], lo_t[:, k, cols_of(t)], *w, k == 0, k == KT - 1)
                            if k == KT - 1:
                                mm.then_inc(proj_done, 1)
                        if gi == 2 and k % per == per - 1 and k < KT - 1:
                            mm.then_inc(w_used, 1)

            pe.wait_ge(consts_in, 48)
            for o in range(NT):
                transpose_rows(o, xn[0:rows_of(ALL[o]), o % 2, :], rows_of(ALL[o]))
            pe.wait_ge(hi_ready, NT)
            pe.wait_ge(lo_ready, NT)
            project(0, N_KIW, KIW, proj_evac)
            project(1, N_QI, 512, proj_evac)
            project(2, N_QI + 4, 512, proj_evac)
            pe.wait_ge(proj_evac, BASE[3])
            pe.wait_ge(kiw_ready, 1)
            for t in range(S // P):
                pe.transpose(ps[0:ID, 6 + t // 4, (t % 4) * P:(t % 4 + 1) * P], kiw[:, t, 0:ID], ident)
            pe.transpose(ps[0:ID, 5, 0:SR], kiw[0:SR, SAMPLE, 0:ID], ident[0:SR, 0:SR])
            pe.transpose(ps[0:NI, 5, SR:2 * SR], wi_tok[0:SR, SAMPLE, :], ident[0:SR, 0:SR]).then_inc(kit_ps, 1)
            pe.wait_ge(kit_ready, 6)
            pe.matmul(ps[:, 5, 0:SR], kf[0:NI, K_E:K_E + P], wts[:, :], start=True, stop=True).then_inc(wx_done, 1)
            pe.wait_ge(wall_ready, 1)

            def index_transposes(i):
                pe.wait_ge(qi_ready, 2 * (NSEL + 1))
                if i > 0:
                    pe.wait_ge(qit_ready, 2 * i)
                for j in range(8):
                    mm = pe.transpose(ps[:, 6 + j // 4, (j % 4) * P:(j % 4 + 1) * P],
                                      qi_tok[:, i, j * P:(j + 1) * P], ident)
                mm.then_inc(qit_ps, 1)

            index_transposes(0)
            for i in range(NSEL):
                keys = (FIRST + i + 1) * P
                pe.wait_ge(qit_ready, 2 * i + 2)
                for h in range(NI):
                    n = i * NI + h
                    if n >= 3:
                        pe.wait_ge(relu_done, n - 2)
                    half = slice((h % 2) * ID, (h % 2 + 1) * ID)
                    for a in range(0, keys, 512):
                        w = min(512, keys - a)
                        mm = pe.matmul(ps[:, 2 * (n % 3) + a // 512, 0:w], qi_t[half, i % 2, h // 2, :],
                                       ki_t[half, a:a + w], start=True, stop=True)
                    mm.then_inc(idx_mm, 1)
                    if h == 3 and i + 1 < NSEL:
                        index_transposes(i + 1)
            pe.wait_ge(qit_ready, 2 * NSEL)
            for h in range(NI):
                mm = pe.transpose(ps[0:ID, 6 + h // 8, (h % 8) * SR:(h % 8 + 1) * SR],
                                  qi_tok[0:SR, NSEL, h * ID:(h + 1) * ID], ident[0:SR, 0:SR])
            mm.then_inc(qist_ps, 1)
            pe.wait_ge(qist_ready, 2)
            pe.wait_ge(relu_done, nsteps)
            KB = [(0, 512), (512, 1024), (1024, SKEYS)]

            def weigh(b):
                pe.wait_ge(srelu_done, b + 1)
                for j, (a, z) in enumerate(KB):
                    mm = pe.matmul(ps[0:SR, 3 + j, 0:z - a], w_all[:, b, :], rl[:, b % 2, a:z],
                                   start=(b == 0), stop=(b == NS - 1))
                mm.then_inc(sw_mm, 1)

            for b in range(NS):
                pe.wait_ge(kis_in[b % 2], 16 * NPG * (b // 2 + 1))
                pe.wait_ge(kin_done, b + 1)
                if b > 0:
                    pe.wait_ge(srelu_done, b)
                for j, (a, z) in enumerate(KB):
                    mm = pe.matmul(ps[:, j, 0:z - a], qis_t[:, b, :, :].rearrange("p h t -> p (h t)"),
                                   kis_t[b % 2][:, a:z], start=True, stop=True)
                mm.then_inc(sidx_mm, 1)
                if b > 0:
                    weigh(b - 1)
            weigh(NS - 1)
            pe.wait_ge(masks_ready, 1)
            project(3, N_KV, 512, proj_evac)
            project(4, N_Q, 512, proj_evac)
            pe.wait_ge(proj_evac, BASE[5])
            pe.wait_ge(k_ready, NT)
            for t in range(S // P):
                for p in range(2):
                    pe.transpose(ps[:, 2 * p + t // 4, (t % 4) * P:(t % 4 + 1) * P],
                                 k_tok[:, t, p * P:(p + 1) * P], ident)
            for p in range(2):
                mm = pe.transpose(ps[:, 4, p * SR:(p + 1) * SR], k_tok[0:SR, SAMPLE, p * P:(p + 1) * P],
                                  ident[0:SR, 0:SR])
            mm.then_inc(kt_ps, 1)
            pe.wait_ge(kt_ready, 3)
            for ct in range(CT):
                for g in range(2):
                    n = N_U + 2 * ct + g
                    pe.wait_ge(split_lo, n + 1)
                    for j, (a, z) in enumerate(BLOCKS):
                        s = (2 * ct + g) * 3 + j
                        if s >= 8:
                            before = s - 8
                            c2, g2, j2 = before // 6, before // 3 % 2, before % 3
                            pe.wait_ge(glu_sig if g2 else glu_mul, 3 * c2 + j2 + 1)
                        for k in range(KT):
                            w = unit(n, k, P)
                            mm = three(ps[:, s % 8, 0:z - a], *w, hi_t[:, k, a:z], lo_t[:, k, a:z],
                                       k == 0, k == KT - 1)
                        mm.then_inc(u_mm, 1)
            pe.wait_ge(ulast_ready, CT)
            pe.wait_ge(glu_mul, 3 * CT)
            pe.wait_ge(glu_sig, 3 * CT)
            for ct in range(CT):
                pe.transpose(ps[0:PU, 0, ct * P:(ct + 1) * P], u_last[:, ct, 0:PU], ident)
                mm = pe.transpose(ps[0:SR, 1, ct * P:(ct + 1) * P], u_last[:, ct, PU:], ident)
            mm.then_inc(ut_ps, 1)
            pe.wait_ge(conv_done, 2 * CT)
            pe.wait_ge(consts_made, 2)
            for k, (a, z) in enumerate(BLOCKS):
                if k > 0:
                    pe.wait_ge(yc_ready, k)
                for ct in range(CT):
                    mm = pe.matmul(ps[:, 2, 0:z - a], ones[:, :], y[:, ct, a:z], start=(ct == 0), stop=(ct == CT - 1))
                mm.then_inc(mean_mm, 1)
                pe.wait_ge(ysq_ready, k + 1)
                for ct in range(CT):
                    mm = pe.matmul(ps[:, 3, 0:z - a], ones[:, :], ysq[:, ct, 0:z - a],
                                   start=(ct == 0), stop=(ct == CT - 1))
                mm.then_inc(var_mm, 1)
            pe.wait_ge(lnv_ready, len(BLOCKS))
            pe.wait_ge(cst_ready, 2)
            pe.wait_ge(masks_ready, 2 + S // P)
            NA = NH * (S // P)

            def query_transposes(i):
                pe.wait_ge(q_in[i % 2], 16 * (i // 2 + 1))
                if i > 1:
                    pe.wait_ge(mixa_hi, i - 1)
                    pe.wait_ge(mixa_lo, i - 1)
                r = rows_of(i)
                for j in range(4):
                    mm = pe.transpose(ps[:, 7, j * P:j * P + r], q_ld[0:r, i % 2, j * P:(j + 1) * P], ident[0:r, 0:r])
                mm.then_inc(qt_ps, 1)

            def head(h):
                g = h // 2
                return g % 2, g // 2, (g // 2) * 2 + h % 2

            def scores(n):
                i, h = divmod(n, NH)
                if h == 0:
                    pe.wait_ge(qt_ready, i + 1)
                if n >= 2:
                    pe.wait_ge(sm_done, n - 1)
                kh, pair, j = head(h)
                half = slice(kh * HD, (kh + 1) * HD)
                keys = (i + 1) * P
                for a in range(0, keys, 512):
                    w = min(512, keys - a)
                    mm = pe.matmul(ps[:, 2 * (n % 2) + a // 512, 0:w], q_t[half, i % 2, j, :],
                                   k_t[half, pair, a:a + w], start=True, stop=True)
                mm.then_inc(qk_done, 1)

            def turn(n):
                i = n // NH
                pe.wait_ge(exp_done, n + 1)
                if n > 0:
                    pe.wait_ge(pt_act, n)
                if dve_parts(n - 1) > 0:
                    pe.wait_ge(pt_dve, dve_parts(n - 1))
                for s in range(i + 1):
                    mm = pe.transpose(ps[:, 4 + s // 4, (s % 4) * P:(s % 4 + 1) * P],
                                      sm[:, n % 3, s * P:(s + 1) * P], ident)
                mm.then_inc(pt_ps, 1)

            def values(n):
                i, h = divmod(n, NH)
                pe.wait_ge(pt_act, n + 1)
                if dve_parts(n) > 0:
                    pe.wait_ge(pt_dve, dve_parts(n))
                if h == 0 and i > 0:
                    pe.wait_ge(o_ready, i)
                for s in range(i + 1):
                    mm = pe.matmul(ps[:, 6, h * HD:(h + 1) * HD], pt[:, n % 2, s * P:(s + 1) * P],
                                   v_tok[:, s, (h // 2) * HD:(h // 2 + 1) * HD], start=(s == 0), stop=(s == i))
                mm.then_inc(pv_done, 1)

            def output_transposes(i):
                pe.wait_ge(o_ready, i + 1)
                pe.wait_ge(qt_ready, min(i + 2, S // P + 1))
                for j in range(4):
                    mm = pe.transpose(ps[:, 7, j * P:(j + 1) * P], o_tok[:, j * P:(j + 1) * P], ident)
                mm.then_inc(ot_ps, 1)

            query_transposes(0)
            for n in range(NA + 2):
                if n < NA:
                    scores(n)
                if n >= 1 and n - 1 < NA:
                    turn(n - 1)
                if n >= 2:
                    values(n - 2)
                if n % NH == 3 and n < NA:
                    query_transposes(n // NH + 1)
                if n % NH == 2 and n > NH:
                    output_transposes(n // NH - 1)
            output_transposes(S // P - 1)
            pe.wait_ge(mixa_hi, S // P)
            pe.wait_ge(mixa_lo, S // P)
            for pr in range(NS // 2):
                for par in range(2):
                    b = 2 * pr + par
                    pe.wait_ge(kv_in[par], 32 * NPG * (pr + 1))
                    pe.wait_ge(ktn_ready, b + 1)
                    if par == 0:
                        pe.wait_ge(qblk_ready, 1)
                        if pr > 0:
                            pe.wait_ge(sexp_done, pr)
                    rows = slice(par * SR, (par + 1) * SR)
                    for j, (a, z) in enumerate(KB):
                        out = ps[rows, j, 0:z - a]
                        pe.matmul(out, q_blk[:, b, 0, :], kt_b[par][:, 0, a:z], start=True, stop=False)
                        pe.matmul(out, q_blk[:, b, 1, :], kt_b[par][:, 1, a:z], start=False, stop=False)
                        mm = pe.matmul(out, kb[0:SR, P + b * SR:P + (b + 1) * SR], smneg[:, a:z],
                                       start=False, stop=True)
                mm.then_inc(sqk_done, 1)
                pe.wait_ge(sexp_done, pr + 1)
                if pr > 0:
                    pe.wait_ge(spt_ready, 2 * pr)
                for s in range(NPG + 1):
                    w = P if s < NPG else TS
                    mm = pe.transpose(ps[0:w, 3 + s // 4, (s % 4) * P:(s % 4 + 1) * P],
                                      p_s[:, s * P:s * P + w], ident)
                mm.then_inc(spt_ps, 1)
                pe.wait_ge(spt_ready, 2 * pr + 2)
                pe.wait_ge(vn_in, 16)
                if pr > 0:
                    pe.wait_ge(so_ready, pr)
                for par in range(2):
                    b = 2 * pr + par
                    rows = slice(par * SR, (par + 1) * SR)
                    for s in range(NPG + 1):
                        k = P if s < NPG else TS
                        v = v_b[par][:, s, :] if s < NPG else v_new[:, b, :]
                        mm = pe.matmul(ps[rows, 6, 0:NKV * HD], pt_s[0:k, s, rows], v, start=(s == 0), stop=(s == NPG))
                    mm.then_inc(spv_done, 1)
                pe.wait_ge(so_ready, pr + 1)
                if pr > 0:
                    pe.wait_ge(sot_ready, pr)
                for p in range(2):
                    mm = pe.transpose(ps[:, 7, p * P:(p + 1) * P], o_s[:, p * P:(p + 1) * P], ident)
                mm.then_inc(sot_ps, 1)
            pe.wait_ge(sot_ready, NS // 2)
            pe.wait_ge(mixs_hi, 1)
            pe.wait_ge(mixs_lo, 1)
            project(5, N_OUT, 512, x1_ready)
            project(6, N_OUT + 4, 512, x1_ready)
            pe.wait_ge(x1_ready, 2 * NT)
            for o in range(NT):
                transpose_rows(NT + o, xn1[0:rows_of(ALL[o]), o % 2, :], rows_of(ALL[o]))
            pe.wait_ge(hi_ready, 2 * NT)
            pe.wait_ge(lo_ready, 2 * NT)
            pe.sem_inc(down_mm, 1)
            with pe.Fori(0, FG) as g:
                for c in range(2):
                    for gu in range(2):
                        n = N_FFN + 2 * c + gu
                        pe.wait_ge(split_lo, g * 6 + (n + 1))
                        for j, (a, z) in enumerate(BLOCKS):
                            done = 3 * c + j
                            pe.wait_ge(f_ready if gu else silu_f, g * 6 + (1 + max(0, done - 2)))
                            for k in range(KT):
                                w = unit(n, k, P)
                                mm = three(ps[:, 3 * gu + j, 0:z - a], *w, hi_t[:, k, a:z], lo_t[:, k, a:z],
                                           k == 0, k == KT - 1)
                            mm.then_inc(up_mm if gu else gate_mm, 1)
                pe.wait_ge(f_hi_ready, g * 6 + 6)
                pe.wait_ge(f_lo_ready, g * 6 + 6)
                pe.wait_ge(split_lo, g * 6 + (N_FFN + 6))
                for o in range(NT):
                    t = ALL[o]
                    r = rows_of(t)
                    for nh in range(2):
                        pe.wait_ge(y_added, g * (2 * NT) + (1 + max(0, 2 * o + nh - 1)))
                        for c in range(2):
                            n = N_FFN + 4 + c
                            mm = three(ps[0:r, 6 + nh, :], f_hi[:, c, cols_of(t)], f_lo[:, c, cols_of(t)],
                                       *unit(n, nh, 512), c == 0, c == 1)
                            if o == NT - 1 and nh == 1 and c == 0:
                                mm.then_inc(w_used, 1)
                        mm.then_inc(down_mm, 1)

        @block.scalar
        def _(act):
            steps = [0]

            def link(ins):
                steps[0] += 1
                ins.then_inc(act_step, 1)
                act.wait_ge(act_step, steps[0])

            def square_rows(q, src, junk, r):
                if q > 0:
                    act.wait_ge(ms_ready, q)
                act.activation(junk[0:r, :], src, ACT.Square, accum_out=ms[0:r, q:q + 1]).then_inc(ms_ready, 1)

            def take_hi(q):
                t = ALL[q % NT]
                r = rows_of(t)
                act.wait_ge(xt_done, q + 1)
                for half in range(2):
                    b = 2 * (q % NT % 4) + half
                    ins = act.activation(hi_t[:, 4 * half:4 * half + 4, cols_of(t)],
                                         ps[:, b, :].rearrange("p (k c) -> p k c", k=4)[:, :, 0:r], ACT.Copy)
                ins.then_inc(hi_ready, 1)

            for o in range(NT + 1):
                if o < NT:
                    t = ALL[o]
                    act.wait_ge(x_in[o % 3], 16 * (o // 3 + 1))
                    square_rows(o, xin[0:rows_of(t), o % 3, :], sq, rows_of(t))
                if o > 0:
                    take_hi(o - 1)
            for o, t in enumerate(CHUNKS[0]):
                r = rows_of(t)
                act.wait_ge(proj_done, BASE[0] + o + 1)
                act.activation(kiw[0:r, t, :], ps[0:r, 4 if t == SAMPLE else t, 0:KIW], ACT.Copy
                               ).then_inc(proj_evac, 1)
            act.wait_ge(kiw_ready, 1)
            act.dma_start(O["ki_prompt"].rearrange("(t p) d -> p t d", p=P), kiw[:, 0:SAMPLE, 0:ID]).then_inc(stores, 16)
            act.dma_start(O["ki_sample"], kiw[0:SR, SAMPLE, 0:ID]).then_inc(stores, 16)
            for c in (1, 2):
                for o, t in enumerate(CHUNKS[c]):
                    r = rows_of(t)
                    act.wait_ge(proj_done, BASE[c] + o + 1)
                    act.activation(qi_tok[0:r, t - FIRST, (c - 1) * 512:c * 512],
                                   ps[0:r, 4 if t == SAMPLE else t, :], ACT.Copy).then_inc(proj_evac, 1)
            act.wait_ge(kit_ps, 1)
            for b in range(2):
                for half in range(2):
                    act.activation(ki_t[half * ID:(half + 1) * ID, b * 512:(b + 1) * 512], ps[0:ID, 6 + b, :],
                                   ACT.Copy).then_inc(kit_ready, 1)
            act.activation(kin_t[:, :], ps[0:ID, 5, 0:SR], ACT.Copy).then_inc(kit_ready, 1)
            act.activation(wts[:, :], ps[0:NI, 5, SR:2 * SR], ACT.Copy).then_inc(kit_ready, 1)

            def take_index_queries(i):
                act.wait_ge(qit_ps, i + 1)
                for b in range(2):
                    act.activation(qi_t[:, i % 2, 4 * b:4 * b + 4, :],
                                   ps[:, 6 + b, :].rearrange("p (j c) -> p j c", j=4), ACT.Copy
                                   ).then_inc(qit_ready, 1)

            take_index_queries(0)
            for i in range(NSEL):
                keys = (FIRST + i + 1) * P
                for h in range(NI):
                    n = i * NI + h
                    act.wait_ge(idx_mm, n + 1)
                    if n >= 2:
                        act.wait_ge(acc_done, n - 1)
                    act.activation(rl[:, n % 2, 0:keys], wide(2 * (n % 3), keys), ACT.Relu).then_inc(relu_done, 1)
                    if h == 8 and i + 1 < NSEL:
                        take_index_queries(i + 1)
            act.wait_ge(qist_ps, 1)
            for b in range(2):
                for hh in range(2):
                    ins = act.activation(
                        qis_t[:, :, 8 * b + 4 * hh:8 * b + 4 * hh + 4, :].rearrange("p b h t -> p h b t"),
                        ps[0:ID, 6 + b, hh * 256:(hh + 1) * 256].rearrange("p (h b t) -> p h b t", h=4, b=NS), ACT.Copy)
                ins.then_inc(qist_ready, 1)
            act.wait_ge(acc_done, nsteps)
            for b in range(NS):
                if b >= 2:
                    act.wait_ge(sidx_mm, b - 1)
                act.activation(kis_t[b % 2][:, PAST:SKEYS], kin_t[:, b * TS:(b + 1) * TS], ACT.Copy).then_inc(kin_done, 1)
                act.wait_ge(sidx_mm, b + 1)
                if b >= 2:
                    act.wait_ge(sw_mm, b - 1)
                act.activation(rl[:, b % 2, :], wide(0, SKEYS), ACT.Relu).then_inc(srelu_done, 1)

            def q_view(ap):
                return ap.rearrange("p (a r k d) -> p a k r d", a=2, r=2, k=2)

            for n in range(2 * NT + 1):
                if n < 2 * NT:
                    c, o = 3 + n // NT, n % NT
                    t = CHUNKS[c][o]
                    r = rows_of(t)
                    src = ps[0:r, 4 if t == SAMPLE else t, :]
                    act.wait_ge(proj_done, BASE[c] + o + 1)
                    if n == 0:
                        act.wait_ge(masks_ready, 1)
                    if c == 3:
                        act.activation(v_tok[0:r, t, :], src[:, 256:512], ACT.Copy)
                        link(act.activation(k_tok[0:r, t, :], src[:, 0:256], ACT.Copy))
                        if n > 0:
                            act.wait_ge(head_ms, n)
                        act.activation(hsq[0:r, 0:256], k_tok[0:r, t, :], ACT.Square).then_inc(proj_evac, 1)
                    else:
                        if o >= 3:
                            act.wait_ge(q_out[o % 3], 16 * (o // 3))
                        qs = qst[0:r, o % 3, :]
                        for a in range(2):
                            ins = act.activation(
                                qs[:, a * 256:(a + 1) * 256].rearrange("p (r k d) -> p k r d", r=2, k=2),
                                src[:, a * 256:(a + 1) * 256].rearrange("p (k r d) -> p k r d", k=2, r=2), ACT.Copy)
                        link(ins)
                        if n > 0:
                            act.wait_ge(head_ms, n)
                        act.activation(hsq[0:r, :], qs, ACT.Square).then_inc(proj_evac, 1)
                if n > NT:
                    o = n - 1 - NT
                    r = rows_of(ALL[o])
                    act.wait_ge(q_ready, o + 1)
                    act.dma_start(q_scr[ALL[o], 0:r, :], qst[0:r, o % 3, :]).then_inc(q_out[o % 3], 16)
                if n == NT:
                    act.wait_ge(k_ready, NT)
                    act.wait_ge(proj_evac, BASE[4])
                    act.dma_start(O["k_prompt"].rearrange("(t p) d -> p t d", p=P), k_tok[:, 0:SAMPLE, :]).then_inc(stores, 16)
                    act.dma_start(O["k_sample"], k_tok[0:SR, SAMPLE, :]).then_inc(stores, 16)
                    act.dma_start(O["v_prompt"].rearrange("(t p) d -> p t d", p=P), v_tok[:, 0:SAMPLE, :]).then_inc(stores, 16)
                    act.dma_start(O["v_sample"].rearrange("b t c -> (b t) c"), v_tok[0:SR, SAMPLE, :]).then_inc(stores, 16)
            act.wait_ge(kt_ps, 1)
            for p in range(2):
                act.activation(k_t[:, p, 0:S], wide(2 * p, S), ACT.Copy).then_inc(kt_ready, 1)
            act.activation(k_t[:, :, S:ROWS], ps[:, 4, 0:2 * SR].rearrange("p (a c) -> p a c", a=2), ACT.Copy
                           ).then_inc(kt_ready, 1)
            for ct in range(CT):
                for j, (a, z) in enumerate(BLOCKS):
                    n = 3 * ct + j
                    s = (2 * ct + 1) * 3 + j
                    act.wait_ge(u_mm, s + 1)
                    if n >= 2:
                        act.wait_ge(glu_mul, n - 1)
                    act.activation(sig[:, n % 2, 0:z - a], ps[:, s % 8, 0:z - a], ACT.Sigmoid).then_inc(glu_sig, 1)
            act.wait_ge(ut_ps, 1)
            act.activation(cst[0:PU, 0, :], ps[0:PU, 0, :], ACT.Copy).then_inc(cst_ready, 1)
            act.activation(cst[:, 1, :], ps[0:SR, 1, :], ACT.Copy).then_inc(cst_ready, 1)
            act.wait_ge(cst_ready, 2)
            act.dma_start(O["conv_prompt"], cst[0:PU, 0, :]).then_inc(cst_out, 16)
            act.dma_start(O["conv_sample"][:, PU - TS:PU, :], cst[:, 1, :]).then_inc(cst_out, 16)
            for k, (a, z) in enumerate(BLOCKS):
                act.wait_ge(yc_ready, k + 1)
                if k > 0:
                    act.wait_ge(var_mm, k)
                act.activation(ysq[:, :, 0:z - a], y[:, :, a:z], ACT.Square).then_inc(ysq_ready, 1)
                act.wait_ge(yn_ready, k + 1)
                for ct in range(CT):
                    ins = act.activation(y[:, ct, a:z], y[:, ct, a:z], ACT.Silu, bias=kf[:, K_LB + ct:K_LB + ct + 1],
                                         scale=kf[:, K_LG + ct:K_LG + ct + 1])
                link(ins)
                act.activation(hi_t[:, 0:CT, a:z], y[:, :, a:z], ACT.Copy).then_inc(mixc_hi, 1)
            NA = NH * (S // P)

            def take_queries(i):
                act.wait_ge(qt_ps, i + 1)
                r = rows_of(i)
                act.activation(q_t[:, i % 2, :, 0:r], ps[:, 7, :].rearrange("p (j c) -> p j c", j=4)[:, :, 0:r],
                               ACT.Copy).then_inc(qt_ready, 1)

            def exps(n):
                i = n // NH
                keys = (i + 1) * P
                act.wait_ge(nmax, n + 1)
                act.activation(sm[:, n % 3, 0:keys], sm[:, n % 3, 0:keys], ACT.Exp, bias=stat[:, 0, n % 16:n % 16 + 1],
                               scale=HD ** -0.5, accum_out=stat[:, 1, n % 16:n % 16 + 1]).then_inc(exp_done, 1)

            def take_weights(n):
                keys = (n // NH + 1) * P
                act.wait_ge(pt_ps, n + 1)
                if n >= 2:
                    act.wait_ge(pv_done, n - 1)
                act.activation(pt[:, n % 2, 0:min(keys, 512)], ps[:, 4, 0:min(keys, 512)], ACT.Copy
                               ).then_inc(pt_act, 1)

            def take_outputs(i):
                act.wait_ge(ot_ps, i + 1)
                act.activation(hi_t[:, CT:KT, cols_of(i)], ps[:, 7, :].rearrange("p (j c) -> p j c", j=4), ACT.Copy
                               ).then_inc(mixa_hi, 1)

            take_queries(0)
            for n in range(NA + 2):
                if n < NA:
                    if n % NH == 0 and n >= 2 * NH:
                        act.wait_ge(o_ready, n // NH - 1)
                    exps(n)
                if n >= 1 and n - 1 < NA:
                    take_weights(n - 1)
                if n % NH == 4 and n < NA:
                    take_queries(n // NH + 1)
                if n % NH == 3 and n > NH or n == NA + 1:
                    take_outputs(n // NH - 1 if n < NA else S // P - 1)
            for pr in range(NS // 2):
                for par in range(2):
                    b = 2 * pr + par
                    if b == 0:
                        act.wait_ge(mixa_lo, S // P)
                        act.wait_ge(cst_out, 16 * 3)
                    if b >= 2:
                        act.wait_ge(spv_done, b - 1)
                    act.activation(kt_b[par][:, :, PAST:SKEYS], k_t[:, :, S + b * TS:S + (b + 1) * TS], ACT.Copy
                                   ).then_inc(ktn_ready, 1)
                act.wait_ge(smax, pr + 1)
                if pr > 0:
                    act.wait_ge(spt_ps, pr)
                    act.wait_ge(so_ready, pr)
                act.activation(p_s[:, :], wide(0, SKEYS), ACT.Exp, bias=stat[:, 0, 0:1], scale=HD ** -0.5,
                               accum_out=stat[:, 1, 0:1]).then_inc(sexp_done, 1)
                act.wait_ge(spt_ps, pr + 1)
                if pr > 0:
                    act.wait_ge(spv_done, 2 * pr)
                act.activation(pt_s[:, 0:NPG, :], wide(3, NPG * P).rearrange("p (s c) -> p s c", s=NPG), ACT.Copy
                               ).then_inc(spt_ready, 1)
                act.activation(pt_s[0:TS, NPG, :], ps[0:TS, 5, 0:P], ACT.Copy).then_inc(spt_ready, 1)
                act.wait_ge(sot_ps, pr + 1)
                act.activation(o_st[:, :, pr, :], ps[:, 7, 0:2 * P].rearrange("p (a c) -> p a c", a=2), ACT.Copy
                               ).then_inc(sot_ready, 1)
            act.wait_ge(mixs_ready, 1)
            act.activation(hi_t[:, CT:KT, cols_of(SAMPLE)], mix_s[:, :, :], ACT.Copy).then_inc(mixs_hi, 1)
            for o in range(NT + 1):
                if o < NT:
                    t = ALL[o]
                    act.wait_ge(x1_ready, NT + o + 1)
                    square_rows(NT + o, x1[0:rows_of(t), t, :], sq1, rows_of(t))
            for o in range(NT):
                take_hi(NT + o)
            act.wait_ge(lo_ready, 2 * NT)
            act.sem_inc(silu_f, 1)
            with act.Fori(0, FG) as g:
                for m in range(7):
                    if m < 6:
                        a, z = BLOCKS[m % 3]
                        act.wait_ge(gate_mm, g * 6 + (m + 1))
                        act.wait_ge(f_ready, g * 6 + (1 + max(0, m - 1)))
                        act.activation(sg[:, m % 2, 0:z - a], ps[:, m % 3, 0:z - a], ACT.Silu).then_inc(silu_f, 1)
                    if m > 0:
                        c, j = divmod(m - 1, 3)
                        a, z = BLOCKS[j]
                        if m == 1:
                            act.wait_ge(down_mm, g * (2 * NT) + 1)
                        act.wait_ge(f_ready, g * 6 + (1 + m))
                        act.activation(f_hi[:, c, a:z], ff[:, (m - 1) % 2, 0:z - a], ACT.Copy).then_inc(f_hi_ready, 1)

        @block.vector
        def _(dve):
            steps = [0]

            def link(ins):
                steps[0] += 1
                ins.then_inc(dve_step, 1)
                dve.wait_ge(dve_step, steps[0])

            def norm_rows(q, src, dst, g_tile, r):
                dve.wait_ge(rs_ready, q + 1)
                if q % NT >= 2:
                    dve.wait_ge(xt_done, q - 1)
                dve.scalar_tensor_tensor(dst, src, rs[0:r, q:q + 1], g_tile[0:r, :], ALU.mult, ALU.mult
                                         ).then_inc(xn_ready, 1)

            def take_lo(q):
                t = ALL[q % NT]
                r = rows_of(t)
                dve.wait_ge(hi_ready, q + 1)
                for half in range(2):
                    b = 2 * (q % NT % 4) + half
                    ks = slice(4 * half, 4 * half + 4)
                    ins = dve.tensor_tensor(lo_t[:, ks, cols_of(t)],
                                            ps[:, b, :].rearrange("p (k c) -> p k c", k=4)[:, :, 0:r],
                                            hi_t[:, ks, cols_of(t)].bitcast(F32), ALU.subtract)
                ins.then_inc(lo_ready, 1)

            def rope(x, cos, sin, t1, t2):
                dve.tensor_tensor(t1, x[:, :, 0:16], cos, ALU.mult)
                dve.tensor_tensor(t2[:, :, 0:8], x[:, :, 8:16], sin[:, :, 0:8], ALU.mult)
                link(dve.tensor_tensor(t2[:, :, 8:16], x[:, :, 0:8], sin[:, :, 8:16], ALU.mult))
                return dve.tensor_tensor(x[:, :, 0:16], t1, t2, ALU.add)

            def rope_tile(x, t, heads):
                r = rows_of(t)
                cos = kf[0:r, K_COS + 16 * t:K_COS + 16 * t + 16].unsqueeze(1).broadcast_to([r, heads, 16])
                sin = kf[0:r, K_SIN + 16 * t:K_SIN + 16 * t + 16].unsqueeze(1).broadcast_to([r, heads, 16])
                t1, t2 = (rt[0:r, i, 0:heads * 16].rearrange("p (h d) -> p h d", h=heads) for i in range(2))
                return rope(x, cos, sin, t1, t2)

            link(dve.memset(rt[:, :, :], 0.0))
            dve.wait_ge(g_in, 16)
            for o in range(NT + 1):
                if o < NT:
                    r = rows_of(ALL[o])
                    norm_rows(o, xin[0:r, o % 3, :], xn[0:r, o % 2, :], gbc, r)
                if o > 0:
                    take_lo(o - 1)
            dve.wait_ge(consts_in, 48)
            dve.wait_ge(proj_evac, NT)
            for t0, t1, r in ((0, SAMPLE, P), (SAMPLE, NT, SR)):
                cos = kf[0:r, K_COS + 16 * t0:K_COS + 16 * t1].rearrange("p (t d) -> p t d", d=16)
                sin = kf[0:r, K_SIN + 16 * t0:K_SIN + 16 * t1].rearrange("p (t d) -> p t d", d=16)
                ta, tb = (rt[0:r, i, 0:(t1 - t0) * 16].rearrange("p (h d) -> p h d", d=16) for i in range(2))
                link(rope(kiw[0:r, t0:t1, 0:ID], cos, sin, ta, tb))
                ins = dve.tensor_scalar(wi_tok[0:r, t0:t1, :], kiw[0:r, t0:t1, ID:KIW], (NI * ID) ** -0.5, None, ALU.mult)
            ins.then_inc(kiw_ready, 1)
            for c in (1, 2):
                for o, t in enumerate(CHUNKS[c]):
                    r = rows_of(t)
                    dve.wait_ge(proj_evac, BASE[c] + o + 1)
                    if BASE[c] + o > NT:
                        dve.wait_ge(qi_ready, BASE[c] + o - NT)
                    x = qi_tok[0:r, t - FIRST, (c - 1) * 512:c * 512].rearrange("p (h d) -> p h d", d=ID)
                    rope_tile(x, t, 8).then_inc(qi_ready, 1)
            dve.wait_ge(wx_done, 1)
            dve.wait_ge(consts_made, 1)
            for b in range(NS):
                s = slice(b * TS, (b + 1) * TS)
                ins = dve.tensor_tensor(w_all[:, b, s], ps[:, 5, s], kf[:, K_M + b * TS:K_M + (b + 1) * TS], ALU.mult)
            ins.then_inc(wall_ready, 1)
            for i in range(NSEL):
                t = FIRST + i
                a0, keys = acc_at(t), (t + 1) * P
                for h in range(NI):
                    n = i * NI + h
                    dve.wait_ge(relu_done, n + 1)
                    w = wi_tok[:, t, h:h + 1]
                    if h == 0:
                        dve.tensor_scalar(acc[:, a0:a0 + t * P], rl[:, n % 2, 0:t * P], w, None, ALU.mult)
                        dve.scalar_tensor_tensor(acc[:, a0 + t * P:a0 + keys], rl[:, n % 2, t * P:keys], w,
                                                 kf[:, K_TRI:K_TRI + P], ALU.mult, ALU.add).then_inc(acc_done, 1)
                    else:
                        dve.wait_ge(acc_done, n)
                        dve.scalar_tensor_tensor(acc[:, a0:a0 + keys], rl[:, n % 2, 0:keys], w, acc[:, a0:a0 + keys],
                                                 ALU.mult, ALU.add).then_inc(acc_done, 1)
            dve.wait_ge(sw_mm, NS)
            dve.tensor_copy(sacc[:, 0:PAST], wide(3, PAST, slice(0, SR)))
            dve.tensor_tensor(sacc[:, PAST:SKEYS], ps[0:SR, 5, 0:TS], kf[0:SR, K_NEW:K_NEW + TS], ALU.add
                              ).then_inc(masks_ready, 1)

            for n in range(2 * NT):
                c, o = 3 + n // NT, n % NT
                t = CHUNKS[c][o]
                r, heads = rows_of(t), (NKV if c == 3 else NH)
                x = (k_tok[0:r, t, :] if c == 3 else qst[0:r, o % 3, :]).rearrange("p (h d) -> p h d", d=HD)
                dve.wait_ge(proj_evac, BASE[c] + o + 1)
                link(dve.tensor_reduce(hs[0:r, n % 2, 0:heads],
                                       hsq[0:r, 0:heads * HD].rearrange("p (h d) -> p h d", d=HD), AX_X, ALU.add))
                dve.tensor_scalar(hs[0:r, n % 2, 0:heads], hs[0:r, n % 2, 0:heads], 1.0 / HD, RMS_EPS,
                                  ALU.mult, ALU.add).then_inc(head_ms, 1)
                dve.wait_ge(head_rs, n + 1)
                link(dve.tensor_tensor(x, x, hs[0:r, 2 + n % 2, 0:heads].unsqueeze(2).broadcast_to([r, heads, HD]),
                                       ALU.mult))
                gain = K_GK if c == 3 else K_GQ
                link(dve.tensor_tensor(x, x, kf[0:r, gain:gain + HD].unsqueeze(1).broadcast_to([r, heads, HD]), ALU.mult))
                if o > 0:
                    dve.wait_ge(k_ready if c == 3 else q_ready, o)
                elif c == 4:
                    dve.wait_ge(k_ready, NT)
                else:
                    dve.wait_ge(qi_ready, 2 * (NSEL + 1))
                rope_tile(x, t, heads).then_inc(k_ready if c == 3 else q_ready, 1)

            for t in list(range(FIRST, S // P)) + [SAMPLE]:
                r = rows_of(t)
                keys = SKEYS if t == SAMPLE else (t + 1) * P
                work = sacc[:, :] if t == SAMPLE else acc[:, acc_at(t):acc_at(t) + keys]
                base = steps[0]
                with dve.Fori(0, TOPK // 8) as i:
                    dve.max(m8[0:r, :], work).then_inc(dve_step, 1)
                    dve.wait_ge(dve_step, 2 * i + (base + 1))
                    dve.sem_inc(fence_dve, 1)
                    dve.match_replace(work, m8[0:r, :], work, TAKEN).then_inc(dve_step, 1)
                    dve.wait_ge(dve_step, 2 * i + (base + 2))
                steps[0] += 2 * (TOPK // 8)
                out = smneg[:, :] if t == SAMPLE else mneg[:, mask_at(t):mask_at(t) + keys]
                dve.tensor_scalar(out, work, TAKEN, DROP, ALU.not_equal, ALU.mult).then_inc(masks_ready, 1)
            for t in range(FIRST):
                if t > 0:
                    dve.memset(mneg[:, mask_at(t):mask_at(t) + t * P], 0.0)
                dve.tensor_copy(mneg[:, mask_at(t) + t * P:mask_at(t + 1)], kb[:, 0:P]).then_inc(masks_ready, 1)

            dve.wait_ge(kt_ready, 3)
            dve.wait_ge(stores, 16 * 6)
            for i in range(2):
                dve.memset(u[:, i, 0:PU], 0.0)
            for ct in range(CT):
                if ct == 0:
                    for r in range(3):
                        dve.wait_ge(q_out[r], 48)
                new = u[:, ct % 2, PU + S:].rearrange("p (b w) -> p b w", b=NS)[:, :, PU:]
                for j, (a, z) in enumerate(BLOCKS):
                    n = 3 * ct + j
                    s = 2 * ct * 3 + j
                    dve.wait_ge(glu_sig, n + 1)
                    if z <= S:
                        ins = dve.tensor_tensor(u[:, ct % 2, PU + a:PU + z], ps[:, s % 8, 0:z - a], sig[:, n % 2, 0:z - a],
                                                ALU.mult)
                    else:
                        dve.tensor_tensor(u[:, ct % 2, PU + a:PU + S], ps[:, s % 8, 0:S - a], sig[:, n % 2, 0:S - a],
                                          ALU.mult)
                        ins = dve.tensor_tensor(new, ps[:, s % 8, S - a:z - a].rearrange("p (b t) -> p b t", b=NS),
                                                sig[:, n % 2, S - a:z - a].rearrange("p (b t) -> p b t", b=NS), ALU.mult)
                    ins.then_inc(glu_mul, 1)
                dve.wait_ge(glu_mul, 3 * ct + 3)
                dve.tensor_copy(u_last[:, ct, 0:PU], u[:, ct % 2, S:S + PU])
                dve.tensor_copy(u_last[:, ct, PU:].rearrange("p (b t) -> p b t", b=NS), new).then_inc(ulast_ready, 1)
                dve.wait_ge(u_state[ct % 2], 16 * (ct // 2 + 1))
                yp, ys = y[:, ct, 0:S], y[:, ct, S:ROWS].rearrange("p (b t) -> p b t", b=NS)
                us = u[:, ct % 2, PU + S:].rearrange("p (b w) -> p b w", b=NS)
                for j in range(W):
                    w = kf[:, K_CW + ct * W + j:K_CW + ct * W + j + 1]
                    up, un = u[:, ct % 2, j:j + S], us[:, :, j:j + TS]
                    if j == 0:
                        bias = kf[:, K_CB + ct:K_CB + ct + 1]
                        dve.tensor_scalar(yp, up, w, bias, ALU.mult, ALU.add)
                        link(dve.tensor_scalar(ys, un, w, bias, ALU.mult, ALU.add))
                    elif j < W - 1:
                        dve.scalar_tensor_tensor(yp, up, w, yp, ALU.mult, ALU.add)
                        link(dve.scalar_tensor_tensor(ys, un, w, ys, ALU.mult, ALU.add))
                    else:
                        dve.scalar_tensor_tensor(yp, up, w, yp, ALU.mult, ALU.add).then_inc(conv_done, 1)
                        dve.scalar_tensor_tensor(ys, un, w, ys, ALU.mult, ALU.add).then_inc(conv_done, 1)
            for k, (a, z) in enumerate(BLOCKS):
                dve.wait_ge(mean_mm, k + 1)
                for ct in range(CT):
                    ins = dve.tensor_tensor(y[:, ct, a:z], y[:, ct, a:z], ps[:, 2, 0:z - a], ALU.subtract)
                ins.then_inc(yc_ready, 1)
                dve.wait_ge(var_mm, k + 1)
                if k > 0:
                    dve.wait_ge(yn_ready, k)
                dve.tensor_scalar(lnr[:, 0:z - a], ps[:, 3, 0:z - a], LN_EPS, None, ALU.add).then_inc(lnv_ready, 1)
                dve.wait_ge(lnr_ready, k + 1)
                for ct in range(CT):
                    ins = dve.tensor_tensor(y[:, ct, a:z], y[:, ct, a:z], lnr[:, 0:z - a], ALU.mult)
                ins.then_inc(yn_ready, 1)
                dve.wait_ge(mixc_hi, k + 1)
                dve.tensor_tensor(lo_t[:, 0:CT, a:z], y[:, :, a:z], hi_t[:, 0:CT, a:z].bitcast(F32), ALU.subtract
                                  ).then_inc(mixc_lo, 1)
            NA = NH * (S // P)

            def mask_scores(n):
                i = n // NH
                keys = (i + 1) * P
                dve.wait_ge(qk_done, n + 1)
                if n >= 3:
                    dve.wait_ge(pt_ps, n - 2)
                if n == 0:
                    dve.wait_ge(mixc_lo, len(BLOCKS))
                dve.tensor_tensor_reduce(sm[:, n % 3, 0:keys], wide(2 * (n % 2), keys),
                                         mneg[:, mask_at(i):mask_at(i) + keys], 1.0, -3.0e38, ALU.add, ALU.max,
                                         mx[:, n % 2:n % 2 + 1]).then_inc(sm_done, 1)
                dve.wait_ge(sm_done, n + 1)
                if n >= 16:
                    dve.wait_ge(exp_done, n - 15)
                dve.tensor_scalar(stat[:, 0, n % 16:n % 16 + 1], mx[:, n % 2:n % 2 + 1], -(HD ** -0.5), None, ALU.mult
                                  ).then_inc(nmax, 1)

            def take_weights(n):
                keys = (n // NH + 1) * P
                if keys <= 512:
                    return
                dve.wait_ge(pt_ps, n + 1)
                dve.wait_ge(pv_done, n - 1)
                dve.tensor_copy(pt[:, n % 2, 512:keys], ps[:, 5, 0:keys - 512]).then_inc(pt_dve, 1)

            def outputs(i):
                dve.wait_ge(exp_done, NH * (i + 1))
                link(dve.reciprocal(rinv[:, :], stat[:, 1, i % 2 * NH:(i % 2 + 1) * NH]))
                dve.wait_ge(pv_done, NH * (i + 1))
                if i > 0:
                    dve.wait_ge(ot_ps, i)
                dve.tensor_tensor(o_tok[:, :].rearrange("p (h d) -> p h d", d=HD),
                                  ps[:, 6, :].rearrange("p (h d) -> p h d", d=HD),
                                  rinv[:, :].unsqueeze(2).broadcast_to([P, NH, HD]), ALU.mult).then_inc(o_ready, 1)

            def lows(i):
                dve.wait_ge(mixa_hi, i + 1)
                dve.tensor_tensor(lo_t[:, CT:KT, cols_of(i)], ps[:, 7, :].rearrange("p (j c) -> p j c", j=4),
                                  hi_t[:, CT:KT, cols_of(i)].bitcast(F32), ALU.subtract).then_inc(mixa_lo, 1)

            for n in range(NA + 2):
                if n < NA:
                    mask_scores(n)
                if n >= 1 and n - 1 < NA:
                    take_weights(n - 1)
                if n % NH == 1 and n > NH:
                    outputs(n // NH - 1)
                if n % NH == 3 and n > NH:
                    lows(n // NH - 1)
            lows(S // P - 1)
            link(dve.memset(q_blk[:, :, :, :], 0.0))
            dve.wait_ge(qt_ready, S // P + 1)
            for h in range(NH):
                kh, pair, j = (h // 2) % 2, h // 4, (h // 4) * 2 + h % 2
                half = slice(kh * HD, (kh + 1) * HD)
                ins = dve.tensor_copy(q_blk[half, :, pair, h * TS:(h + 1) * TS],
                                      q_t[half, 0, j, 0:SR].rearrange("p (b t) -> p b t", b=NS))
            ins.then_inc(qblk_ready, 1)
            for pr in range(NS // 2):
                dve.wait_ge(sqk_done, pr + 1)
                link(dve.reduce_max(mx[:, 0:1], wide(0, SKEYS), AX_X))
                dve.tensor_scalar(stat[:, 0, 0:1], mx[:, 0:1], -(HD ** -0.5), None, ALU.mult).then_inc(smax, 1)
                dve.wait_ge(sexp_done, pr + 1)
                link(dve.reciprocal(rinv[:, 0:1], stat[:, 1, 0:1]))
                dve.wait_ge(spv_done, 2 * pr + 2)
                if pr > 0:
                    dve.wait_ge(sot_ps, pr)
                dve.tensor_scalar(o_s[:, :], ps[:, 6, 0:NKV * HD], rinv[:, 0:1], None, ALU.mult).then_inc(so_ready, 1)
            dve.wait_ge(sot_ready, NS // 2)
            for h in range(NH):
                kh, pair = (h // 2) % 2, h // 4
                src = o_st[kh * HD:(kh + 1) * HD, pair, :, :].rearrange("p a (b c) -> p (a b) c", b=2)
                dst = mix_s[(h % 2) * HD:(h % 2 + 1) * HD, h // 2, :].rearrange("p (b t) -> p b t", b=NS)
                ins = dve.tensor_copy(dst, src[:, :, h * TS:(h + 1) * TS])
            ins.then_inc(mixs_ready, 1)
            dve.wait_ge(mixs_hi, 1)
            dve.tensor_tensor(lo_t[:, CT:KT, cols_of(SAMPLE)], mix_s[:, :, :],
                              hi_t[:, CT:KT, cols_of(SAMPLE)].bitcast(F32), ALU.subtract).then_inc(mixs_lo, 1)
            dve.wait_ge(x1_in, 32)
            for n in range(2 * NT):
                t, c = ALL[n % NT], n // NT
                r = rows_of(t)
                dve.wait_ge(proj_done, BASE[5] + n + 1)
                xs = x1[0:r, t, c * 512:(c + 1) * 512]
                dve.tensor_tensor(xs, xs, ps[0:r, 4 if t == SAMPLE else t, :], ALU.add).then_inc(x1_ready, 1)
            dve.wait_ge(g_in, 32)
            for o in range(NT + 1):
                if o < NT:
                    t = ALL[o]
                    r = rows_of(t)
                    norm_rows(NT + o, x1[0:r, t, :], xn1[0:r, o % 2, :], gbc1, r)
                if o > 0:
                    take_lo(NT + o - 1)
            dve.sem_inc(f_ready, 1)
            dve.sem_inc(y_added, 1)
            with dve.Fori(0, FG) as g:
                for m in range(7):
                    if m < 6:
                        a, z = BLOCKS[m % 3]
                        dve.wait_ge(up_mm, g * 6 + (m + 1))
                        dve.wait_ge(silu_f, g * 6 + (m + 2))
                        if m >= 2:
                            dve.wait_ge(f_hi_ready, g * 6 + (m - 1))
                            dve.wait_ge(f_lo_ready, g * 6 + (m - 1))
                        dve.tensor_tensor(ff[:, m % 2, 0:z - a], ps[:, 3 + m % 3, 0:z - a], sg[:, m % 2, 0:z - a],
                                          ALU.mult).then_inc(f_ready, 1)
                    if m > 0:
                        c, j = divmod(m - 1, 3)
                        a, z = BLOCKS[j]
                        dve.wait_ge(f_hi_ready, g * 6 + m)
                        dve.tensor_tensor(f_lo[:, c, a:z], ff[:, (m - 1) % 2, 0:z - a], f_hi[:, c, a:z].bitcast(F32),
                                          ALU.subtract).then_inc(f_lo_ready, 1)
                dve.wait_ge(y_added, g * (2 * NT) + 1)
                for o in range(NT):
                    t = ALL[o]
                    r = rows_of(t)
                    for nh in range(2):
                        dve.wait_ge(down_mm, g * (2 * NT) + (2 * o + nh + 2))
                        xs = x1[0:r, t, nh * 512:(nh + 1) * 512]
                        dve.tensor_tensor(xs, xs, ps[0:r, 6 + nh, :], ALU.add).then_inc(y_added, 1)

_OUTS = [
    ("y_prompt", (S, D), (1, S, D)), ("y_sample", (SR, D), (NS, TS, D)),
    ("k_prompt", (S, NKV * HD), (1, 1, S, NKV, HD)), ("v_prompt", (S, NKV * HD), (1, 1, S, NKV, HD)),
    ("ki_prompt", (S, ID), (1, 1, S, ID)), ("conv_prompt", (W - 1, C), (1, 1, W - 1, C)),
    ("k_sample", (SR, NKV * HD), (1, NS, TS, NKV, HD)), ("v_sample", (NS, TS, NKV * HD), (1, NS, TS, NKV, HD)),
    ("ki_sample", (SR, ID), (1, NS, TS, ID)), ("conv_sample", (NS, W - 1, C), (1, NS, W - 1, C)),
]

def kernel(**inputs):
    import ml_dtypes
    import concourse.bacc as bacc
    from concourse.bass_utils import run_bass_kernel_spmd

    a = {k: np.asarray(v) for k, v in inputs.items()}
    pool = a["cache_k"].shape[1]
    f, b = shape_constants()

    def spread(row, at, kf):
        kf[:, at:at + row.size] = row.reshape(1, -1)

    def by_channel(x):
        return x.reshape(-1, CT, P).transpose(2, 1, 0).reshape(P, -1)

    spread(a["q_norm_g"][0], K_GQ, f)
    spread(a["k_norm_g"][0], K_GK, f)
    f[:, K_CW:K_CB] = by_channel(a["conv_dw_w"][0])
    f[:, K_CB:K_LG] = by_channel(a["conv_dw_b"][0])
    f[:, K_LG:K_LB] = by_channel(a["conv_ln_g"][0])
    f[:, K_LB:K_END] = by_channel(a["conv_ln_b"][0])
    arrays = {
        "x_prompt": a["x_prompt"][0], "x_sample": a["x_sample"].reshape(SR, D),
        "cache_kt": a["cache_k"][0].reshape(pool, PAGE, NKV * HD).transpose(0, 2, 1),
        "cache_v": a["cache_v"][0].reshape(pool, PAGE, NKV * HD),
        "cache_it": a["cache_idx_k"][0].transpose(0, 2, 1),
        "state_t": a["state_conv"][0].transpose(2, 0, 1), "state": a["state_conv"][0],
        "page_table": a["page_table"].reshape(1, -1),
        "attn_norm_g": a["attn_norm_g"], "ffn_norm_g": a["ffn_norm_g"],
        "w_in": a["w_in"][0], "w_out": a["w_out"][0], "w_gate": a["w_gate"][0], "w_up": a["w_up"][0],
        "w_down": a["w_down"][0], "kf": f, "kb": b.astype(ml_dtypes.bfloat16),
    }
    arrays = {k: np.ascontiguousarray(v) for k, v in arrays.items()}
    nc = bacc.Bacc("TRN2", target_bir_lowering=False, num_devices=1)
    A = {k: nc.dram_tensor(f"in_{k}", v.shape, mybir.dt.from_np(v.dtype), kind="ExternalInput").ap()
         for k, v in arrays.items()}
    O = {k: nc.dram_tensor(f"out_{k}", s, F32, kind="ExternalOutput").ap() for k, s, _ in _OUTS}
    decoder_program(nc, A, O)
    r = run_bass_kernel_spmd(nc, [{f"in_{k}": v for k, v in arrays.items()}], core_ids=[0])
    return tuple(r.results[0][f"out_{k}"].reshape(shape) for k, _, shape in _OUTS)
```

```python
from contextlib import ExitStack

import numpy as np

import concourse.bass as bass
from concourse import mybir

F32 = mybir.dt.float32
F32R = mybir.dt.float32r
BF16 = mybir.dt.bfloat16
I32 = mybir.dt.int32
ALU = mybir.AluOpType
ACT = mybir.ActivationFunctionType
AX_X = mybir.AxisListType.X

P = 128
D = 1024
S = 1024
NS, TS = 8, 8
PAST, PAGE = 1024, 128
NPG = PAST // PAGE
C = 512
NH, NKV, HD = 8, 4, 64
NI, ID = 16, 64
TOPK = 256
W = 31
F = 2816
KT = D // P
CT = C // P
SR = NS * TS
ROWS = S + SR
NT = S // P + 1
SAMPLE = NT - 1
SKEYS = PAST + TS
FIRST = TOPK // P
NSEL = S // P - FIRST

U_VAL, U_GATE, Q_AT, KV_AT = 0, C, 2 * C, 2 * C + NH * HD
QI_AT = KV_AT + 2 * NKV * HD
KI_AT = QI_AT + NI * ID
KIW = ID + NI

FAR = -2.0e38
TAKEN = -3.0e38
DROP = -1.0e30
RMS_EPS, LN_EPS = 1e-6, 1e-5

RAW, SLOTS = 2, 6
N_KIW, N_QI, N_KV, N_Q, N_U, N_OUT, N_FFN = 0, 1, 9, 13, 17, 25, 33
FG = F // P // 2
BLOCKS = [(0, 384), (384, 768), (768, ROWS)]

ALL = [SAMPLE] + list(range(S // P))
SEL = [SAMPLE] + list(range(FIRST, S // P))
CHUNKS = [ALL, SEL, SEL, ALL, ALL, ALL, ALL]
BASE = [sum(len(c) for c in CHUNKS[:i]) for i in range(8)]

COUNT_ACT = (2, 4, NSEL)
COUNT_DVE = tuple(k for k in range(NSEL + 1) if k not in COUNT_ACT)
HALVINGS = 11
TAPS_BESIDE_U = 14

def rows_of(t):
    return SR if t == SAMPLE else P

def cols_of(t):
    return slice(t * P, t * P + rows_of(t))

def acc_at(t):
    return sum((j + 1) * P for j in range(FIRST, t))

def dve_parts(n):
    return max(0, n + 1 - 4 * NH)

def mask_at(t):
    return sum((j + 1) * P for j in range(t))

K_ID, K_TRI, K_COS, K_SIN = 0, P, 2 * P, 2 * P + NT * 16
K_M = K_SIN + NT * 16
K_E = K_M + SR
K_NEW = K_E + P
K_GQ = K_NEW + TS
K_GK = K_GQ + HD
K_CW = K_GK + HD
K_CB = K_CW + CT * W
K_LG = K_CB + CT
K_LB = K_LG + CT
K_IOTA = K_LB + CT
K_FEW = K_IOTA + 8
K_END = K_FEW + NSEL + 1

def shape_constants():
    f = np.zeros((P, K_END), np.float32)
    f[:, K_ID:K_ID + P] = np.eye(P)
    after = np.arange(P)[None, :] > np.arange(P)[:, None]
    f[:, K_TRI:K_TRI + P] = np.where(after, FAR, 0.0)
    half = HD // 8
    inv = (500000.0 ** (-np.arange(half, dtype=np.float32) / half)).astype(np.float32)
    pos = np.arange(S, dtype=np.float32).reshape(S // P, P).T
    pos = np.concatenate([pos, np.zeros((P, 1), np.float32)], 1)
    pos[:SR, SAMPLE] = PAST + np.arange(SR) % TS
    ang = (pos[:, :, None] * inv).astype(np.float32).astype(np.float64)
    cos, sin = np.cos(ang), np.sin(ang)
    f[:, K_COS:K_SIN] = np.concatenate([cos, cos], 2).reshape(P, -1)
    f[:, K_SIN:K_M] = np.concatenate([-sin, sin], 2).reshape(P, -1)
    r, c = np.arange(P)[:, None], np.arange(SR)[None, :]
    f[:, K_M:K_M + SR] = r % TS == c % TS
    f[:NI, K_E:K_E + P] = np.arange(NI)[:, None] == np.arange(P)[None, :] // TS
    f[:, K_IOTA:K_FEW] = np.arange(8)
    for k in range(NSEL + 1):
        keys = SKEYS if k == NSEL else (FIRST + k + 1) * P
        f[:, K_FEW + k] = keys - 2 * TOPK if k in COUNT_ACT else keys - TOPK
    f[:SR, K_NEW:K_NEW + TS] = np.where(np.arange(TS)[None, :] > np.arange(SR)[:, None] % TS, FAR, 0.0)
    b = np.zeros((P, P + NS * SR), np.float32)
    b[:, 0:P] = np.where(after, DROP, 0.0)
    bt, s, gt = np.arange(SR)[:, None, None], np.arange(NS)[None, :, None], np.arange(SR)[None, None, :]
    b[:SR, P:] = ((bt // TS == s) & (bt % TS == gt % TS)).reshape(SR, -1)
    return f, b

def decoder_program(nc, A, O):
    ctx = ExitStack()
    with ctx:
        def sb(name, shape, dt=F32):
            return ctx.enter_context(nc.sbuf_tensor(name, shape, dt))

        def sem(name):
            return ctx.enter_context(nc.semaphore(name))

        hi_t = sb("hi_t", [P, KT, ROWS], F32R)
        lo_t = sb("lo_t", [P, KT, ROWS], F32R)
        w_base = (nc.sbuf_base + 31) // 32 * 32
        w_hi = sb("w_hi", [P, SLOTS, D], F32R)
        w_lo = sb("w_lo", [P, SLOTS, D], F32R)
        w_raw = sb("w_raw", [P, RAW, D])
        kf = sb("kf", [P, K_END])
        kb = sb("kb", [P, P + NS * SR], BF16)
        half_neg = sb("half_neg", [P, 4 * NT])
        ms = sb("ms", [P, 2 * NT])
        rs = sb("rs", [P, 2 * NT])
        hs = sb("hs", [P, 4, 8])
        rt = sb("rt", [P, 2, NT * 16])
        wi_tok = sb("wi_tok", [P, NT, NI])
        wts = sb("wts", [NI, SR])
        kin_t = sb("kin_t", [ID, SR])
        m8 = sb("m8", [P, 8])
        ones = sb("ones", [P, P])
        stat = sb("stat", [P, 2, 16])
        mx = sb("mx", [P, 2])
        rinv = sb("rinv", [P, 8])
        lnr = sb("lnr", [P, NT])
        pages = sb("pages", [1, NS * NPG], I32)

        s_lo = sb("s_lo", [P, NSEL + 1])
        s_hi = sb("s_hi", [P, NSEL + 1])
        s_w = sb("s_w", [P, HALVINGS, NSEL + 1])
        s_mid = sb("s_mid", [P, NSEL + 1])
        s_cnt = sb("s_cnt", [P, NSEL + 1])
        s_few = sb("s_few", [P, NSEL + 1])
        s_up = sb("s_up", [P, NSEL + 1])
        s_add = sb("s_add", [P, NSEL + 1])
        s_m8 = sb("s_m8", [P, NSEL + 1, 8])
        s_eq = sb("s_eq", [P, 2, NSEL + 1, 8])
        s_thr = sb("s_thr", [P, 2, NSEL + 1])
        s_bad = sb("s_bad", [P, 1])
        s_row = sb("s_row", [1, P + 1])
        s_flag = sb("s_flag", [1, 1], I32)
        hk = sb("hk", [P, 2, NT * NKV])

        arena = (nc.sbuf_base + 31) // 32 * 32
        room = nc.sbuf_usable_end - arena

        def at(name, off, shape, dt=F32):
            return nc.alloc_sbuf_tensor_at(name, shape, dt, offset=arena + off)

        def at_w(name, off, shape, dt=F32):
            return nc.alloc_sbuf_tensor_at(name, shape, dt, offset=w_base + off)

        xin = at("xin", 0, [P, 3, D])
        xn = at("xn", 12288, [P, 2, D])
        sq = at("sq", 20480, [P, D])
        gbc = at("gbc", 24576, [P, D])
        qi_tok = at("qi_tok", 0, [P, NSEL + 1, D])
        qi_t = at("qi_t", 28672, [P, 2, 8, P])
        ki_t = at("ki_t", 36864, [P, S])
        acc = at("acc", 40960, [P, acc_at(S // P)])
        sacc = at("sacc", 57856, [SR, SKEYS])
        w_all = at("w_all", 57856, [P, NS, SR])
        rl = at("rl", 61984, [P, 2, SKEYS])
        kiw = at("kiw", 71200, [P, NT, KIW])
        kis_t = [at(f"kis_t{i}", 4128 * i, [ID, SKEYS]) for i in range(2)]
        qis_t = at("qis_t", 8256, [ID, NS, NI, TS])
        mneg = at("mneg", 0, [P, mask_at(S // P)], BF16)
        smneg = at("smneg", 9216, [SR, SKEYS], BF16)
        v_tok = at("v_tok", 11296, [P, NT, NKV * HD])
        k_t = at("k_t", 20512, [P, 2, ROWS])
        qst = at("qst", 29760, [P, 3, NH * HD])
        hsq = at("hsq", 35904, [P, NH * HD])
        hsq_k = at("hsq_k", 20512, [P, NT, NKV * HD])
        rt_k = at("rt_k", 20512, [P, 2, NT * NKV * 16])
        left = at("left", 20512, [P, 2, SKEYS])
        k_tok = at("k_tok", 61984, [P, NT, NKV * HD])
        PU = W - 1
        UC = PU + S + NS * (PU + TS)
        u = at("u", 29216, [P, CT, UC])
        y = at("y", 50944, [P, CT, ROWS])
        sig = at("sig", 64000, [P, 2, 384])
        u_last = at("u_last", 68352, [P, CT, PU + SR])
        cst = at("cst", 69856, [SR, 2, C])
        q_ld = at_w("q_ld", 4096, [P, 2, NH * HD])
        q_t = at_w("q_t", 8192, [P, 2, 4, P])
        sm = at_w("sm", 12288, [P, 3, S])
        pt = at_w("pt", 24576, [P, 2, S])
        o_tok = at_w("o_tok", 32768, [P, NH * HD])
        ysq = at_w("ysq", 34816, [P, CT, 384])
        lnd = at_w("lnd", 40960, [P, 3, P])
        kt_b = [at("kt_b0", 29216, [P, 2, SKEYS]), at("kt_b1", 50944, [P, 2, SKEYS])]
        v_b = [at("v_b0", 37472, [P, NPG, NKV * HD]), at("v_b1", 59200, [P, NPG, NKV * HD])]
        p_s = at("p_s", 45664, [P, SKEYS])
        pt_s = at("pt_s", 67392, [P, NPG + 1, P])
        o_s = at("o_s", 72000, [P, NKV * HD])
        v_new = at("v_new", 0, [TS, NS, NKV * HD])
        q_blk = at("q_blk", 11296, [P, NS, 2, SR])
        o_st = at("o_st", 15392, [P, 2, 4, P])
        mix_s = at("mix_s", 19488, [P, CT, SR])
        x1 = at("x1", 0, [P, NT, D])
        xn1 = at("xn1", 36864, [P, 2, D])
        sq1 = at("sq1", 45056, [P, D])
        gbc1 = at("gbc1", 49152, [P, D])
        f_hi = at("f_hi", 36864, [P, 2, ROWS], F32R)
        f_lo = at("f_lo", 45568, [P, 2, ROWS], F32R)
        sg = at("sg", 54272, [P, 2, 384])
        ff = at("ff", 57344, [P, 2, 384])
        assert 71200 + NT * KIW * 4 <= room, room

        q_scr = nc.dram_tensor("q_scratch", [NT, P, NH * HD], F32, kind="Internal").ap()

        ps = ctx.enter_context(nc.psum_tensor("ps", [P, 8, 512], F32))

        def wide(b, n, r=slice(0, P)):
            return ps[r, b:b + -(-n // 512), :].rearrange("p a b -> p (a b)")[:, 0:n]

        consts_in = sem("consts_in")
        consts_made = sem("consts_made")
        x_in = [sem(f"x_in{i}") for i in range(3)]
        g_in = sem("g_in")
        x1_in = sem("x1_in")
        ms_ready = sem("ms_ready")
        rs_ready = sem("rs_ready")
        xn_ready = sem("xn_ready")
        xt_done = sem("xt_done")
        hi_ready = sem("hi_ready")
        lo_ready = sem("lo_ready")
        raw_in = [sem(f"raw_in{i}") for i in range(RAW)]
        split_hi = sem("split_hi")
        split_lo = sem("split_lo")
        w_used = sem("w_used")
        proj_done = sem("proj_done")
        proj_evac = sem("proj_evac")
        dve_step = sem("dve_step")
        act_step = sem("act_step")
        pool_step = sem("pool_step")
        kiw_ready = sem("kiw_ready")
        qi_ready = sem("qi_ready")
        kit_ps = sem("kit_ps")
        kit_ready = sem("kit_ready")
        wx_done = sem("wx_done")
        wall_ready = sem("wall_ready")
        qit_ps = sem("qit_ps")
        qit_ready = sem("qit_ready")
        idx_mm = sem("idx_mm")
        relu_done = sem("relu_done")
        acc_done = sem("acc_done")
        kis_in = [sem(f"kis_in{i}") for i in range(2)]
        kin_done = sem("kin_done")
        qist_ps = sem("qist_ps")
        qist_ready = sem("qist_ready")
        sidx_mm = sem("sidx_mm")
        srelu_done = sem("srelu_done")
        sw_mm = sem("sw_mm")
        head_ms = sem("head_ms")
        head_rs = sem("head_rs")
        head_sq = sem("head_sq")
        k_ready = sem("k_ready")
        q_ready = sem("q_ready")
        q_out = [sem(f"q_out{i}") for i in range(3)]
        kt_ps = sem("kt_ps")
        kt_ready = sem("kt_ready")
        masks_ready = sem("masks_ready")
        u_mm = sem("u_mm")
        glu_sig = sem("glu_sig")
        glu_mul = sem("glu_mul")
        u_state = sem("u_state")
        sel_mid = sem("sel_mid")
        sel_cnt = sem("sel_cnt")
        bad_ready = sem("bad_ready")
        flag_in = sem("flag_in")
        round_done = sem("round_done")
        ut_ps = sem("ut_ps")
        ulast_ready = sem("ulast_ready")
        cst_ready = sem("cst_ready")
        cst_out = sem("cst_out")
        conv_done = sem("conv_done")
        mean_mm = sem("mean_mm")
        yc_ready = sem("yc_ready")
        ysq_ready = sem("ysq_ready")
        var_mm = sem("var_mm")
        lnv_ready = sem("lnv_ready")
        lnr_ready = sem("lnr_ready")
        lnd_ready = sem("lnd_ready")
        lnb_mm = sem("lnb_mm")
        yn_ready = sem("yn_ready")
        silu_done = sem("silu_done")
        mixc_hi = sem("mixc_hi")
        mixc_lo = sem("mixc_lo")
        q_in = [sem(f"q_in{i}") for i in range(2)]
        qt_ps = sem("qt_ps")
        qt_ready = sem("qt_ready")
        qk_done = sem("qk_done")
        sm_done = sem("sm_done")
        nmax = sem("nmax")
        exp_done = sem("exp_done")
        pt_ps = sem("pt_ps")
        pt_act = sem("pt_act")
        pt_dve = sem("pt_dve")
        pv_done = sem("pv_done")
        o_ready = sem("o_ready")
        ot_ps = sem("ot_ps")
        mixa_hi = sem("mixa_hi")
        mixa_lo = sem("mixa_lo")
        kv_in = [sem(f"kv_in{i}") for i in range(2)]
        vn_in = sem("vn_in")
        qblk_ready = sem("qblk_ready")
        sqt_ps = sem("sqt_ps")
        ktn_ready = sem("ktn_ready")
        sqk_done = sem("sqk_done")
        smax = sem("smax")
        sexp_done = sem("sexp_done")
        spt_ps = sem("spt_ps")
        spt_ready = sem("spt_ready")
        spv_done = sem("spv_done")
        so_ready = sem("so_ready")
        sot_ps = sem("sot_ps")
        sot_ready = sem("sot_ready")
        mixs_ready = sem("mixs_ready")
        mixs_hi = sem("mixs_hi")
        mixs_lo = sem("mixs_lo")
        x1_ready = sem("x1_ready")
        gate_mm = sem("gate_mm")
        up_mm = sem("up_mm")
        silu_f = sem("silu_f")
        f_ready = sem("f_ready")
        f_hi_ready = sem("f_hi_ready")
        f_lo_ready = sem("f_lo_ready")
        down_mm = sem("down_mm")
        y_added = sem("y_added")
        stores = sem("stores")
        fence_pool = sem("fence_pool")
        fence_dve = sem("fence_dve")

        ident = kf[:, K_ID:K_ID + P]
        nsteps = NSEL * NI
        ck = A["cache_kt"]

        def select_tile(k):
            if k == NSEL:
                return sacc[:, :], smneg[:, :], SR
            t = FIRST + k
            keys = (t + 1) * P
            return acc[:, acc_at(t):acc_at(t) + keys], mneg[:, mask_at(t):mask_at(t) + keys], P

        block = ctx.enter_context(nc.Block())

        @block.sync
        def _(sp):
            def unit_source(n):
                if n < N_QI:
                    return A["w_in"][:, KI_AT:KI_AT + KIW].rearrange("(k p) n -> p k n", p=P)
                if n < N_U:
                    c, pair = divmod(n - N_QI, 4)
                    col = [QI_AT, QI_AT + 512, KV_AT, Q_AT][c]
                    return A["w_in"][pair * 256:pair * 256 + 256, col:col + 512].rearrange("(k p) n -> p k n", p=P)
                if n < N_OUT:
                    ct, g = divmod(n - N_U, 2)
                    col = (U_GATE if g else U_VAL) + ct * P
                    return A["w_in"][:, col:col + P].rearrange("(k p) n -> p k n", p=P)
                c, pair = divmod(n - N_OUT, 4)
                return A["w_out"][pair * 256:pair * 256 + 256, c * 512:c * 512 + 512].rearrange(
                    "(k p) n -> p k n", p=P)

            def load_unit(n):
                if n >= RAW:
                    sp.wait_ge(split_lo, n - RAW + 1)
                dst = w_raw[:, n % RAW, :]
                if n < N_QI:
                    dst = dst[:, 0:KT * KIW].rearrange("p (k n) -> p k n", k=KT)
                elif N_U <= n < N_OUT:
                    dst = dst.rearrange("p (k n) -> p k n", k=KT)
                else:
                    dst = dst.rearrange("p (k n) -> p k n", k=2)
                sp.dma_start(dst, unit_source(n)).then_inc(raw_in[n % RAW], 16)

            def load_x(o):
                t = ALL[o]
                if o >= 3:
                    sp.wait_ge(xn_ready, o - 2)
                src = A["x_sample"] if t == SAMPLE else A["x_prompt"][cols_of(t), :]
                sp.dma_start(xin[0:rows_of(t), o % 3, :], src).then_inc(x_in[o % 3], 16)

            load_x(0)
            sp.dma_start(gbc[:, :], A["attn_norm_g"].broadcast_to([P, D])).then_inc(g_in, 16)
            load_x(1)
            load_x(2)
            sp.dma_start(kf[:, :], A["kf"]).then_inc(consts_in, 16)
            sp.dma_start(pages[:, :], A["page_table"]).then_inc(consts_in, 16)
            sp.dma_start(kb[:, :], A["kb"]).then_inc(consts_in, 16)
            load_unit(0)
            load_unit(1)
            for o in range(3, NT):
                load_x(o)
            sp.dma_start(O["conv_sample"][:, 0:PU - TS, :], A["state"][:, TS:PU, :]).then_inc(cst_out, 16)
            for n in range(2, 17):
                load_unit(n)
            sp.wait_ge(consts_in, 48)
            sp.wait_ge(qit_ps, NSEL)
            for b in range(NS):
                if b >= 2:
                    sp.wait_ge(sidx_mm, b - 1)
                for j in range(NPG):
                    pg = sp.value_load(pages[0:1, b * NPG + j:b * NPG + j + 1], min_val=0,
                                       max_val=ck.shape[0] - 1)
                    sp.dma_start(kis_t[b % 2][:, j * PAGE:(j + 1) * PAGE],
                                 A["cache_it"][bass.ds(pg, 1)].rearrange("o d s -> d (o s)")
                                 ).then_inc(kis_in[b % 2], 16)
            for n in range(17, 19):
                load_unit(n)
            sp.wait_ge(masks_ready, 2 + FIRST)
            for r in range(3):
                sp.wait_ge(q_out[r], 48)
            for ct in range(CT):
                dst = u[:, ct, PU + S:].rearrange("p (b w) -> p b w", b=NS)[:, :, 0:PU]
                sp.dma_start(dst, A["state_t"][ct * P:(ct + 1) * P]).then_inc(u_state, 16)
            for n in range(19, 27):
                load_unit(n)
            sp.wait_ge(u_mm, 3 * 4)
            for i in range(NT):
                if i >= 2:
                    sp.wait_ge(qt_ps, i - 1)
                r = rows_of(i)
                sp.dma_start(q_ld[0:r, i % 2, :], q_scr[i, 0:r, :]).then_inc(q_in[i % 2], 16)

            def load_sequence(b):
                if b >= 2:
                    sp.wait_ge(spv_done, b - 1)
                for j in range(NPG):
                    pg = sp.value_load(pages[0:1, b * NPG + j:b * NPG + j + 1], min_val=0,
                                       max_val=ck.shape[0] - 1)
                    sp.dma_start(kt_b[b % 2][:, :, j * PAGE:(j + 1) * PAGE],
                                 ck[bass.ds(pg, 1)].rearrange("o (a p) s -> p (o a) s", a=2)
                                 ).then_inc(kv_in[b % 2], 16)
                    sp.dma_start(v_b[b % 2][:, j, :],
                                 A["cache_v"][bass.ds(pg, 1)].rearrange("o s c -> s (o c)")
                                 ).then_inc(kv_in[b % 2], 16)

            sp.wait_ge(conv_done, 2 * CT)
            load_sequence(0)
            sp.wait_ge(mixa_lo, S // P)
            sp.wait_ge(mixa_hi, S // P)
            sp.dma_start(v_new[:, :, :], O["v_sample"].rearrange("b t c -> t b c")).then_inc(vn_in, 16)
            sp.wait_ge(mixc_lo, len(BLOCKS))
            sp.wait_ge(cst_out, 16 * 3)
            load_sequence(1)
            for b in range(2, NS):
                if b < 5:
                    load_unit(23 + 2 * b)
                    load_unit(24 + 2 * b)
                load_sequence(b)
            sp.wait_ge(mixs_lo, 1)
            sp.wait_ge(mixs_hi, 1)
            sp.dma_start(x1[:, 0:SAMPLE, :], A["x_prompt"].rearrange("(t p) d -> p t d", p=P)).then_inc(x1_in, 16)
            sp.dma_start(x1[0:SR, SAMPLE, :], A["x_sample"]).then_inc(x1_in, 16)
            sp.dma_start(gbc1[:, :], A["ffn_norm_g"].broadcast_to([P, D])).then_inc(g_in, 16)
            gv = A["w_gate"].rearrange("(k p) f -> p k f", p=P)
            uv = A["w_up"].rearrange("(k p) f -> p k f", p=P)
            with sp.Fori(0, FG) as g:
                for j in range(6):
                    sp.wait_ge(split_lo, g * 6 + (N_FFN + j - RAW + 1))
                    slot = (N_FFN + j) % RAW
                    c = 2 * g + (j // 2 if j < 4 else j - 4)
                    if j < 4:
                        sp.dma_start(w_raw[:, slot, :].rearrange("p (k n) -> p k n", k=KT),
                                     (gv, uv)[j % 2][:, :, bass.ds(c * P, P)]).then_inc(raw_in[slot], 16)
                    else:
                        sp.dma_start(w_raw[:, slot, :], A["w_down"][bass.ds(c * P, P), :]).then_inc(raw_in[slot], 16)
            for o in range(NT):
                t = ALL[o]
                sp.wait_ge(y_added, 1 + 2 * NT * (FG - 1) + 2 * o + 2)
                dst = O["y_sample"] if t == SAMPLE else O["y_prompt"][cols_of(t), :]
                sp.dma_start(dst, x1[0:rows_of(t), t, :]).then_inc(stores, 16)
            sp.wait_ge(stores, 16 * (6 + NT))

        @block.gpsimd
        def _(pool):
            pool.memset(half_neg[:, :], -0.5).then_inc(pool_step, 1)
            pool.memset(w_all[:, :, :], 0.0).then_inc(consts_made, 1)
            pool.memset(ones[:, :], 1.0 / C).then_inc(consts_made, 1)

            def width(n):
                return KT * KIW if n == 0 else D

            def used(n):
                if n == 0:
                    return proj_done, BASE[1]
                if N_U <= n < N_OUT:
                    return u_mm, 3 * (n - N_U + 1)
                c, i = divmod(n - N_QI, 4) if n < N_U else divmod(n - N_OUT, 4)
                late = 0 if n < N_U else 4
                return (w_used, 3 * (c + late) + i + 1) if i < 3 else (proj_done, BASE[c + late + 2])

            def split(n):
                w = width(n)
                pool.wait_ge(raw_in[n % RAW], 16 * (n // RAW + 1))
                if n >= SLOTS:
                    pool.wait_ge(*used(n - SLOTS))
                pool.tensor_copy(w_hi[:, n % SLOTS, 0:w], w_raw[:, n % RAW, 0:w]).then_inc(split_hi, 1)
                pool.wait_ge(split_hi, n + 1)
                pool.tensor_tensor(w_lo[:, n % SLOTS, 0:w], w_raw[:, n % RAW, 0:w],
                                   w_hi[:, n % SLOTS, 0:w].bitcast(F32), ALU.subtract).then_inc(split_lo, 1)

            def row_rs(q, r, width_):
                pool.wait_ge(ms_ready, q + 1)
                pool.tensor_scalar(rs[0:r, q:q + 1], ms[0:r, q:q + 1], 1.0 / width_, RMS_EPS,
                                   ALU.mult, ALU.add).then_inc(pool_step, 1)
                pool.wait_ge(pool_step, q + 2)
                pool.tensor_tensor(rs[0:r, q:q + 1], rs[0:r, q:q + 1], half_neg[0:r, 0:1],
                                   ALU.pow).then_inc(rs_ready, 1)

            def key_inverses():
                pool.wait_ge(head_ms, 1)
                m = SAMPLE * NKV
                pool.tensor_tensor(hk[:, 1, 0:m], hk[:, 0, 0:m], half_neg[:, 0:m], ALU.pow)
                pool.tensor_tensor(hk[0:SR, 1, m:], hk[0:SR, 0, m:], half_neg[0:SR, 0:NKV], ALU.pow).then_inc(head_rs, 1)

            def query_inverses(o):
                r = rows_of(ALL[o])
                pool.wait_ge(head_ms, o + 2)
                pool.tensor_tensor(hs[0:r, 2 + o % 2, :], hs[0:r, o % 2, :], half_neg[0:r, 0:NH], ALU.pow
                                   ).then_inc(head_rs, 1)

            for o in range(NT):
                row_rs(o, rows_of(ALL[o]), D)
                if o % 3 == 1:
                    split(o // 3)
            for n in range(3, 17):
                split(n)
            key_inverses()
            split(17)
            split(18)
            for o in range(NT):
                query_inverses(o)
            for n in range(19, 25):
                split(n)
            for k in range(len(BLOCKS)):
                pool.wait_ge(lnv_ready, k + 1)
                pool.tensor_tensor(lnr[:, 3 * k:3 * k + 3], lnr[:, 3 * k:3 * k + 3], half_neg[:, 0:3],
                                   ALU.pow).then_inc(lnr_ready, 1)
            pool.wait_ge(mixc_lo, len(BLOCKS))
            pool.wait_ge(qblk_ready, 1)
            for n in range(25, 33):
                split(n)
            for o in range(NT):
                row_rs(NT + o, rows_of(ALL[o]), D)
            for j in range(6):
                split(N_FFN + j)
            with pool.Fori(0, FG - 1) as g:
                for j in range(6):
                    n = N_FFN + 6 + j
                    slot, raw = n % SLOTS, n % RAW
                    pool.wait_ge(raw_in[raw], g * 48 + 16 * (n // RAW + 1))
                    if j < 4:
                        pool.wait_ge((gate_mm, up_mm)[j % 2], g * 6 + 3 * (j // 2 + 1))
                    elif j == 4:
                        pool.wait_ge(w_used, g + (3 * 6 + 1))
                    else:
                        pool.wait_ge(down_mm, g * (2 * NT) + (2 * NT + 1))
                    pool.sem_inc(fence_pool, 1)
                    pool.tensor_copy(w_hi[:, slot, :], w_raw[:, raw, :]).then_inc(split_hi, 1)
                    pool.wait_ge(split_hi, g * 6 + (n + 1))
                    pool.tensor_tensor(w_lo[:, slot, :], w_raw[:, raw, :], w_hi[:, slot, :].bitcast(F32),
                                       ALU.subtract).then_inc(split_lo, 1)

        @block.tensor
        def _(pe):
            def unit(n, k, width_):
                s = slice(k * width_, (k + 1) * width_)
                return w_hi[:, n % SLOTS, s], w_lo[:, n % SLOTS, s]

            def three(out, a_hi, a_lo, b_hi, b_lo, first, last):
                pe.matmul(out, a_hi, b_hi, start=first, stop=False)
                pe.matmul(out, a_hi, b_lo, start=False, stop=False)
                return pe.matmul(out, a_lo, b_hi, start=False, stop=last)

            def transpose_rows(q, src, r):
                pe.wait_ge(xn_ready, q + 1)
                if q % NT >= 4:
                    pe.wait_ge(hi_ready, q - 3)
                    pe.wait_ge(lo_ready, q - 3)
                for k in range(KT):
                    b = 2 * (q % NT % 4) + k // 4
                    mm = pe.transpose(ps[:, b, (k % 4) * P:(k % 4) * P + r], src[:, k * P:(k + 1) * P],
                                      ident[0:r, 0:r])
                mm.then_inc(xt_done, 1)

            def last_in_bank(c, t):
                first = 5 if c >= 5 else 0
                if t == 4:
                    return BASE[c] - BASE[first] + 1
                b = 4 if t == SAMPLE else t
                if c == first or b not in CHUNKS[c - 1]:
                    return None
                return BASE[c - 1] - BASE[first] + CHUNKS[c - 1].index(b) + 1

            def project(c, n0, width_, evac):
                tiles = CHUNKS[c]
                groups = [tiles[0:1], [t for t in tiles[1:] if t < 4], [t for t in tiles[1:] if t >= 4]]
                units = 1 if n0 == 0 else 4
                per = KT // units
                for gi, group in enumerate(groups):
                    for t in group:
                        before = last_in_bank(c, t)
                        if before is not None:
                            pe.wait_ge(evac, before)
                    for k in range(KT):
                        n = n0 + k // per
                        if gi == 0 and k % per == 0:
                            pe.wait_ge(split_lo, n + 1)
                        w = unit(n, k % per, width_)
                        for t in group:
                            r = rows_of(t)
                            out = ps[0:r, 4 if t == SAMPLE else t, 0:width_]
                            mm = three(out, hi_t[:, k, cols_of(t)], lo_t[:, k, cols_of(t)], *w, k == 0, k == KT - 1)
                            if k == KT - 1:
                                mm.then_inc(proj_done, 1)
                        if gi == 2 and k % per == per - 1 and k < KT - 1:
                            mm.then_inc(w_used, 1)

            pe.wait_ge(consts_in, 48)
            for o in range(NT):
                transpose_rows(o, xn[0:rows_of(ALL[o]), o % 2, :], rows_of(ALL[o]))
            pe.wait_ge(hi_ready, NT)
            pe.wait_ge(lo_ready, NT)
            project(0, N_KIW, KIW, proj_evac)
            project(1, N_QI, 512, proj_evac)
            project(2, N_QI + 4, 512, proj_evac)
            pe.wait_ge(proj_evac, BASE[3])
            pe.wait_ge(kiw_ready, 1)
            for t in range(S // P):
                pe.transpose(ps[0:ID, 6 + t // 4, (t % 4) * P:(t % 4 + 1) * P], kiw[:, t, 0:ID], ident)
            pe.transpose(ps[0:ID, 5, 0:SR], kiw[0:SR, SAMPLE, 0:ID], ident[0:SR, 0:SR])
            pe.transpose(ps[0:NI, 5, SR:2 * SR], wi_tok[0:SR, SAMPLE, :], ident[0:SR, 0:SR]).then_inc(kit_ps, 1)
            pe.wait_ge(kit_ready, 6)
            pe.matmul(ps[:, 5, 0:SR], kf[0:NI, K_E:K_E + P], wts[:, :], start=True, stop=True).then_inc(wx_done, 1)
            pe.wait_ge(wall_ready, 1)

            def index_transposes(i):
                pe.wait_ge(qi_ready, 2 * (NSEL + 1))
                if i > 0:
                    pe.wait_ge(qit_ready, 2 * i)
                for j in range(8):
                    mm = pe.transpose(ps[:, 6 + j // 4, (j % 4) * P:(j % 4 + 1) * P],
                                      qi_tok[:, i, j * P:(j + 1) * P], ident)
                mm.then_inc(qit_ps, 1)

            index_transposes(0)
            for i in range(NSEL):
                keys = (FIRST + i + 1) * P
                pe.wait_ge(qit_ready, 2 * i + 2)
                for h in range(NI):
                    n = i * NI + h
                    if n >= 3:
                        pe.wait_ge(relu_done, n - 2)
                    half = slice((h % 2) * ID, (h % 2 + 1) * ID)
                    for a in range(0, keys, 512):
                        w = min(512, keys - a)
                        mm = pe.matmul(ps[:, 2 * (n % 3) + a // 512, 0:w], qi_t[half, i % 2, h // 2, :],
                                       ki_t[half, a:a + w], start=True, stop=True)
                    mm.then_inc(idx_mm, 1)
                    if h == 3 and i + 1 < NSEL:
                        index_transposes(i + 1)
            pe.wait_ge(qit_ready, 2 * NSEL)
            for h in range(NI):
                mm = pe.transpose(ps[0:ID, 6 + h // 8, (h % 8) * SR:(h % 8 + 1) * SR],
                                  qi_tok[0:SR, NSEL, h * ID:(h + 1) * ID], ident[0:SR, 0:SR])
            mm.then_inc(qist_ps, 1)
            pe.wait_ge(qist_ready, 2)
            pe.wait_ge(relu_done, nsteps)
            KB = [(0, 512), (512, 1024), (1024, SKEYS)]

            def weigh(b):
                pe.wait_ge(srelu_done, b + 1)
                for j, (a, z) in enumerate(KB):
                    mm = pe.matmul(ps[0:SR, 3 + j, 0:z - a], w_all[:, b, :], rl[:, b % 2, a:z],
                                   start=(b == 0), stop=(b == NS - 1))
                mm.then_inc(sw_mm, 1)

            for b in range(NS):
                pe.wait_ge(kis_in[b % 2], 16 * NPG * (b // 2 + 1))
                pe.wait_ge(kin_done, b + 1)
                if b > 0:
                    pe.wait_ge(srelu_done, b)
                for j, (a, z) in enumerate(KB):
                    mm = pe.matmul(ps[:, j, 0:z - a], qis_t[:, b, :, :].rearrange("p h t -> p (h t)"),
                                   kis_t[b % 2][:, a:z], start=True, stop=True)
                mm.then_inc(sidx_mm, 1)
                if b > 0:
                    weigh(b - 1)
            weigh(NS - 1)
            pe.wait_ge(masks_ready, 1)
            project(3, N_KV, 512, proj_evac)
            project(4, N_Q, 512, proj_evac)
            pe.wait_ge(proj_evac, BASE[5])
            pe.wait_ge(k_ready, 1)
            for t in range(S // P):
                for p in range(2):
                    pe.transpose(ps[:, 2 * p + t // 4, (t % 4) * P:(t % 4 + 1) * P],
                                 k_tok[:, t, p * P:(p + 1) * P], ident)
            for p in range(2):
                mm = pe.transpose(ps[:, 4, p * SR:(p + 1) * SR], k_tok[0:SR, SAMPLE, p * P:(p + 1) * P],
                                  ident[0:SR, 0:SR])
            mm.then_inc(kt_ps, 1)
            pe.wait_ge(kt_ready, 3)
            for ct in range(CT):
                for g in range(2):
                    n = N_U + 2 * ct + g
                    pe.wait_ge(split_lo, n + 1)
                    for j, (a, z) in enumerate(BLOCKS):
                        s = (2 * ct + g) * 3 + j
                        if s >= 8:
                            before = s - 8
                            c2, g2, j2 = before // 6, before // 3 % 2, before % 3
                            pe.wait_ge(glu_sig if g2 else glu_mul, 3 * c2 + j2 + 1)
                        for k in range(KT):
                            w = unit(n, k, P)
                            mm = three(ps[:, s % 8, 0:z - a], *w, hi_t[:, k, a:z], lo_t[:, k, a:z],
                                       k == 0, k == KT - 1)
                        mm.then_inc(u_mm, 1)
            pe.wait_ge(ulast_ready, CT)
            pe.wait_ge(glu_mul, 3 * CT)
            pe.wait_ge(glu_sig, 3 * CT)
            for ct in range(CT):
                pe.transpose(ps[0:PU, 0, ct * P:(ct + 1) * P], u_last[:, ct, 0:PU], ident)
                mm = pe.transpose(ps[0:SR, 1, ct * P:(ct + 1) * P], u_last[:, ct, PU:], ident)
            mm.then_inc(ut_ps, 1)
            pe.wait_ge(cst_ready, 2)
            NA = NH * (S // P)

            def query_transposes(i):
                pe.wait_ge(q_in[i % 2], 16 * (i // 2 + 1))
                if i > 1:
                    pe.wait_ge(mixa_hi, i - 1)
                    pe.wait_ge(mixa_lo, i - 1)
                r = rows_of(i)
                for j in range(4):
                    mm = pe.transpose(ps[:, 7, j * P:j * P + r], q_ld[0:r, i % 2, j * P:(j + 1) * P], ident[0:r, 0:r])
                mm.then_inc(qt_ps, 1)

            def head(h):
                g = h // 2
                return g % 2, g // 2, (g // 2) * 2 + h % 2

            def scores(n):
                i, h = divmod(n, NH)
                if h == 0:
                    pe.wait_ge(qt_ready, i + 1)
                if n >= 2:
                    pe.wait_ge(sm_done, n - 1)
                kh, pair, j = head(h)
                half = slice(kh * HD, (kh + 1) * HD)
                keys = (i + 1) * P
                for a in range(0, keys, 512):
                    w = min(512, keys - a)
                    mm = pe.matmul(ps[:, 2 * (n % 2) + a // 512, 0:w], q_t[half, i % 2, j, :],
                                   k_t[half, pair, a:a + w], start=True, stop=True)
                mm.then_inc(qk_done, 1)

            def turn(n):
                i = n // NH
                pe.wait_ge(exp_done, n + 1)
                if n > 0:
                    pe.wait_ge(pt_act, n)
                if dve_parts(n - 1) > 0:
                    pe.wait_ge(pt_dve, dve_parts(n - 1))
                for s in range(i + 1):
                    mm = pe.transpose(ps[:, 4 + s // 4, (s % 4) * P:(s % 4 + 1) * P],
                                      sm[:, n % 3, s * P:(s + 1) * P], ident)
                mm.then_inc(pt_ps, 1)

            def values(n):
                i, h = divmod(n, NH)
                pe.wait_ge(pt_act, n + 1)
                if dve_parts(n) > 0:
                    pe.wait_ge(pt_dve, dve_parts(n))
                if h == 0 and i > 0:
                    pe.wait_ge(o_ready, i)
                for s in range(i + 1):
                    mm = pe.matmul(ps[:, 6, h * HD:(h + 1) * HD], pt[:, n % 2, s * P:(s + 1) * P],
                                   v_tok[:, s, (h // 2) * HD:(h // 2 + 1) * HD], start=(s == 0), stop=(s == i))
                mm.then_inc(pv_done, 1)

            def output_transposes(i):
                pe.wait_ge(o_ready, i + 1)
                pe.wait_ge(qt_ready, min(i + 2, S // P + 1))
                for j in range(4):
                    mm = pe.transpose(ps[:, 7, j * P:(j + 1) * P], o_tok[:, j * P:(j + 1) * P], ident)
                mm.then_inc(ot_ps, 1)

            query_transposes(0)
            for n in range(NA + 2):
                if n < NA:
                    scores(n)
                if n >= 1 and n - 1 < NA:
                    turn(n - 1)
                if n >= 2:
                    values(n - 2)
                if n % NH == 3 and n < NA:
                    query_transposes(n // NH + 1)
                if n % NH == 2 and n > NH:
                    output_transposes(n // NH - 1)
            output_transposes(S // P - 1)
            pe.wait_ge(conv_done, 2 * CT)
            pe.wait_ge(consts_made, 2)
            pe.wait_ge(sm_done, NA)
            for k, (a, z) in enumerate(BLOCKS):
                if k > 0:
                    pe.wait_ge(yc_ready, k)
                for ct in range(CT):
                    mm = pe.matmul(ps[:, 2, 0:z - a], ones[:, :], y[:, ct, a:z], start=(ct == 0), stop=(ct == CT - 1))
                mm.then_inc(mean_mm, 1)
                pe.wait_ge(ysq_ready, k + 1)
                for t in range(3 * k, 3 * k + 3):
                    r = rows_of(t)
                    for ct in range(CT):
                        mm = pe.matmul(ps[0:r, 3, t:t + 1], ysq[:, ct, t * P - a:t * P - a + r], ones[:, 0:1],
                                       start=(ct == 0), stop=(ct == CT - 1))
                mm.then_inc(var_mm, 1)
                pe.wait_ge(lnd_ready, k + 1)
                for t in range(3 * k, 3 * k + 3):
                    r = rows_of(t)
                    mm = pe.matmul(ps[:, 4, t * P - a:t * P - a + r], ones[0:r, :], lnd[0:r, t % 3, 0:r],
                                   start=True, stop=True)
                mm.then_inc(lnb_mm, 1)
            pe.wait_ge(mixa_hi, S // P)
            pe.wait_ge(mixa_lo, S // P)
            pe.wait_ge(yn_ready, len(BLOCKS))
            for pr in range(NS // 2):
                for par in range(2):
                    b = 2 * pr + par
                    pe.wait_ge(kv_in[par], 32 * NPG * (pr + 1))
                    pe.wait_ge(ktn_ready, b + 1)
                    if par == 0:
                        pe.wait_ge(qblk_ready, 1)
                        if pr > 0:
                            pe.wait_ge(sexp_done, pr)
                    rows = slice(par * SR, (par + 1) * SR)
                    for j, (a, z) in enumerate(KB):
                        out = ps[rows, j, 0:z - a]
                        pe.matmul(out, q_blk[:, b, 0, :], kt_b[par][:, 0, a:z], start=True, stop=False)
                        pe.matmul(out, q_blk[:, b, 1, :], kt_b[par][:, 1, a:z], start=False, stop=False)
                        mm = pe.matmul(out, kb[0:SR, P + b * SR:P + (b + 1) * SR], smneg[:, a:z],
                                       start=False, stop=True)
                mm.then_inc(sqk_done, 1)
                pe.wait_ge(sexp_done, pr + 1)
                if pr > 0:
                    pe.wait_ge(spt_ready, 2 * pr)
                for s in range(NPG + 1):
                    w = P if s < NPG else TS
                    mm = pe.transpose(ps[0:w, 3 + s // 4, (s % 4) * P:(s % 4 + 1) * P],
                                      p_s[:, s * P:s * P + w], ident)
                mm.then_inc(spt_ps, 1)
                pe.wait_ge(spt_ready, 2 * pr + 2)
                pe.wait_ge(vn_in, 16)
                if pr > 0:
                    pe.wait_ge(so_ready, pr)
                for par in range(2):
                    b = 2 * pr + par
                    rows = slice(par * SR, (par + 1) * SR)
                    for s in range(NPG + 1):
                        k = P if s < NPG else TS
                        v = v_b[par][:, s, :] if s < NPG else v_new[:, b, :]
                        mm = pe.matmul(ps[rows, 6, 0:NKV * HD], pt_s[0:k, s, rows], v, start=(s == 0), stop=(s == NPG))
                    mm.then_inc(spv_done, 1)
                pe.wait_ge(so_ready, pr + 1)
                if pr > 0:
                    pe.wait_ge(sot_ready, pr)
                for p in range(2):
                    mm = pe.transpose(ps[:, 7, p * P:(p + 1) * P], o_s[:, p * P:(p + 1) * P], ident)
                mm.then_inc(sot_ps, 1)
            pe.wait_ge(sot_ready, NS // 2)
            pe.wait_ge(mixs_hi, 1)
            pe.wait_ge(mixs_lo, 1)
            project(5, N_OUT, 512, x1_ready)
            project(6, N_OUT + 4, 512, x1_ready)
            pe.wait_ge(x1_ready, 2 * NT)
            for o in range(NT):
                transpose_rows(NT + o, xn1[0:rows_of(ALL[o]), o % 2, :], rows_of(ALL[o]))
            pe.wait_ge(hi_ready, 2 * NT)
            pe.wait_ge(lo_ready, 2 * NT)
            pe.sem_inc(down_mm, 1)
            with pe.Fori(0, FG) as g:
                for c in range(2):
                    for gu in range(2):
                        n = N_FFN + 2 * c + gu
                        pe.wait_ge(split_lo, g * 6 + (n + 1))
                        for j, (a, z) in enumerate(BLOCKS):
                            done = 3 * c + j
                            pe.wait_ge(f_ready if gu else silu_f, g * 6 + (1 + max(0, done - 2)))
                            for k in range(KT):
                                w = unit(n, k, P)
                                mm = three(ps[:, 3 * gu + j, 0:z - a], *w, hi_t[:, k, a:z], lo_t[:, k, a:z],
                                           k == 0, k == KT - 1)
                            mm.then_inc(up_mm if gu else gate_mm, 1)
                pe.wait_ge(f_hi_ready, g * 6 + 6)
                pe.wait_ge(f_lo_ready, g * 6 + 6)
                pe.wait_ge(split_lo, g * 6 + (N_FFN + 6))
                for o in range(NT):
                    t = ALL[o]
                    r = rows_of(t)
                    for nh in range(2):
                        pe.wait_ge(y_added, g * (2 * NT) + (1 + max(0, 2 * o + nh - 1)))
                        for c in range(2):
                            n = N_FFN + 4 + c
                            mm = three(ps[0:r, 6 + nh, :], f_hi[:, c, cols_of(t)], f_lo[:, c, cols_of(t)],
                                       *unit(n, nh, 512), c == 0, c == 1)
                            if o == NT - 1 and nh == 1 and c == 0:
                                mm.then_inc(w_used, 1)
                        mm.then_inc(down_mm, 1)

        @block.scalar
        def _(act):
            steps = [0]

            def link(ins):
                steps[0] += 1
                ins.then_inc(act_step, 1)
                act.wait_ge(act_step, steps[0])

            def square_rows(q, src, junk, r):
                if q > 0:
                    act.wait_ge(ms_ready, q)
                act.activation(junk[0:r, :], src, ACT.Square, accum_out=ms[0:r, q:q + 1]).then_inc(ms_ready, 1)

            def take_hi(q):
                t = ALL[q % NT]
                r = rows_of(t)
                act.wait_ge(xt_done, q + 1)
                for half in range(2):
                    b = 2 * (q % NT % 4) + half
                    ins = act.activation(hi_t[:, 4 * half:4 * half + 4, cols_of(t)],
                                         ps[:, b, :].rearrange("p (k c) -> p k c", k=4)[:, :, 0:r], ACT.Copy)
                ins.then_inc(hi_ready, 1)

            for o in range(NT + 1):
                if o < NT:
                    t = ALL[o]
                    act.wait_ge(x_in[o % 3], 16 * (o // 3 + 1))
                    square_rows(o, xin[0:rows_of(t), o % 3, :], sq, rows_of(t))
                if o > 0:
                    take_hi(o - 1)
            for o, t in enumerate(CHUNKS[0]):
                r = rows_of(t)
                act.wait_ge(proj_done, BASE[0] + o + 1)
                act.activation(kiw[0:r, t, :], ps[0:r, 4 if t == SAMPLE else t, 0:KIW], ACT.Copy
                               ).then_inc(proj_evac, 1)
            act.wait_ge(kiw_ready, 1)
            act.dma_start(O["ki_prompt"].rearrange("(t p) d -> p t d", p=P), kiw[:, 0:SAMPLE, 0:ID]).then_inc(stores, 16)
            act.dma_start(O["ki_sample"], kiw[0:SR, SAMPLE, 0:ID]).then_inc(stores, 16)
            for c in (1, 2):
                for o, t in enumerate(CHUNKS[c]):
                    r = rows_of(t)
                    act.wait_ge(proj_done, BASE[c] + o + 1)
                    act.activation(qi_tok[0:r, t - FIRST, (c - 1) * 512:c * 512],
                                   ps[0:r, 4 if t == SAMPLE else t, :], ACT.Copy).then_inc(proj_evac, 1)
            act.wait_ge(kit_ps, 1)
            for b in range(2):
                for half in range(2):
                    act.activation(ki_t[half * ID:(half + 1) * ID, b * 512:(b + 1) * 512], ps[0:ID, 6 + b, :],
                                   ACT.Copy).then_inc(kit_ready, 1)
            act.activation(kin_t[:, :], ps[0:ID, 5, 0:SR], ACT.Copy).then_inc(kit_ready, 1)
            act.activation(wts[:, :], ps[0:NI, 5, SR:2 * SR], ACT.Copy).then_inc(kit_ready, 1)

            def take_index_queries(i):
                act.wait_ge(qit_ps, i + 1)
                for b in range(2):
                    act.activation(qi_t[:, i % 2, 4 * b:4 * b + 4, :],
                                   ps[:, 6 + b, :].rearrange("p (j c) -> p j c", j=4), ACT.Copy
                                   ).then_inc(qit_ready, 1)

            take_index_queries(0)
            for i in range(NSEL):
                keys = (FIRST + i + 1) * P
                for h in range(NI):
                    n = i * NI + h
                    act.wait_ge(idx_mm, n + 1)
                    if n >= 2:
                        act.wait_ge(acc_done, n - 1)
                    act.activation(rl[:, n % 2, 0:keys], wide(2 * (n % 3), keys), ACT.Relu).then_inc(relu_done, 1)
                    if h == 8 and i + 1 < NSEL:
                        take_index_queries(i + 1)
            act.wait_ge(qist_ps, 1)
            for b in range(2):
                for hh in range(2):
                    ins = act.activation(
                        qis_t[:, :, 8 * b + 4 * hh:8 * b + 4 * hh + 4, :].rearrange("p b h t -> p h b t"),
                        ps[0:ID, 6 + b, hh * 256:(hh + 1) * 256].rearrange("p (h b t) -> p h b t", h=4, b=NS), ACT.Copy)
                ins.then_inc(qist_ready, 1)
            act.wait_ge(acc_done, nsteps)
            for b in range(NS):
                if b >= 2:
                    act.wait_ge(sidx_mm, b - 1)
                act.activation(kis_t[b % 2][:, PAST:SKEYS], kin_t[:, b * TS:(b + 1) * TS], ACT.Copy).then_inc(kin_done, 1)
                act.wait_ge(sidx_mm, b + 1)
                if b >= 2:
                    act.wait_ge(sw_mm, b - 1)
                act.activation(rl[:, b % 2, :], wide(0, SKEYS), ACT.Relu).then_inc(srelu_done, 1)

            def take_keys_values(o):
                t = CHUNKS[3][o]
                r = rows_of(t)
                src = ps[0:r, 4 if t == SAMPLE else t, :]
                act.wait_ge(proj_done, BASE[3] + o + 1)
                act.activation(v_tok[0:r, t, :], src[:, 256:512], ACT.Copy)
                act.activation(k_tok[0:r, t, :], src[:, 0:256], ACT.Copy).then_inc(proj_evac, 1)

            act.wait_ge(masks_ready, 1)
            for i in range(HALVINGS):
                act.wait_ge(sel_mid, i + 1)
                for k in COUNT_ACT:
                    work, place, r = select_tile(k)
                    act.activation(place, work, ACT.Sign, bias=s_mid[0:r, k:k + 1], scale=-1.0,
                                   accum_out=s_cnt[0:r, k:k + 1]).then_inc(sel_cnt, 1)
                if i == 2:
                    take_keys_values(0)
                if i == 7:
                    for o in range(1, 5):
                        take_keys_values(o)
            for o in range(5, NT):
                take_keys_values(o)
            act.wait_ge(proj_evac, BASE[4])
            act.activation(hsq_k[:, 0:SAMPLE, :], k_tok[:, 0:SAMPLE, :], ACT.Square)
            act.activation(hsq_k[0:SR, SAMPLE, :], k_tok[0:SR, SAMPLE, :], ACT.Square).then_inc(head_sq, 1)

            for o in range(NT + 1):
                if o < NT:
                    t = ALL[o]
                    r = rows_of(t)
                    src = ps[0:r, 4 if t == SAMPLE else t, :]
                    act.wait_ge(proj_done, BASE[4] + o + 1)
                    if o >= 3:
                        act.wait_ge(q_out[o % 3], 16 * (o // 3))
                    qs = qst[0:r, o % 3, :]
                    for a in range(2):
                        ins = act.activation(
                            qs[:, a * 256:(a + 1) * 256].rearrange("p (r k d) -> p k r d", r=2, k=2),
                            src[:, a * 256:(a + 1) * 256].rearrange("p (k r d) -> p k r d", k=2, r=2), ACT.Copy)
                    link(ins)
                    if o > 0:
                        act.wait_ge(head_ms, o + 1)
                    act.activation(hsq[0:r, :], qs, ACT.Square).then_inc(proj_evac, 1)
                if o > 0:
                    r = rows_of(ALL[o - 1])
                    act.wait_ge(q_ready, o)
                    act.dma_start(q_scr[ALL[o - 1], 0:r, :], qst[0:r, (o - 1) % 3, :]).then_inc(q_out[(o - 1) % 3], 16)
                if o == 1:
                    act.wait_ge(k_ready, 1)
                    act.dma_start(O["k_prompt"].rearrange("(t p) d -> p t d", p=P), k_tok[:, 0:SAMPLE, :]).then_inc(stores, 16)
                    act.dma_start(O["k_sample"], k_tok[0:SR, SAMPLE, :]).then_inc(stores, 16)
                    act.dma_start(O["v_prompt"].rearrange("(t p) d -> p t d", p=P), v_tok[:, 0:SAMPLE, :]).then_inc(stores, 16)
                    act.dma_start(O["v_sample"].rearrange("b t c -> (b t) c"), v_tok[0:SR, SAMPLE, :]).then_inc(stores, 16)
            act.wait_ge(bad_ready, 1)
            act.dma_start(s_row[0:1, 0:P], s_bad[:, :]).then_inc(flag_in, 16)
            act.wait_ge(kt_ps, 1)
            for p in range(2):
                act.activation(k_t[:, p, 0:S], wide(2 * p, S), ACT.Copy).then_inc(kt_ready, 1)
            act.activation(k_t[:, :, S:ROWS], ps[:, 4, 0:2 * SR].rearrange("p (a c) -> p a c", a=2), ACT.Copy
                           ).then_inc(kt_ready, 1)
            act.wait_ge(stores, 16 * 6)
            for ct in range(CT):
                for j, (a, z) in enumerate(BLOCKS):
                    n = 3 * ct + j
                    s = (2 * ct + 1) * 3 + j
                    act.wait_ge(u_mm, s + 1)
                    if n >= 2:
                        act.wait_ge(glu_mul, n - 1)
                    act.activation(sig[:, n % 2, 0:z - a], ps[:, s % 8, 0:z - a], ACT.Sigmoid).then_inc(glu_sig, 1)
            act.wait_ge(ut_ps, 1)
            act.activation(cst[0:PU, 0, :], ps[0:PU, 0, :], ACT.Copy).then_inc(cst_ready, 1)
            act.activation(cst[:, 1, :], ps[0:SR, 1, :], ACT.Copy).then_inc(cst_ready, 1)
            act.wait_ge(cst_ready, 2)
            act.dma_start(O["conv_prompt"], cst[0:PU, 0, :]).then_inc(cst_out, 16)
            act.dma_start(O["conv_sample"][:, PU - TS:PU, :], cst[:, 1, :]).then_inc(cst_out, 16)
            NA = NH * (S // P)

            def take_queries(i):
                act.wait_ge(qt_ps, i + 1)
                r = rows_of(i)
                act.activation(q_t[:, i % 2, :, 0:r], ps[:, 7, :].rearrange("p (j c) -> p j c", j=4)[:, :, 0:r],
                               ACT.Copy).then_inc(qt_ready, 1)

            def exps(n):
                i = n // NH
                keys = (i + 1) * P
                act.wait_ge(nmax, n + 1)
                act.activation(sm[:, n % 3, 0:keys], sm[:, n % 3, 0:keys], ACT.Exp, bias=stat[:, 0, n % 16:n % 16 + 1],
                               scale=HD ** -0.5, accum_out=stat[:, 1, n % 16:n % 16 + 1]).then_inc(exp_done, 1)

            def take_weights(n):
                keys = (n // NH + 1) * P
                act.wait_ge(pt_ps, n + 1)
                if n >= 2:
                    act.wait_ge(pv_done, n - 1)
                act.activation(pt[:, n % 2, 0:min(keys, 512)], ps[:, 4, 0:min(keys, 512)], ACT.Copy
                               ).then_inc(pt_act, 1)

            def take_outputs(i):
                act.wait_ge(ot_ps, i + 1)
                act.activation(hi_t[:, CT:KT, cols_of(i)], ps[:, 7, :].rearrange("p (j c) -> p j c", j=4), ACT.Copy
                               ).then_inc(mixa_hi, 1)

            take_queries(0)
            for n in range(NA + 2):
                if n < NA:
                    if n % NH == 0 and n >= 2 * NH:
                        act.wait_ge(o_ready, n // NH - 1)
                    exps(n)
                if n >= 1 and n - 1 < NA:
                    take_weights(n - 1)
                if n % NH == 4 and n < NA:
                    take_queries(n // NH + 1)
                if n % NH == 3 and n > NH or n == NA + 1:
                    take_outputs(n // NH - 1 if n < NA else S // P - 1)
            for k, (a, z) in enumerate(BLOCKS):
                act.wait_ge(yc_ready, k + 1)
                if k > 0:
                    act.wait_ge(var_mm, k)
                act.activation(ysq[:, :, 0:z - a], y[:, :, a:z], ACT.Square).then_inc(ysq_ready, 1)
                act.wait_ge(yn_ready, k + 1)
                for ct in range(CT):
                    ins = act.activation(y[:, ct, a:z], y[:, ct, a:z], ACT.Silu, bias=kf[:, K_LB + ct:K_LB + ct + 1],
                                         scale=kf[:, K_LG + ct:K_LG + ct + 1])
                link(ins)
                act.activation(hi_t[:, 0:CT, a:z], y[:, :, a:z], ACT.Copy).then_inc(mixc_hi, 1)
            for pr in range(NS // 2):
                for par in range(2):
                    b = 2 * pr + par
                    if b == 0:
                        act.wait_ge(mixc_lo, len(BLOCKS))
                        act.wait_ge(mixa_lo, S // P)
                        act.wait_ge(cst_out, 16 * 3)
                    if b >= 2:
                        act.wait_ge(spv_done, b - 1)
                    act.activation(kt_b[par][:, :, PAST:SKEYS], k_t[:, :, S + b * TS:S + (b + 1) * TS], ACT.Copy
                                   ).then_inc(ktn_ready, 1)
                act.wait_ge(smax, pr + 1)
                if pr > 0:
                    act.wait_ge(spt_ps, pr)
                    act.wait_ge(so_ready, pr)
                act.activation(p_s[:, :], wide(0, SKEYS), ACT.Exp, bias=stat[:, 0, 0:1], scale=HD ** -0.5,
                               accum_out=stat[:, 1, 0:1]).then_inc(sexp_done, 1)
                act.wait_ge(spt_ps, pr + 1)
                if pr > 0:
                    act.wait_ge(spv_done, 2 * pr)
                act.activation(pt_s[:, 0:NPG, :], wide(3, NPG * P).rearrange("p (s c) -> p s c", s=NPG), ACT.Copy
                               ).then_inc(spt_ready, 1)
                act.activation(pt_s[0:TS, NPG, :], ps[0:TS, 5, 0:P], ACT.Copy).then_inc(spt_ready, 1)
                act.wait_ge(sot_ps, pr + 1)
                act.activation(o_st[:, :, pr, :], ps[:, 7, 0:2 * P].rearrange("p (a c) -> p a c", a=2), ACT.Copy
                               ).then_inc(sot_ready, 1)
            act.wait_ge(mixs_ready, 1)
            act.activation(hi_t[:, CT:KT, cols_of(SAMPLE)], mix_s[:, :, :], ACT.Copy).then_inc(mixs_hi, 1)
            for o in range(NT + 1):
                if o < NT:
                    t = ALL[o]
                    act.wait_ge(x1_ready, NT + o + 1)
                    square_rows(NT + o, x1[0:rows_of(t), t, :], sq1, rows_of(t))
            for o in range(NT):
                take_hi(NT + o)
            act.wait_ge(lo_ready, 2 * NT)
            act.sem_inc(silu_f, 1)
            with act.Fori(0, FG) as g:
                for m in range(7):
                    if m < 6:
                        a, z = BLOCKS[m % 3]
                        act.wait_ge(gate_mm, g * 6 + (m + 1))
                        act.wait_ge(f_ready, g * 6 + (1 + max(0, m - 1)))
                        act.activation(sg[:, m % 2, 0:z - a], ps[:, m % 3, 0:z - a], ACT.Silu).then_inc(silu_f, 1)
                    if m > 0:
                        c, j = divmod(m - 1, 3)
                        a, z = BLOCKS[j]
                        if m == 1:
                            act.wait_ge(down_mm, g * (2 * NT) + 1)
                        act.wait_ge(f_ready, g * 6 + (1 + m))
                        act.activation(f_hi[:, c, a:z], ff[:, (m - 1) % 2, 0:z - a], ACT.Copy).then_inc(f_hi_ready, 1)

        @block.vector
        def _(dve):
            steps = [0]

            def link(ins):
                steps[0] += 1
                ins.then_inc(dve_step, 1)
                dve.wait_ge(dve_step, steps[0])

            def norm_rows(q, src, dst, g_tile, r):
                dve.wait_ge(rs_ready, q + 1)
                if q % NT >= 2:
                    dve.wait_ge(xt_done, q - 1)
                dve.scalar_tensor_tensor(dst, src, rs[0:r, q:q + 1], g_tile[0:r, :], ALU.mult, ALU.mult
                                         ).then_inc(xn_ready, 1)

            def take_lo(q):
                t = ALL[q % NT]
                r = rows_of(t)
                dve.wait_ge(hi_ready, q + 1)
                for half in range(2):
                    b = 2 * (q % NT % 4) + half
                    ks = slice(4 * half, 4 * half + 4)
                    ins = dve.tensor_tensor(lo_t[:, ks, cols_of(t)],
                                            ps[:, b, :].rearrange("p (k c) -> p k c", k=4)[:, :, 0:r],
                                            hi_t[:, ks, cols_of(t)].bitcast(F32), ALU.subtract)
                ins.then_inc(lo_ready, 1)

            def rope(x, cos, sin, t1, t2):
                dve.tensor_tensor(t1, x[:, :, 0:16], cos, ALU.mult)
                dve.tensor_tensor(t2[:, :, 0:8], x[:, :, 8:16], sin[:, :, 0:8], ALU.mult)
                link(dve.tensor_tensor(t2[:, :, 8:16], x[:, :, 0:8], sin[:, :, 8:16], ALU.mult))
                return dve.tensor_tensor(x[:, :, 0:16], t1, t2, ALU.add)

            def rope_tile(x, t, heads):
                r = rows_of(t)
                cos = kf[0:r, K_COS + 16 * t:K_COS + 16 * t + 16].unsqueeze(1).broadcast_to([r, heads, 16])
                sin = kf[0:r, K_SIN + 16 * t:K_SIN + 16 * t + 16].unsqueeze(1).broadcast_to([r, heads, 16])
                t1, t2 = (rt[0:r, i, 0:heads * 16].rearrange("p (h d) -> p h d", h=heads) for i in range(2))
                return rope(x, cos, sin, t1, t2)

            dve.memset(lnr[:, :], 1.0)
            link(dve.memset(rt[:, :, :], 0.0))
            dve.wait_ge(g_in, 16)
            for o in range(NT + 1):
                if o < NT:
                    r = rows_of(ALL[o])
                    norm_rows(o, xin[0:r, o % 3, :], xn[0:r, o % 2, :], gbc, r)
                if o > 0:
                    take_lo(o - 1)
            dve.wait_ge(consts_in, 48)
            dve.wait_ge(proj_evac, NT)
            for t0, t1, r in ((0, SAMPLE, P), (SAMPLE, NT, SR)):
                cos = kf[0:r, K_COS + 16 * t0:K_COS + 16 * t1].rearrange("p (t d) -> p t d", d=16)
                sin = kf[0:r, K_SIN + 16 * t0:K_SIN + 16 * t1].rearrange("p (t d) -> p t d", d=16)
                ta, tb = (rt[0:r, i, 0:(t1 - t0) * 16].rearrange("p (h d) -> p h d", d=16) for i in range(2))
                link(rope(kiw[0:r, t0:t1, 0:ID], cos, sin, ta, tb))
                ins = dve.tensor_scalar(wi_tok[0:r, t0:t1, :], kiw[0:r, t0:t1, ID:KIW], (NI * ID) ** -0.5, None, ALU.mult)
            ins.then_inc(kiw_ready, 1)
            for c in (1, 2):
                for o, t in enumerate(CHUNKS[c]):
                    r = rows_of(t)
                    dve.wait_ge(proj_evac, BASE[c] + o + 1)
                    if BASE[c] + o > NT:
                        dve.wait_ge(qi_ready, BASE[c] + o - NT)
                    x = qi_tok[0:r, t - FIRST, (c - 1) * 512:c * 512].rearrange("p (h d) -> p h d", d=ID)
                    rope_tile(x, t, 8).then_inc(qi_ready, 1)
            dve.wait_ge(wx_done, 1)
            dve.wait_ge(consts_made, 1)
            for b in range(NS):
                s = slice(b * TS, (b + 1) * TS)
                ins = dve.tensor_tensor(w_all[:, b, s], ps[:, 5, s], kf[:, K_M + b * TS:K_M + (b + 1) * TS], ALU.mult)
            ins.then_inc(wall_ready, 1)
            for i in range(NSEL):
                t = FIRST + i
                a0, keys = acc_at(t), (t + 1) * P
                for h in range(NI):
                    n = i * NI + h
                    dve.wait_ge(relu_done, n + 1)
                    w = wi_tok[:, t, h:h + 1]
                    if h == 0:
                        dve.tensor_scalar(acc[:, a0:a0 + t * P], rl[:, n % 2, 0:t * P], w, None, ALU.mult)
                        dve.scalar_tensor_tensor(acc[:, a0 + t * P:a0 + keys], rl[:, n % 2, t * P:keys], w,
                                                 kf[:, K_TRI:K_TRI + P], ALU.mult, ALU.add).then_inc(acc_done, 1)
                    else:
                        dve.wait_ge(acc_done, n)
                        dve.scalar_tensor_tensor(acc[:, a0:a0 + keys], rl[:, n % 2, 0:keys], w, acc[:, a0:a0 + keys],
                                                 ALU.mult, ALU.add).then_inc(acc_done, 1)
            dve.wait_ge(sw_mm, NS)
            dve.tensor_copy(sacc[:, 0:PAST], wide(3, PAST, slice(0, SR)))
            dve.tensor_tensor(sacc[:, PAST:SKEYS], ps[0:SR, 5, 0:TS], kf[0:SR, K_NEW:K_NEW + TS], ALU.add
                              ).then_inc(masks_ready, 1)

            dve.memset(s_lo[:, :], 0.0)
            dve.memset(s_hi[:, :], 0.0)
            dve.memset(s_cnt[:, :], 0.0)
            link(dve.tensor_scalar(s_m8[:, :, :], kf[:, K_IOTA:K_IOTA + 8].unsqueeze(1).broadcast_to([P, NSEL + 1, 8]),
                                   -1.0, None, ALU.mult))
            dve.wait_ge(masks_ready, 1)
            for k in range(NSEL + 1):
                work, place, r = select_tile(k)
                dve.tensor_reduce(s_lo[0:r, k:k + 1], work[:, 0:TOPK], AX_X, ALU.min)
                ins = dve.reduce_max(s_hi[0:r, k:k + 1], work, AX_X)
            link(ins)
            link(dve.tensor_tensor(s_up[:, :], s_hi[:, :], s_lo[:, :], ALU.subtract))
            for i in range(HALVINGS):
                ins = dve.tensor_scalar(s_w[:, i, :], s_up[:, :], 0.5 ** (i + 1), None, ALU.mult)
            link(ins)
            dve.tensor_tensor(s_mid[:, :], s_lo[:, :], s_w[:, 0, :], ALU.add).then_inc(sel_mid, 1)
            dve.wait_ge(sel_mid, 1)
            for i in range(HALVINGS):
                for k in COUNT_DVE:
                    work, place, r = select_tile(k)
                    ins = dve.tensor_scalar(place, work, s_mid[0:r, k:k + 1], None, ALU.is_lt, ALU.add,
                                            accum_out=s_cnt[0:r, k:k + 1])
                link(ins)
                dve.wait_ge(sel_cnt, len(COUNT_ACT) * (i + 1))
                link(dve.tensor_tensor(s_few[:, :], s_cnt[:, :], kf[:, K_FEW:K_FEW + NSEL + 1], ALU.is_le))
                dve.scalar_tensor_tensor(s_up[:, :], s_few[:, :], 3.0e38, s_mid[:, :], ALU.mult, ALU.add)
                link(dve.tensor_tensor(s_add[:, :], s_few[:, :], s_w[:, i, :], ALU.mult))
                ins = dve.tensor_tensor(s_hi[:, :], s_hi[:, :], s_up[:, :], ALU.min)
                if i < HALVINGS - 1:
                    link(dve.tensor_tensor(s_lo[:, :], s_lo[:, :], s_add[:, :], ALU.add))
                    dve.tensor_tensor(s_mid[:, :], s_lo[:, :], s_w[:, i + 1, :], ALU.add).then_inc(sel_mid, 1)
                    dve.wait_ge(sel_mid, i + 2)
                else:
                    link(ins)

            dve.wait_ge(head_sq, 1)
            parts = ((slice(0, P), slice(0, SAMPLE)), (slice(0, SR), slice(SAMPLE, NT)))
            for r, t in parts:
                n = (t.stop - t.start) * NKV
                ins = dve.tensor_reduce(hk[r, 0, t.start * NKV:t.stop * NKV],
                                        hsq_k[r, t, :].rearrange("p t (h d) -> p (t h) d", d=HD), AX_X, ALU.add)
            link(ins)
            for r, t in parts:
                h = hk[r, 0, t.start * NKV:t.stop * NKV]
                ins = dve.tensor_scalar(h, h, 1.0 / HD, RMS_EPS, ALU.mult, ALU.add)
            ins.then_inc(head_ms, 1)
            dve.wait_ge(head_rs, 1)
            for r, t in parts:
                n = (t.stop - t.start) * NKV
                x = k_tok[r, t, :].rearrange("p t (h d) -> p (t h) d", d=HD)
                ins = dve.tensor_tensor(x, x, hk[r, 1, t.start * NKV:t.stop * NKV].unsqueeze(2).broadcast_to(
                    [r.stop, n, HD]), ALU.mult)
            link(ins)
            for r, t in parts:
                n = (t.stop - t.start) * NKV
                x = k_tok[r, t, :].rearrange("p t (h d) -> p (t h) d", d=HD)
                ins = dve.tensor_tensor(x, x, kf[r, K_GK:K_GK + HD].unsqueeze(1).broadcast_to([r.stop, n, HD]), ALU.mult)
            link(ins)
            for r, t in parts:
                nt = t.stop - t.start
                cos, sin = (kf[r, c + 16 * t.start:c + 16 * t.stop].rearrange("p (t d) -> p t d", d=16)
                            for c in (K_COS, K_SIN))
                x = k_tok[r, t, :].rearrange("p t (h d) -> p t h d", d=HD)
                t1, t2 = (rt_k[r, i, t.start * NKV * 16:t.stop * NKV * 16].rearrange("p (t h d) -> p t h d", t=nt, h=NKV)
                          for i in range(2))
                for h in range(NKV):
                    dve.tensor_tensor(t1[:, :, h, :], x[:, :, h, 0:16], cos, ALU.mult)
                    dve.tensor_tensor(t2[:, :, h, 0:8], x[:, :, h, 8:16], sin[:, :, 0:8], ALU.mult)
                    ins = dve.tensor_tensor(t2[:, :, h, 8:16], x[:, :, h, 0:8], sin[:, :, 8:16], ALU.mult)
                link(ins)
                for h in range(NKV):
                    ins = dve.tensor_tensor(x[:, :, h, 0:16], t1[:, :, h, :], t2[:, :, h, :], ALU.add)
            ins.then_inc(k_ready, 1)

            def largest_left(k):
                work, place, r = select_tile(k)
                keys = work.shape[1]
                link(dve.tensor_scalar(place, work, s_hi[0:r, k:k + 1], None, ALU.is_gt, ALU.add,
                                       accum_out=s_cnt[0:r, k:k + 1]))
                link(dve.scalar_tensor_tensor(left[0:r, k % 2, 0:keys], place, TAKEN, work, ALU.mult, ALU.add))
                dve.max(s_m8[0:r, k, :], left[0:r, k % 2, 0:keys])

            for o in range(NT):
                t = ALL[o]
                r = rows_of(t)
                x = qst[0:r, o % 3, :].rearrange("p (h d) -> p h d", d=HD)
                dve.wait_ge(proj_evac, BASE[4] + o + 1)
                link(dve.tensor_reduce(hs[0:r, o % 2, :], hsq[0:r, :].rearrange("p (h d) -> p h d", d=HD), AX_X, ALU.add))
                dve.tensor_scalar(hs[0:r, o % 2, :], hs[0:r, o % 2, :], 1.0 / HD, RMS_EPS,
                                  ALU.mult, ALU.add).then_inc(head_ms, 1)
                if o <= NSEL:
                    if o == 0:
                        link(dve.memset(s_cnt[:, :], float(TOPK - 1)))
                        dve.wait_ge(k_ready, 1)
                    largest_left(o)
                dve.wait_ge(head_rs, o + 2)
                link(dve.tensor_tensor(x, x, hs[0:r, 2 + o % 2, :].unsqueeze(2).broadcast_to([r, NH, HD]), ALU.mult))
                link(dve.tensor_tensor(x, x, kf[0:r, K_GQ:K_GQ + HD].unsqueeze(1).broadcast_to([r, NH, HD]), ALU.mult))
                if o > 0:
                    dve.wait_ge(q_ready, o)
                rope_tile(x, t, NH).then_inc(q_ready, 1)

            rank, iota = s_up, kf[:, K_IOTA:K_IOTA + 8].unsqueeze(1).broadcast_to([P, NSEL + 1, 8])
            link(dve.tensor_scalar(rank[:, :], s_cnt[:, :], -1.0, float(TOPK), ALU.mult, ALU.add))
            link(dve.tensor_scalar(s_add[:, :], rank[:, :], -1.0, None, ALU.add))
            dve.tensor_tensor(s_eq[:, 0], iota, s_add[:, :].unsqueeze(2).broadcast_to([P, NSEL + 1, 8]), ALU.is_equal)
            link(dve.tensor_tensor(s_eq[:, 1], iota, rank[:, :].unsqueeze(2).broadcast_to([P, NSEL + 1, 8]), ALU.is_equal))
            for i in range(2):
                ins = dve.tensor_tensor(s_eq[:, i], s_eq[:, i], s_m8[:, :, :], ALU.mult)
            link(ins)
            for i in range(2):
                ins = dve.tensor_reduce(s_thr[:, i], s_eq[:, i], AX_X, ALU.add)
            link(ins)
            dve.tensor_tensor(s_few[:, :], s_thr[:, 1], s_thr[:, 0], ALU.is_ge)
            link(dve.tensor_scalar(s_lo[:, :], rank[:, :], 8.0, None, ALU.is_ge))
            link(dve.tensor_tensor(s_few[:, :], s_few[:, :], s_lo[:, :], ALU.max))
            dve.reduce_max(s_bad[:, :], s_few[:, :], AX_X).then_inc(bad_ready, 1)
            for k in range(NSEL + 1):
                work, place, r = select_tile(k)
                ins = dve.tensor_scalar(place, work, s_thr[0:r, 0, k:k + 1], DROP, ALU.is_lt, ALU.mult)
            link(ins)
            dve.wait_ge(flag_in, 16)
            link(dve.reduce_max(s_row[:, P:P + 1], s_row[:, 0:P], AX_X))
            link(dve.tensor_copy(s_flag[:, :], s_row[:, P:P + 1]))
            again = dve.value_load(s_flag[0:1, 0:1], min_val=0, max_val=1)
            with dve.If(again > 0):
                base = 0
                for k in range(NSEL + 1):
                    work, place, r = select_tile(k)
                    with dve.Fori(0, TOPK // 8) as i:
                        dve.max(m8[0:r, :], work).then_inc(round_done, 1)
                        dve.wait_ge(round_done, 2 * i + (base + 1))
                        dve.sem_inc(fence_dve, 1)
                        dve.match_replace(work, m8[0:r, :], work, TAKEN).then_inc(round_done, 1)
                        dve.wait_ge(round_done, 2 * i + (base + 2))
                    base += 2 * (TOPK // 8) + 1
                    dve.tensor_scalar(place, work, TAKEN, DROP, ALU.not_equal, ALU.mult).then_inc(round_done, 1)
                dve.wait_ge(round_done, base)
            for t in range(FIRST):
                if t > 0:
                    dve.memset(mneg[:, mask_at(t):mask_at(t) + t * P], 0.0)
                dve.tensor_copy(mneg[:, mask_at(t) + t * P:mask_at(t + 1)], kb[:, 0:P]).then_inc(masks_ready, 1)
            link(dve.memset(s_lo[:, :], 0.0))
            dve.sem_inc(masks_ready, 1)

            def conv_taps(first, last):
                for q in range(first, last):
                    ct, j = divmod(q, W)
                    if q == 0:
                        dve.wait_ge(u_state, 16 * CT)
                    w = kf[:, K_CW + q:K_CW + q + 1]
                    up = u[:, ct, j:j + S]
                    un = u[:, ct, PU + S:].rearrange("p (b w) -> p b w", b=NS)[:, :, j:j + TS]
                    yp, ys = y[:, ct, 0:S], y[:, ct, S:ROWS].rearrange("p (b t) -> p b t", b=NS)
                    if j == 0:
                        bias = kf[:, K_CB + ct:K_CB + ct + 1]
                        dve.tensor_scalar(yp, up, w, bias, ALU.mult, ALU.add)
                        link(dve.tensor_scalar(ys, un, w, bias, ALU.mult, ALU.add))
                    elif j < W - 1:
                        dve.scalar_tensor_tensor(yp, up, w, yp, ALU.mult, ALU.add)
                        link(dve.scalar_tensor_tensor(ys, un, w, ys, ALU.mult, ALU.add))
                    else:
                        dve.scalar_tensor_tensor(yp, up, w, yp, ALU.mult, ALU.add).then_inc(conv_done, 1)
                        dve.scalar_tensor_tensor(ys, un, w, ys, ALU.mult, ALU.add).then_inc(conv_done, 1)

            dve.wait_ge(kt_ready, 3)
            dve.wait_ge(stores, 16 * 6)
            for r in range(3):
                dve.wait_ge(q_out[r], 48)
            dve.memset(u[:, :, 0:PU], 0.0)
            for ct in range(CT):
                new = u[:, ct, PU + S:].rearrange("p (b w) -> p b w", b=NS)[:, :, PU:]
                for j, (a, z) in enumerate(BLOCKS):
                    n = 3 * ct + j
                    s = 2 * ct * 3 + j
                    dve.wait_ge(glu_sig, n + 1)
                    if z <= S:
                        ins = dve.tensor_tensor(u[:, ct, PU + a:PU + z], ps[:, s % 8, 0:z - a], sig[:, n % 2, 0:z - a],
                                                ALU.mult)
                    else:
                        dve.tensor_tensor(u[:, ct, PU + a:PU + S], ps[:, s % 8, 0:S - a], sig[:, n % 2, 0:S - a],
                                          ALU.mult)
                        ins = dve.tensor_tensor(new, ps[:, s % 8, S - a:z - a].rearrange("p (b t) -> p b t", b=NS),
                                                sig[:, n % 2, S - a:z - a].rearrange("p (b t) -> p b t", b=NS), ALU.mult)
                    ins.then_inc(glu_mul, 1)
                dve.wait_ge(glu_mul, 3 * ct + 3)
                dve.tensor_copy(u_last[:, ct, 0:PU], u[:, ct, S:S + PU])
                dve.tensor_copy(u_last[:, ct, PU:].rearrange("p (b t) -> p b t", b=NS), new).then_inc(ulast_ready, 1)
                if ct < CT - 1:
                    conv_taps(TAPS_BESIDE_U * ct, TAPS_BESIDE_U * (ct + 1))
            NA = NH * (S // P)

            def mask_scores(n):
                i = n // NH
                keys = (i + 1) * P
                dve.wait_ge(qk_done, n + 1)
                if n >= 3:
                    dve.wait_ge(pt_ps, n - 2)
                if n == 0:
                    dve.wait_ge(u_mm, 3 * 2 * CT)
                dve.tensor_tensor_reduce(sm[:, n % 3, 0:keys], wide(2 * (n % 2), keys),
                                         mneg[:, mask_at(i):mask_at(i) + keys], 1.0, -3.0e38, ALU.add, ALU.max,
                                         mx[:, n % 2:n % 2 + 1]).then_inc(sm_done, 1)
                dve.wait_ge(sm_done, n + 1)
                if n >= 16:
                    dve.wait_ge(exp_done, n - 15)
                dve.tensor_scalar(stat[:, 0, n % 16:n % 16 + 1], mx[:, n % 2:n % 2 + 1], -(HD ** -0.5), None, ALU.mult
                                  ).then_inc(nmax, 1)

            def take_weights(n):
                keys = (n // NH + 1) * P
                if keys <= 512:
                    return
                dve.wait_ge(pt_ps, n + 1)
                dve.wait_ge(pv_done, n - 1)
                dve.tensor_copy(pt[:, n % 2, 512:keys], ps[:, 5, 0:keys - 512]).then_inc(pt_dve, 1)

            def outputs(i):
                dve.wait_ge(exp_done, NH * (i + 1))
                link(dve.reciprocal(rinv[:, :], stat[:, 1, i % 2 * NH:(i % 2 + 1) * NH]))
                dve.wait_ge(pv_done, NH * (i + 1))
                if i > 0:
                    dve.wait_ge(ot_ps, i)
                dve.tensor_tensor(o_tok[:, :].rearrange("p (h d) -> p h d", d=HD),
                                  ps[:, 6, :].rearrange("p (h d) -> p h d", d=HD),
                                  rinv[:, :].unsqueeze(2).broadcast_to([P, NH, HD]), ALU.mult).then_inc(o_ready, 1)

            def lows(i):
                dve.wait_ge(mixa_hi, i + 1)
                dve.tensor_tensor(lo_t[:, CT:KT, cols_of(i)], ps[:, 7, :].rearrange("p (j c) -> p j c", j=4),
                                  hi_t[:, CT:KT, cols_of(i)].bitcast(F32), ALU.subtract).then_inc(mixa_lo, 1)

            taken = TAPS_BESIDE_U * (CT - 1)
            weight = [n // NH + 1 for n in range(NA)]
            for n in range(NA + 2):
                if n < NA:
                    mask_scores(n)
                    until = TAPS_BESIDE_U * (CT - 1) + -(-(CT * W - TAPS_BESIDE_U * (CT - 1)) * sum(weight[:n + 1])
                                                         // sum(weight))
                    conv_taps(taken, until)
                    taken = until
                if n >= 1 and n - 1 < NA:
                    take_weights(n - 1)
                if n % NH == 1 and n > NH:
                    outputs(n // NH - 1)
                if n % NH == 3 and n > NH:
                    lows(n // NH - 1)
            lows(S // P - 1)
            dve.wait_ge(conv_done, 2 * CT)
            for k, (a, z) in enumerate(BLOCKS):
                dve.wait_ge(mean_mm, k + 1)
                for ct in range(CT):
                    ins = dve.tensor_tensor(y[:, ct, a:z], y[:, ct, a:z], ps[:, 2, 0:z - a], ALU.subtract)
                ins.then_inc(yc_ready, 1)
                dve.wait_ge(var_mm, k + 1)
                if k == 2:
                    dve.tensor_scalar(lnr[0:SR, SAMPLE:NT], ps[0:SR, 3, SAMPLE:NT], LN_EPS, None, ALU.add)
                full = slice(3 * k, min(3 * k + 3, SAMPLE))
                dve.tensor_scalar(lnr[:, full], ps[:, 3, full], LN_EPS, None, ALU.add).then_inc(lnv_ready, 1)
                dve.wait_ge(lnr_ready, k + 1)
                if k > 0:
                    dve.wait_ge(lnb_mm, k)
                for t in range(3 * k, 3 * k + 3):
                    r = rows_of(t)
                    ins = dve.tensor_scalar(lnd[0:r, t % 3, 0:r], ident[0:r, 0:r], lnr[0:r, t:t + 1], float(C),
                                            ALU.mult, ALU.mult)
                ins.then_inc(lnd_ready, 1)
                dve.wait_ge(lnb_mm, k + 1)
                for ct in range(CT):
                    ins = dve.tensor_tensor(y[:, ct, a:z], y[:, ct, a:z], ps[:, 4, 0:z - a], ALU.mult)
                ins.then_inc(yn_ready, 1)
                dve.wait_ge(mixc_hi, k + 1)
                dve.tensor_tensor(lo_t[:, 0:CT, a:z], y[:, :, a:z], hi_t[:, 0:CT, a:z].bitcast(F32), ALU.subtract
                                  ).then_inc(mixc_lo, 1)
            link(dve.memset(q_blk[:, :, :, :], 0.0))
            dve.wait_ge(qt_ready, S // P + 1)
            for h in range(NH):
                kh, pair, j = (h // 2) % 2, h // 4, (h // 4) * 2 + h % 2
                half = slice(kh * HD, (kh + 1) * HD)
                ins = dve.tensor_copy(q_blk[half, :, pair, h * TS:(h + 1) * TS],
                                      q_t[half, 0, j, 0:SR].rearrange("p (b t) -> p b t", b=NS))
            ins.then_inc(qblk_ready, 1)
            for pr in range(NS // 2):
                dve.wait_ge(sqk_done, pr + 1)
                link(dve.reduce_max(mx[:, 0:1], wide(0, SKEYS), AX_X))
                dve.tensor_scalar(stat[:, 0, 0:1], mx[:, 0:1], -(HD ** -0.5), None, ALU.mult).then_inc(smax, 1)
                dve.wait_ge(sexp_done, pr + 1)
                link(dve.reciprocal(rinv[:, 0:1], stat[:, 1, 0:1]))
                dve.wait_ge(spv_done, 2 * pr + 2)
                if pr > 0:
                    dve.wait_ge(sot_ps, pr)
                dve.tensor_scalar(o_s[:, :], ps[:, 6, 0:NKV * HD], rinv[:, 0:1], None, ALU.mult).then_inc(so_ready, 1)
            dve.wait_ge(sot_ready, NS // 2)
            for h in range(NH):
                kh, pair = (h // 2) % 2, h // 4
                src = o_st[kh * HD:(kh + 1) * HD, pair, :, :].rearrange("p a (b c) -> p (a b) c", b=2)
                dst = mix_s[(h % 2) * HD:(h % 2 + 1) * HD, h // 2, :].rearrange("p (b t) -> p b t", b=NS)
                ins = dve.tensor_copy(dst, src[:, :, h * TS:(h + 1) * TS])
            ins.then_inc(mixs_ready, 1)
            dve.wait_ge(mixs_hi, 1)
            dve.tensor_tensor(lo_t[:, CT:KT, cols_of(SAMPLE)], mix_s[:, :, :],
                              hi_t[:, CT:KT, cols_of(SAMPLE)].bitcast(F32), ALU.subtract).then_inc(mixs_lo, 1)
            dve.wait_ge(x1_in, 32)
            for n in range(2 * NT):
                t, c = ALL[n % NT], n // NT
                r = rows_of(t)
                dve.wait_ge(proj_done, BASE[5] + n + 1)
                xs = x1[0:r, t, c * 512:(c + 1) * 512]
                dve.tensor_tensor(xs, xs, ps[0:r, 4 if t == SAMPLE else t, :], ALU.add).then_inc(x1_ready, 1)
            dve.wait_ge(g_in, 32)
            for o in range(NT + 1):
                if o < NT:
                    t = ALL[o]
                    r = rows_of(t)
                    norm_rows(NT + o, x1[0:r, t, :], xn1[0:r, o % 2, :], gbc1, r)
                if o > 0:
                    take_lo(NT + o - 1)
            dve.sem_inc(f_ready, 1)
            dve.sem_inc(y_added, 1)
            with dve.Fori(0, FG) as g:
                for m in range(7):
                    if m < 6:
                        a, z = BLOCKS[m % 3]
                        dve.wait_ge(up_mm, g * 6 + (m + 1))
                        dve.wait_ge(silu_f, g * 6 + (m + 2))
                        if m >= 2:
                            dve.wait_ge(f_hi_ready, g * 6 + (m - 1))
                            dve.wait_ge(f_lo_ready, g * 6 + (m - 1))
                        dve.tensor_tensor(ff[:, m % 2, 0:z - a], ps[:, 3 + m % 3, 0:z - a], sg[:, m % 2, 0:z - a],
                                          ALU.mult).then_inc(f_ready, 1)
                    if m > 0:
                        c, j = divmod(m - 1, 3)
                        a, z = BLOCKS[j]
                        dve.wait_ge(f_hi_ready, g * 6 + m)
                        dve.tensor_tensor(f_lo[:, c, a:z], ff[:, (m - 1) % 2, 0:z - a], f_hi[:, c, a:z].bitcast(F32),
                                          ALU.subtract).then_inc(f_lo_ready, 1)
                dve.wait_ge(y_added, g * (2 * NT) + 1)
                for o in range(NT):
                    t = ALL[o]
                    r = rows_of(t)
                    for nh in range(2):
                        dve.wait_ge(down_mm, g * (2 * NT) + (2 * o + nh + 2))
                        xs = x1[0:r, t, nh * 512:(nh + 1) * 512]
                        dve.tensor_tensor(xs, xs, ps[0:r, 6 + nh, :], ALU.add).then_inc(y_added, 1)

_OUTS = [
    ("y_prompt", (S, D), (1, S, D)), ("y_sample", (SR, D), (NS, TS, D)),
    ("k_prompt", (S, NKV * HD), (1, 1, S, NKV, HD)), ("v_prompt", (S, NKV * HD), (1, 1, S, NKV, HD)),
    ("ki_prompt", (S, ID), (1, 1, S, ID)), ("conv_prompt", (W - 1, C), (1, 1, W - 1, C)),
    ("k_sample", (SR, NKV * HD), (1, NS, TS, NKV, HD)), ("v_sample", (NS, TS, NKV * HD), (1, NS, TS, NKV, HD)),
    ("ki_sample", (SR, ID), (1, NS, TS, ID)), ("conv_sample", (NS, W - 1, C), (1, NS, W - 1, C)),
]

def kernel(**inputs):
    import ml_dtypes
    import concourse.bacc as bacc
    from concourse.bass_utils import run_bass_kernel_spmd

    a = {k: np.asarray(v) for k, v in inputs.items()}
    pool = a["cache_k"].shape[1]
    f, b = shape_constants()

    def spread(row, at, kf):
        kf[:, at:at + row.size] = row.reshape(1, -1)

    def by_channel(x):
        return x.reshape(-1, CT, P).transpose(2, 1, 0).reshape(P, -1)

    spread(a["q_norm_g"][0], K_GQ, f)
    spread(a["k_norm_g"][0], K_GK, f)
    f[:, K_CW:K_CB] = by_channel(a["conv_dw_w"][0])
    f[:, K_CB:K_LG] = by_channel(a["conv_dw_b"][0])
    f[:, K_LG:K_LB] = by_channel(a["conv_ln_g"][0])
    f[:, K_LB:K_IOTA] = by_channel(a["conv_ln_b"][0])
    arrays = {
        "x_prompt": a["x_prompt"][0], "x_sample": a["x_sample"].reshape(SR, D),
        "cache_kt": a["cache_k"][0].reshape(pool, PAGE, NKV * HD).transpose(0, 2, 1),
        "cache_v": a["cache_v"][0].reshape(pool, PAGE, NKV * HD),
        "cache_it": a["cache_idx_k"][0].transpose(0, 2, 1),
        "state_t": a["state_conv"][0].transpose(2, 0, 1), "state": a["state_conv"][0],
        "page_table": a["page_table"].reshape(1, -1),
        "attn_norm_g": a["attn_norm_g"], "ffn_norm_g": a["ffn_norm_g"],
        "w_in": a["w_in"][0], "w_out": a["w_out"][0], "w_gate": a["w_gate"][0], "w_up": a["w_up"][0],
        "w_down": a["w_down"][0], "kf": f, "kb": b.astype(ml_dtypes.bfloat16),
    }
    arrays = {k: np.ascontiguousarray(v) for k, v in arrays.items()}
    nc = bacc.Bacc("TRN2", target_bir_lowering=False, num_devices=1)
    A = {k: nc.dram_tensor(f"in_{k}", v.shape, mybir.dt.from_np(v.dtype), kind="ExternalInput").ap()
         for k, v in arrays.items()}
    O = {k: nc.dram_tensor(f"out_{k}", s, F32, kind="ExternalOutput").ap() for k, s, _ in _OUTS}
    decoder_program(nc, A, O)
    r = run_bass_kernel_spmd(nc, [{f"in_{k}": v for k, v in arrays.items()}], core_ids=[0])
    return tuple(r.results[0][f"out_{k}"].reshape(shape) for k, _, shape in _OUTS)
```

```python
from contextlib import ExitStack

import numpy as np

import concourse.bass as bass
from concourse import mybir

F32 = mybir.dt.float32
F32R = mybir.dt.float32r
BF16 = mybir.dt.bfloat16
I32 = mybir.dt.int32
ALU = mybir.AluOpType
ACT = mybir.ActivationFunctionType
AX_X = mybir.AxisListType.X

P = 128
D = 1024
S = 1024
NS, TS = 8, 8
PAST, PAGE = 1024, 128
NPG = PAST // PAGE
C = 512
NH, NKV, HD = 8, 4, 64
NI, ID = 16, 64
TOPK = 256
W = 31
F = 2816
KT = D // P
CT = C // P
SR = NS * TS
ROWS = S + SR
NT = S // P + 1
SAMPLE = NT - 1
SKEYS = PAST + TS
FIRST = TOPK // P
NSEL = S // P - FIRST

U_VAL, U_GATE, Q_AT, KV_AT = 0, C, 2 * C, 2 * C + NH * HD
QI_AT = KV_AT + 2 * NKV * HD
KI_AT = QI_AT + NI * ID
KIW = ID + NI

FAR = -2.0e38
TAKEN = -3.0e38
DROP = -1.0e30
RMS_EPS, LN_EPS = 1e-6, 1e-5

RAW, SLOTS = 2, 6
N_KIW, N_QI, N_KV, N_Q, N_U, N_OUT, N_FFN = 0, 1, 9, 13, 17, 25, 33
FG = F // P // 2
AHEAD = 4
BLOCKS = [(0, 384), (384, 768), (768, ROWS)]

ALL = [SAMPLE] + list(range(S // P))
SEL = [SAMPLE] + list(range(FIRST, S // P))
CHUNKS = [[], SEL, SEL, ALL, ALL, ALL, ALL]
NX1 = 7
BASE = [sum(len(c) for c in CHUNKS[:i]) for i in range(8)]

COUNT_ACT = (2, 4, NSEL)
COUNT_DVE = tuple(k for k in range(NSEL + 1) if k not in COUNT_ACT)
HALVINGS = 11
CONV_HEADS = 45
LN_AT = (46, 48, 50, 55, 57, 58, 63, 65, 66)
TAP_STOPS = (0, 14, 28, 40, 51)

def rows_of(t):
    return SR if t == SAMPLE else P

def cols_of(t):
    return slice(t * P, t * P + rows_of(t))

def acc_at(t):
    return sum((j + 1) * P for j in range(FIRST, t))

def dve_parts(n):
    return max(0, n + 1 - 4 * NH)

def mask_at(t):
    return sum((j + 1) * P for j in range(t))

K_ID, K_TRI, K_COS, K_SIN = 0, P, 2 * P, 2 * P + NT * 16
K_M = K_SIN + NT * 16
K_E = K_M + SR
K_NEW = K_E + P
K_GQ = K_NEW + TS
K_GK = K_GQ + HD
K_CW = K_GK + HD
K_CB = K_CW + CT * W
K_LG = K_CB + CT
K_LB = K_LG + CT
K_IOTA = K_LB + CT
K_FEW = K_IOTA + 8
K_END = K_FEW + NSEL + 1

def shape_constants():
    f = np.zeros((P, K_END), np.float32)
    f[:, K_ID:K_ID + P] = np.eye(P)
    after = np.arange(P)[None, :] > np.arange(P)[:, None]
    f[:, K_TRI:K_TRI + P] = np.where(after, FAR, 0.0)
    half = HD // 8
    inv = (500000.0 ** (-np.arange(half, dtype=np.float32) / half)).astype(np.float32)
    pos = np.arange(S, dtype=np.float32).reshape(S // P, P).T
    pos = np.concatenate([pos, np.zeros((P, 1), np.float32)], 1)
    pos[:SR, SAMPLE] = PAST + np.arange(SR) % TS
    ang = (pos[:, :, None] * inv).astype(np.float32).astype(np.float64)
    cos, sin = np.cos(ang), np.sin(ang)
    f[:, K_COS:K_SIN] = np.concatenate([cos, cos], 2).reshape(P, -1)
    f[:, K_SIN:K_M] = np.concatenate([-sin, sin], 2).reshape(P, -1)
    r, c = np.arange(P)[:, None], np.arange(SR)[None, :]
    f[:, K_M:K_M + SR] = r % TS == c % TS
    f[:NI, K_E:K_E + P] = np.arange(NI)[:, None] == np.arange(P)[None, :] // TS
    f[:, K_IOTA:K_FEW] = np.arange(8)
    for k in range(NSEL + 1):
        keys = SKEYS if k == NSEL else (FIRST + k + 1) * P
        f[:, K_FEW + k] = keys - 2 * TOPK if k in COUNT_ACT else keys - TOPK
    f[:SR, K_NEW:K_NEW + TS] = np.where(np.arange(TS)[None, :] > np.arange(SR)[:, None] % TS, FAR, 0.0)
    b = np.zeros((P, P + NS * SR), np.float32)
    b[:, 0:P] = np.where(after, DROP, 0.0)
    bt, s, gt = np.arange(SR)[:, None, None], np.arange(NS)[None, :, None], np.arange(SR)[None, None, :]
    b[:SR, P:] = ((bt // TS == s) & (bt % TS == gt % TS)).reshape(SR, -1)
    return f, b

def decoder_program(nc, A, O):
    ctx = ExitStack()
    with ctx:
        def sb(name, shape, dt=F32):
            return ctx.enter_context(nc.sbuf_tensor(name, shape, dt))

        def sem(name):
            return ctx.enter_context(nc.semaphore(name))

        hi_t = sb("hi_t", [P, KT, ROWS], F32R)
        lo_t = sb("lo_t", [P, KT, ROWS], F32R)
        w_base = (nc.sbuf_base + 31) // 32 * 32
        w_hi = sb("w_hi", [P, SLOTS, D], F32R)
        w_lo = sb("w_lo", [P, SLOTS, D], F32R)
        w_raw = sb("w_raw", [P, RAW, D])
        kf = sb("kf", [P, K_END])
        kb = sb("kb", [P, P + NS * SR], BF16)
        ident_r = sb("ident_r", [P, P], F32R)
        half_neg = sb("half_neg", [P, 4 * NT])
        ms = sb("ms", [P, 2 * NT])
        rs = sb("rs", [P, 2 * NT])
        hs = sb("hs", [P, 4, 8])
        rt = sb("rt", [P, 2, SAMPLE * 16])
        wi_tok = sb("wi_tok", [P, NT, NI])
        wts = sb("wts", [NI, SR])
        kin_t = sb("kin_t", [ID, SR])
        m8 = sb("m8", [P, 8])
        ones = sb("ones", [P, P])
        stat = sb("stat", [P, 2, 16])
        mx = sb("mx", [P, 2])
        rinv = sb("rinv", [P, 8])
        lnr = sb("lnr", [P, NT])
        pages = sb("pages", [1, NS * NPG], I32)

        s_lo = sb("s_lo", [P, NSEL + 1])
        s_hi = sb("s_hi", [P, NSEL + 1])
        s_w = sb("s_w", [P, HALVINGS, NSEL + 1])
        s_mid = sb("s_mid", [P, NSEL + 1])
        s_cnt = sb("s_cnt", [P, NSEL + 1])
        s_few = sb("s_few", [P, NSEL + 1])
        s_up = sb("s_up", [P, NSEL + 1])
        s_add = sb("s_add", [P, NSEL + 1])
        s_m8 = sb("s_m8", [P, NSEL + 1, 8])
        s_eq = sb("s_eq", [P, 2, NSEL + 1, 8])
        s_thr = sb("s_thr", [P, 2, NSEL + 1])
        s_bad = sb("s_bad", [P, 1])
        s_row = sb("s_row", [1, P + 1])
        s_flag = sb("s_flag", [1, 1], I32)
        hk = sb("hk", [P, 2, NT * NKV])

        arena = (nc.sbuf_base + 31) // 32 * 32
        room = nc.sbuf_usable_end - arena

        def at(name, off, shape, dt=F32):
            return nc.alloc_sbuf_tensor_at(name, shape, dt, offset=arena + off)

        def at_w(name, off, shape, dt=F32):
            return nc.alloc_sbuf_tensor_at(name, shape, dt, offset=w_base + off)

        xin = at("xin", 0, [P, 3, D])
        xn = at("xn", 12288, [P, 2, D])
        sq = at("sq", 20480, [P, D])
        gbc = at("gbc", 24576, [P, D])
        qi_tok = at("qi_tok", 0, [P, NSEL + 1, D])
        kiw_t = at("kiw_t", 20480, [KIW, ROWS])
        qs_t = [at("qs_t0", 28672, [P, NI, P], F32R), at_w("qs_t1", SLOTS * D * 4, [P, NI, P], F32R)]
        ki_hh = at("ki_hh", 36864, [P, S], F32R)
        ki_lo = at_w("ki_lo", 0, [ID, S], F32R)
        qs_tok = at_w("qs_tok", 4096, [P, NI, 2 * ID], F32R)
        acc = at("acc", 40960, [P, acc_at(S // P)])
        sacc = at("sacc", 57856, [SR, SKEYS])
        w_all = at("w_all", 57856, [P, NS, SR])
        rl = at("rl", 61984, [P, 2, SKEYS])
        rl3 = [rl[:, 0, :], rl[:, 1, :], at_w("rl_2", SLOTS * D * 4 + NI * P * 4, [P, S])]
        kiw = at("kiw", 71200, [P, NT, KIW])
        kis_t = [at(f"kis_t{i}", 4128 * i, [ID, SKEYS]) for i in range(AHEAD)]
        qis_t = at("qis_t", 4128 * AHEAD, [ID, NS, NI, TS])
        mneg = at("mneg", 0, [P, mask_at(S // P)], BF16)
        smneg = at("smneg", 9216, [SR, SKEYS], BF16)
        v_tok = at("v_tok", 11296, [P, NT, NKV * HD])
        k_t = at("k_t", 20512, [P, 2, ROWS])
        qst = at("qst", 29760, [P, 3, NH * HD])
        hsq = at("hsq", 35904, [P, NH * HD])
        hsq_k = at("hsq_k", 20512, [P, NT, NKV * HD])
        rt_k = at("rt_k", 20512, [P, 2, NT * NKV * 16])
        left = at("left", 20512, [P, 2, SKEYS])
        k_tok = at("k_tok", 61984, [P, NT, NKV * HD])
        PU = W - 1
        UC = PU + S + NS * (PU + TS)
        u = at("u", 29216, [P, CT, UC])
        y = at("y", 50944, [P, CT, ROWS])
        sig = at("sig", 20512, [P, 2, 384])
        u_last = at("u_last", 23584, [P, CT, PU + SR])
        cst = at("cst", 69856, [SR, 2, C])
        q_ld = at_w("q_ld", 4096, [P, 2, NH * HD])
        q_t = at_w("q_t", 8192, [P, 2, 4, P])
        sm = at_w("sm", 12288, [P, 4, S])
        pt = at_w("pt", 28672, [P, 2, S])
        o_tok = at_w("o_tok", 36864, [P, NH * HD])
        ysq = at_w("ysq", 38912, [P, CT, 384])
        lnd = at_w("lnd", 45056, [P, 3, P])
        kt_b = [at("kt_b0", 29216, [P, 2, SKEYS]), at("kt_b1", 50944, [P, 2, SKEYS])]
        v_b = [at("v_b0", 37472, [P, NPG, NKV * HD]), at("v_b1", 59200, [P, NPG, NKV * HD])]
        p_s = at("p_s", 45664, [P, SKEYS])
        pt_s = at("pt_s", 67392, [P, NPG + 1, P])
        o_s = at("o_s", 72000, [P, NKV * HD])
        v_new = at("v_new", 0, [TS, NS, NKV * HD])
        q_blk = at("q_blk", 11296, [P, NS, 2, SR])
        o_st = at("o_st", 15392, [P, 2, 4, P])
        mix_s = at("mix_s", 19488, [P, CT, SR])
        x1 = at("x1", 0, [P, NT, D])
        xn1 = at("xn1", 36864, [P, NX1, D])
        sq1 = at("sq1", 65536, [P, D])
        gbc1 = at("gbc1", 69632, [P, D])
        f_hi = at("f_hi", 36864, [P, 2, ROWS], F32R)
        f_lo = at("f_lo", 45568, [P, 2, ROWS], F32R)
        sg = at("sg", 54272, [P, 2, 384])
        ff = at("ff", 57344, [P, 2, 384])
        assert 71200 + NT * KIW * 4 <= room, room

        q_scr = nc.dram_tensor("q_scratch", [NT, P, NH * HD], F32, kind="Internal").ap()

        ps = ctx.enter_context(nc.psum_tensor("ps", [P, 8, 512], F32))

        def wide(b, n, r=slice(0, P)):
            return ps[r, b:b + -(-n // 512), :].rearrange("p a b -> p (a b)")[:, 0:n]

        consts_in = sem("consts_in")
        consts_made = sem("consts_made")
        x_in = [sem(f"x_in{i}") for i in range(3)]
        g_in = sem("g_in")
        x1_in = sem("x1_in")
        ms_ready = sem("ms_ready")
        rs_ready = sem("rs_ready")
        xn_ready = sem("xn_ready")
        xt_done = sem("xt_done")
        hi_ready = sem("hi_ready")
        lo_ready = sem("lo_ready")
        raw_in = [sem(f"raw_in{i}") for i in range(RAW)]
        split_hi = sem("split_hi")
        split_lo = sem("split_lo")
        w_used = sem("w_used")
        proj_done = sem("proj_done")
        proj_evac = sem("proj_evac")
        dve_step = sem("dve_step")
        act_step = sem("act_step")
        pool_step = sem("pool_step")
        kiw_mm = sem("kiw_mm")
        kiw_left = sem("kiw_left")
        kiw_ps = sem("kiw_ps")
        kiw_evac = sem("kiw_evac")
        kiw_ready = sem("kiw_ready")
        qi_ready = sem("qi_ready")
        kit_ps = sem("kit_ps")
        kit_ready = sem("kit_ready")
        wx_done = sem("wx_done")
        wall_ready = sem("wall_ready")
        ki_lo_ready = sem("ki_lo_ready")
        qs_hi = sem("qs_hi")
        qs_lo = sem("qs_lo")
        qit_ps = sem("qit_ps")
        qit_ready = sem("qit_ready")
        idx_mm = sem("idx_mm")
        relu_done = sem("relu_done")
        acc_done = sem("acc_done")
        kis_in = [sem(f"kis_in{i}") for i in range(AHEAD)]
        kin_done = sem("kin_done")
        qist_ps = sem("qist_ps")
        qist_ready = sem("qist_ready")
        sidx_mm = sem("sidx_mm")
        srelu_done = sem("srelu_done")
        sw_mm = sem("sw_mm")
        head_ms = sem("head_ms")
        head_rs = sem("head_rs")
        head_sq = sem("head_sq")
        k_ready = sem("k_ready")
        q_ready = sem("q_ready")
        q_out = [sem(f"q_out{i}") for i in range(3)]
        kt_ps = sem("kt_ps")
        kt_ready = sem("kt_ready")
        masks_ready = sem("masks_ready")
        u_mm = sem("u_mm")
        glu_sig = sem("glu_sig")
        glu_mul = sem("glu_mul")
        u_state = sem("u_state")
        sel_mid = sem("sel_mid")
        sel_cnt = sem("sel_cnt")
        bad_ready = sem("bad_ready")
        flag_in = sem("flag_in")
        round_done = sem("round_done")
        ut_ps = sem("ut_ps")
        ulast_ready = sem("ulast_ready")
        cst_ready = sem("cst_ready")
        cst_out = sem("cst_out")
        tap_done = sem("tap_done")
        mean_mm = sem("mean_mm")
        yc_ready = sem("yc_ready")
        ysq_ready = sem("ysq_ready")
        var_mm = sem("var_mm")
        lnv_ready = sem("lnv_ready")
        lnr_ready = sem("lnr_ready")
        lnd_ready = sem("lnd_ready")
        lnb_mm = sem("lnb_mm")
        yn_ready = sem("yn_ready")
        mixc_hi = sem("mixc_hi")
        mixc_lo = sem("mixc_lo")
        q_in = [sem(f"q_in{i}") for i in range(2)]
        qt_ps = sem("qt_ps")
        qt_ready = sem("qt_ready")
        qk_done = sem("qk_done")
        sm_done = sem("sm_done")
        nmax = sem("nmax")
        exp_done = sem("exp_done")
        pt_ps = sem("pt_ps")
        pt_act = sem("pt_act")
        pt_dve = sem("pt_dve")
        pv_done = sem("pv_done")
        o_ready = sem("o_ready")
        ot_ps = sem("ot_ps")
        mixa_hi = sem("mixa_hi")
        mixa_lo = sem("mixa_lo")
        sk_in = [sem(f"sk_in{i}") for i in range(2)]
        sv_in = [sem(f"sv_in{i}") for i in range(2)]
        vn_in = sem("vn_in")
        qblk_ready = sem("qblk_ready")
        ktn_ready = sem("ktn_ready")
        sqk_done = sem("sqk_done")
        smax = sem("smax")
        sexp_done = sem("sexp_done")
        spt_ps = sem("spt_ps")
        spt_ready = sem("spt_ready")
        spv_done = sem("spv_done")
        so_ready = sem("so_ready")
        sot_ps = sem("sot_ps")
        sot_ready = sem("sot_ready")
        mixs_ready = sem("mixs_ready")
        mixs_hi = sem("mixs_hi")
        mixs_lo = sem("mixs_lo")
        x1_ready = sem("x1_ready")
        gate_mm = sem("gate_mm")
        up_mm = sem("up_mm")
        silu_f = sem("silu_f")
        f_ready = sem("f_ready")
        f_hi_ready = sem("f_hi_ready")
        f_lo_ready = sem("f_lo_ready")
        down_mm = sem("down_mm")
        y_added = sem("y_added")
        stores = sem("stores")
        fence_pool = sem("fence_pool")
        fence_dve = sem("fence_dve")

        ident = kf[:, K_ID:K_ID + P]
        nsteps = NSEL * NI
        ck = A["cache_kt"]

        def select_tile(k):
            if k == NSEL:
                return sacc[:, :], smneg[:, :], SR
            t = FIRST + k
            keys = (t + 1) * P
            return acc[:, acc_at(t):acc_at(t) + keys], mneg[:, mask_at(t):mask_at(t) + keys], P

        def page_numbers(queue, b):
            return [queue.value_load(pages[0:1, b * NPG + j:b * NPG + j + 1], min_val=0, max_val=ck.shape[0] - 1)
                    for j in range(NPG)]

        def load_values(queue, b, page):
            if b >= 2:
                queue.wait_ge(spv_done, b - 1)
            for j in range(NPG):
                queue.dma_start(v_b[b % 2][:, j, :],
                                A["cache_v"][bass.ds(page[j], 1)].rearrange("o s c -> s (o c)")
                                ).then_inc(sv_in[b % 2], 16)

        block = ctx.enter_context(nc.Block())

        @block.sync
        def _(sp):
            def unit_source(n):
                if n < N_QI:
                    return A["w_in"][:, KI_AT:KI_AT + KIW].rearrange("(k p) n -> p k n", p=P)
                if n < N_U:
                    c, pair = divmod(n - N_QI, 4)
                    col = [QI_AT, QI_AT + 512, KV_AT, Q_AT][c]
                    return A["w_in"][pair * 256:pair * 256 + 256, col:col + 512].rearrange("(k p) n -> p k n", p=P)
                if n < N_OUT:
                    ct, g = divmod(n - N_U, 2)
                    col = (U_GATE if g else U_VAL) + ct * P
                    return A["w_in"][:, col:col + P].rearrange("(k p) n -> p k n", p=P)
                c, pair = divmod(n - N_OUT, 4)
                return A["w_out"][pair * 256:pair * 256 + 256, c * 512:c * 512 + 512].rearrange(
                    "(k p) n -> p k n", p=P)

            def load_unit(n):
                if n >= RAW:
                    sp.wait_ge(split_lo, n - RAW + 1)
                dst = w_raw[:, n % RAW, :]
                if n < N_QI:
                    dst = dst[:, 0:KT * KIW].rearrange("p (k n) -> p k n", k=KT)
                elif N_U <= n < N_OUT:
                    dst = dst.rearrange("p (k n) -> p k n", k=KT)
                else:
                    dst = dst.rearrange("p (k n) -> p k n", k=2)
                sp.dma_start(dst, unit_source(n)).then_inc(raw_in[n % RAW], 16)

            def load_x(o):
                t = ALL[o]
                if o >= 3:
                    sp.wait_ge(xn_ready, o - 2)
                src = A["x_sample"] if t == SAMPLE else A["x_prompt"][cols_of(t), :]
                sp.dma_start(xin[0:rows_of(t), o % 3, :], src).then_inc(x_in[o % 3], 16)

            load_x(0)
            sp.dma_start(gbc[:, :], A["attn_norm_g"].broadcast_to([P, D])).then_inc(g_in, 16)
            load_x(1)
            load_x(2)
            sp.dma_start(kf[:, :], A["kf"]).then_inc(consts_in, 16)
            sp.dma_start(pages[:, :], A["page_table"]).then_inc(consts_in, 16)
            sp.dma_start(kb[:, :], A["kb"]).then_inc(consts_in, 16)
            load_unit(0)
            load_unit(1)
            for o in range(3, NT):
                load_x(o)
            sp.dma_start(O["conv_sample"][:, 0:PU - TS, :], A["state"][:, TS:PU, :]).then_inc(cst_out, 16)
            for n in range(2, 14):
                load_unit(n)
            sp.wait_ge(consts_in, 48)
            for b in range(NS):
                page = page_numbers(sp, b)
                if b < AHEAD:
                    sp.wait_ge(qs_lo, b + 2)
                else:
                    sp.wait_ge(sidx_mm, b - AHEAD + 1)
                for j in range(NPG):
                    sp.dma_start(kis_t[b % AHEAD][:, j * PAGE:(j + 1) * PAGE],
                                 A["cache_it"][bass.ds(page[j], 1)].rearrange("o d s -> d (o s)")
                                 ).then_inc(kis_in[b % AHEAD], 16)
            for n in range(14, 21):
                load_unit(n)
            sp.wait_ge(masks_ready, 2 + FIRST)
            for r in range(3):
                sp.wait_ge(q_out[r], 48)
            for ct in range(CT):
                dst = u[:, ct, PU + S:].rearrange("p (b w) -> p b w", b=NS)[:, :, 0:PU]
                sp.dma_start(dst, A["state_t"][ct * P:(ct + 1) * P]).then_inc(u_state, 16)
            for n in range(21, 27):
                load_unit(n)
            sp.wait_ge(u_mm, 3 * 4)
            for i in range(NT):
                if i >= 2:
                    sp.wait_ge(qt_ps, i - 1)
                r = rows_of(i)
                sp.dma_start(q_ld[0:r, i % 2, :], q_scr[i, 0:r, :]).then_inc(q_in[i % 2], 16)

            def load_keys(b, page):
                if b >= 2:
                    sp.wait_ge(sqk_done, b // 2)
                for j in range(NPG):
                    sp.dma_start(kt_b[b % 2][:, :, j * PAGE:(j + 1) * PAGE],
                                 ck[bass.ds(page[j], 1)].rearrange("o (a p) s -> p (o a) s", a=2)
                                 ).then_inc(sk_in[b % 2], 16)

            page = page_numbers(sp, 0)
            sp.wait_ge(tap_done, 2 * CT * W)
            load_keys(0, page)
            load_values(sp, 0, page)
            page, page_2, page_3 = page_numbers(sp, 1), page_numbers(sp, 2), page_numbers(sp, 3)
            sp.wait_ge(mixc_lo, len(BLOCKS))
            sp.wait_ge(cst_out, 16 * 3)
            load_keys(1, page)
            load_values(sp, 1, page)
            sp.wait_ge(mixa_lo, S // P)
            sp.wait_ge(mixa_hi, S // P)
            sp.dma_start(v_new[:, :, :], O["v_sample"].rearrange("b t c -> t b c")).then_inc(vn_in, 16)
            for b in range(2, NS, 2):
                page, page_1 = (page_2, page_3) if b == 2 else (page_numbers(sp, b), page_numbers(sp, b + 1))
                load_keys(b, page)
                load_keys(b + 1, page_1)
                load_unit(25 + b)
                load_unit(26 + b)
                load_values(sp, b, page)
            sp.wait_ge(mixs_lo, 1)
            sp.wait_ge(mixs_hi, 1)
            sp.dma_start(x1[:, 0:SAMPLE, :], A["x_prompt"].rearrange("(t p) d -> p t d", p=P)).then_inc(x1_in, 16)
            sp.dma_start(x1[0:SR, SAMPLE, :], A["x_sample"]).then_inc(x1_in, 16)
            sp.dma_start(gbc1[:, :], A["ffn_norm_g"].broadcast_to([P, D])).then_inc(g_in, 16)
            gv = A["w_gate"].rearrange("(k p) f -> p k f", p=P)
            uv = A["w_up"].rearrange("(k p) f -> p k f", p=P)
            with sp.Fori(0, FG) as g:
                for j in range(6):
                    sp.wait_ge(split_lo, g * 6 + (N_FFN + j - RAW + 1))
                    slot = (N_FFN + j) % RAW
                    c = 2 * g + (j // 2 if j < 4 else j - 4)
                    if j < 4:
                        sp.dma_start(w_raw[:, slot, :].rearrange("p (k n) -> p k n", k=KT),
                                     (gv, uv)[j % 2][:, :, bass.ds(c * P, P)]).then_inc(raw_in[slot], 16)
                    else:
                        sp.dma_start(w_raw[:, slot, :], A["w_down"][bass.ds(c * P, P), :]).then_inc(raw_in[slot], 16)
            for t in range(NT):
                sp.wait_ge(y_added, 1 + 2 * NT * (FG - 1) + 2 * t + 2)
                dst = O["y_sample"] if t == SAMPLE else O["y_prompt"][cols_of(t), :]
                sp.dma_start(dst, x1[0:rows_of(t), t, :]).then_inc(stores, 16)
            sp.wait_ge(stores, 16 * (6 + NT))

        @block.gpsimd
        def _(pool):
            pool.memset(half_neg[:, :], -0.5).then_inc(pool_step, 1)
            pool.memset(w_all[:, :, :], 0.0).then_inc(consts_made, 1)
            pool.memset(ones[:, :], 1.0 / C).then_inc(consts_made, 1)

            def width(n):
                return KT * KIW if n == 0 else D

            def used(n):
                if n == 0:
                    return kiw_mm, len(BLOCKS)
                if N_U <= n < N_OUT:
                    return u_mm, 3 * (n - N_U + 1)
                c, i = divmod(n - N_QI, 4) if n < N_U else divmod(n - N_OUT, 4)
                late = 0 if n < N_U else 4
                return (w_used, 3 * (c + late) + i + 1) if i < 3 else (proj_done, BASE[c + late + 2])

            def split(n):
                w = width(n)
                pool.wait_ge(raw_in[n % RAW], 16 * (n // RAW + 1))
                if n >= SLOTS:
                    pool.wait_ge(*used(n - SLOTS))
                pool.tensor_copy(w_hi[:, n % SLOTS, 0:w], w_raw[:, n % RAW, 0:w]).then_inc(split_hi, 1)
                pool.wait_ge(split_hi, n + 1)
                pool.tensor_tensor(w_lo[:, n % SLOTS, 0:w], w_raw[:, n % RAW, 0:w],
                                   w_hi[:, n % SLOTS, 0:w].bitcast(F32), ALU.subtract).then_inc(split_lo, 1)

            def row_rs(q, r, width_):
                pool.wait_ge(ms_ready, q + 1)
                pool.tensor_scalar(rs[0:r, q:q + 1], ms[0:r, q:q + 1], 1.0 / width_, RMS_EPS,
                                   ALU.mult, ALU.add).then_inc(pool_step, 1)
                pool.wait_ge(pool_step, q + 2)
                pool.tensor_tensor(rs[0:r, q:q + 1], rs[0:r, q:q + 1], half_neg[0:r, 0:1],
                                   ALU.pow).then_inc(rs_ready, 1)

            def key_inverses():
                pool.wait_ge(head_ms, 1)
                m = SAMPLE * NKV
                pool.tensor_tensor(hk[:, 1, 0:m], hk[:, 0, 0:m], half_neg[:, 0:m], ALU.pow)
                pool.tensor_tensor(hk[0:SR, 1, m:], hk[0:SR, 0, m:], half_neg[0:SR, 0:NKV], ALU.pow).then_inc(head_rs, 1)

            def query_inverses(o):
                r = rows_of(ALL[o])
                pool.wait_ge(head_ms, o + 2)
                pool.tensor_tensor(hs[0:r, 2 + o % 2, :], hs[0:r, o % 2, :], half_neg[0:r, 0:NH], ALU.pow
                                   ).then_inc(head_rs, 1)

            for o in range(NT):
                row_rs(o, rows_of(ALL[o]), D)
                if o in (2, 5):
                    split(o // 3)
            for n in range(2, 12):
                split(n)
            for i in range(NSEL):
                pool.wait_ge(qs_hi, i + 1)
                pool.tensor_tensor(qs_tok[:, :, ID:], qi_tok[:, i, :].rearrange("p (h d) -> p h d", d=ID),
                                   qs_tok[:, :, 0:ID].bitcast(F32), ALU.subtract).then_inc(qs_lo, 1)
            pool.wait_ge(idx_mm, nsteps)
            for n in range(12, 17):
                split(n)
            key_inverses()
            split(17)
            split(18)
            for o in range(NT):
                query_inverses(o)
                if o in (4, 6):
                    split(19 + (o - 4) // 2)
            for n in range(21, 25):
                split(n)
            for k in range(len(BLOCKS)):
                pool.wait_ge(lnv_ready, k + 1)
                pool.tensor_tensor(lnr[:, 3 * k:3 * k + 3], lnr[:, 3 * k:3 * k + 3], half_neg[:, 0:3],
                                   ALU.pow).then_inc(lnr_ready, 1)
            pool.wait_ge(mixc_lo, len(BLOCKS))
            pool.wait_ge(mixa_lo, S // P)
            pool.wait_ge(qblk_ready, 1)
            for n in range(25, 33):
                split(n)
            for o in range(NT):
                row_rs(NT + o, rows_of(ALL[o]), D)
                if o == 4:
                    split(N_FFN)
                    split(N_FFN + 1)
            for j in range(2, 6):
                split(N_FFN + j)
            with pool.Fori(0, FG - 1) as g:
                for j in range(6):
                    n = N_FFN + 6 + j
                    slot, raw = n % SLOTS, n % RAW
                    pool.wait_ge(raw_in[raw], g * 48 + 16 * (n // RAW + 1))
                    if j < 4:
                        pool.wait_ge((gate_mm, up_mm)[j % 2], g * 6 + 3 * (j // 2 + 1))
                    elif j == 4:
                        pool.wait_ge(w_used, g + (3 * 6 + 1))
                    else:
                        pool.wait_ge(down_mm, g * (2 * NT) + (2 * NT + 1))
                    pool.sem_inc(fence_pool, 1)
                    pool.tensor_copy(w_hi[:, slot, :], w_raw[:, raw, :]).then_inc(split_hi, 1)
                    pool.wait_ge(split_hi, g * 6 + (n + 1))
                    pool.tensor_tensor(w_lo[:, slot, :], w_raw[:, raw, :], w_hi[:, slot, :].bitcast(F32),
                                       ALU.subtract).then_inc(split_lo, 1)

        @block.tensor
        def _(pe):
            def unit(n, k, width_):
                s = slice(k * width_, (k + 1) * width_)
                return w_hi[:, n % SLOTS, s], w_lo[:, n % SLOTS, s]

            def three(out, a_hi, a_lo, b_hi, b_lo, first, last):
                pe.matmul(out, a_hi, b_hi, start=first, stop=False)
                pe.matmul(out, a_hi, b_lo, start=False, stop=False)
                return pe.matmul(out, a_lo, b_hi, start=False, stop=last)

            def transpose_rows(q, src, r):
                pe.wait_ge(xn_ready, q + 1)
                if q % NT >= 4:
                    pe.wait_ge(hi_ready, q - 3)
                    pe.wait_ge(lo_ready, q - 3)
                for k in range(KT):
                    b = 2 * (q % NT % 4) + k // 4
                    mm = pe.transpose(ps[:, b, (k % 4) * P:(k % 4) * P + r], src[:, k * P:(k + 1) * P],
                                      ident[0:r, 0:r])
                mm.then_inc(xt_done, 1)

            def last_in_bank(c, t):
                first = 5 if c >= 5 else 0
                if t == 4:
                    return BASE[c] - BASE[first] + 1
                b = 4 if t == SAMPLE else t
                if c == first or b not in CHUNKS[c - 1]:
                    return None
                return BASE[c - 1] - BASE[first] + CHUNKS[c - 1].index(b) + 1

            def project(c, n0, width_, evac):
                tiles = CHUNKS[c]
                groups = [tiles[0:1], [t for t in tiles[1:] if t < 4], [t for t in tiles[1:] if t >= 4]]
                per = KT // 4
                for gi, group in enumerate(groups):
                    for t in group:
                        before = last_in_bank(c, t)
                        if before is not None:
                            pe.wait_ge(evac, before)
                    for k in range(KT):
                        n = n0 + k // per
                        if gi == 0 and k % per == 0:
                            pe.wait_ge(split_lo, n + 1)
                        w = unit(n, k % per, width_)
                        for t in group:
                            r = rows_of(t)
                            out = ps[0:r, 4 if t == SAMPLE else t, 0:width_]
                            mm = three(out, hi_t[:, k, cols_of(t)], lo_t[:, k, cols_of(t)], *w, k == 0, k == KT - 1)
                            if k == KT - 1:
                                mm.then_inc(proj_done, 1)
                        if gi == 2 and k % per == per - 1 and k < KT - 1:
                            mm.then_inc(w_used, 1)

            pe.wait_ge(consts_in, 48)
            for o in range(NT):
                transpose_rows(o, xn[0:rows_of(ALL[o]), o % 2, :], rows_of(ALL[o]))
            pe.wait_ge(hi_ready, NT)
            pe.wait_ge(lo_ready, NT)
            pe.wait_ge(split_lo, 1)
            for j, (a, z) in enumerate(BLOCKS):
                for k in range(KT):
                    mm = three(ps[0:KIW, j, 0:z - a], *unit(N_KIW, k, KIW), hi_t[:, k, a:z], lo_t[:, k, a:z],
                               k == 0, k == KT - 1)
                mm.then_inc(kiw_mm, 1)
            pe.wait_ge(kiw_left, len(BLOCKS))
            for t in range(NT):
                r = rows_of(t)
                mm = pe.transpose(ps[0:r, t // 6, t % 6 * KIW:t % 6 * KIW + KIW], kiw_t[:, cols_of(t)],
                                  ident[0:KIW, 0:KIW])
            mm.then_inc(kiw_ps, 1)
            project(1, N_QI, 512, proj_evac)
            project(2, N_QI + 4, 512, proj_evac)
            pe.wait_ge(proj_evac, BASE[3])
            pe.wait_ge(kiw_ready, 1)
            for t in range(S // P):
                pe.transpose(ps[0:ID, 6 + t // 4, (t % 4) * P:(t % 4 + 1) * P], kiw[:, t, 0:ID], ident)
            pe.transpose(ps[0:ID, 5, 0:SR], kiw[0:SR, SAMPLE, 0:ID], ident[0:SR, 0:SR])
            pe.transpose(ps[0:NI, 5, SR:2 * SR], wi_tok[0:SR, SAMPLE, :], ident[0:SR, 0:SR]).then_inc(kit_ps, 1)
            pe.wait_ge(kit_ready, 6)
            pe.matmul(ps[:, 5, 0:SR], kf[0:NI, K_E:K_E + P], wts[:, :], start=True, stop=True).then_inc(wx_done, 1)
            pe.wait_ge(wall_ready, 1)
            pe.wait_ge(ki_lo_ready, 1)

            def index_transposes(i, part):
                pe.wait_ge(qs_lo, i + 1)
                if i + part > 0:
                    pe.wait_ge(qit_ready, 2 * i + part)
                for j in range(8):
                    mm = pe.matmul(ps[:, 6 + j // 4, (j % 4) * P:(j % 4 + 1) * P],
                                   qs_tok[:, 8 * part + j, :], ident_r[:, :], start=True, stop=True)
                mm.then_inc(qit_ps, 1)

            index_transposes(0, 0)
            index_transposes(0, 1)
            for i in range(NSEL):
                keys = (FIRST + i + 1) * P
                pe.wait_ge(qit_ready, 2 * i + 2)
                for h in range(NI):
                    n = i * NI + h
                    if n >= 3:
                        pe.wait_ge(relu_done, n - 2)
                    for a in range(0, keys, 512):
                        w = min(512, keys - a)
                        out = ps[:, 2 * (n % 3) + a // 512, 0:w]
                        pe.matmul(out, qs_t[i % 2][:, h, :], ki_hh[:, a:a + w], start=True, stop=False)
                        mm = pe.matmul(out, qs_t[i % 2][0:ID, h, :], ki_lo[:, a:a + w], start=False, stop=True)
                    mm.then_inc(idx_mm, 1)
                    if h in (5, 10) and i + 1 < NSEL:
                        index_transposes(i + 1, h // 10)
            pe.wait_ge(qit_ready, 2 * NSEL)
            for h in range(NI):
                mm = pe.transpose(ps[0:ID, 6 + h // 8, (h % 8) * SR:(h % 8 + 1) * SR],
                                  qi_tok[0:SR, NSEL, h * ID:(h + 1) * ID], ident[0:SR, 0:SR])
            mm.then_inc(qist_ps, 1)
            pe.wait_ge(qist_ready, 2)
            pe.wait_ge(relu_done, nsteps)
            KB = [(0, 512), (512, 1024), (1024, SKEYS)]

            def weigh(b):
                pe.wait_ge(srelu_done, b + 1)
                for j, (a, z) in enumerate(KB):
                    mm = pe.matmul(ps[0:SR, 3 + j, 0:z - a], w_all[:, b, :], rl[:, b % 2, a:z],
                                   start=(b == 0), stop=(b == NS - 1))
                mm.then_inc(sw_mm, 1)

            for b in range(NS):
                pe.wait_ge(kis_in[b % AHEAD], 16 * NPG * (b // AHEAD + 1))
                pe.wait_ge(kin_done, b + 1)
                if b > 0:
                    pe.wait_ge(srelu_done, b)
                for j, (a, z) in enumerate(KB):
                    mm = pe.matmul(ps[:, j, 0:z - a], qis_t[:, b, :, :].rearrange("p h t -> p (h t)"),
                                   kis_t[b % AHEAD][:, a:z], start=True, stop=True)
                mm.then_inc(sidx_mm, 1)
                if b > 0:
                    weigh(b - 1)
            weigh(NS - 1)
            pe.wait_ge(masks_ready, 1)
            project(3, N_KV, 512, proj_evac)
            project(4, N_Q, 512, proj_evac)
            for ct in range(CT):
                for g in range(2):
                    n = N_U + 2 * ct + g
                    pe.wait_ge(split_lo, n + 1)
                    for j, (a, z) in enumerate(BLOCKS):
                        s = (2 * ct + g) * 3 + j
                        if s < 8:
                            pe.wait_ge(proj_evac, BASE[4] + s + 2)
                        if s >= 8:
                            before = s - 8
                            c2, g2, j2 = before // 6, before // 3 % 2, before % 3
                            pe.wait_ge(glu_sig if g2 else glu_mul, 3 * c2 + j2 + 1)
                        for k in range(KT):
                            w = unit(n, k, P)
                            mm = three(ps[:, s % 8, 0:z - a], *w, hi_t[:, k, a:z], lo_t[:, k, a:z],
                                       k == 0, k == KT - 1)
                        mm.then_inc(u_mm, 1)
            pe.wait_ge(glu_mul, 3 * CT)
            pe.wait_ge(glu_sig, 3 * CT)
            pe.wait_ge(k_ready, 1)
            for t in range(S // P):
                for p in range(2):
                    pe.transpose(ps[:, 2 * p + t // 4, (t % 4) * P:(t % 4 + 1) * P],
                                 k_tok[:, t, p * P:(p + 1) * P], ident)
            for p in range(2):
                mm = pe.transpose(ps[:, 4, p * SR:(p + 1) * SR], k_tok[0:SR, SAMPLE, p * P:(p + 1) * P],
                                  ident[0:SR, 0:SR])
            mm.then_inc(kt_ps, 1)
            pe.wait_ge(ulast_ready, CT)
            for ct in range(CT):
                pe.transpose(ps[0:PU, 5, ct * P:(ct + 1) * P], u_last[:, ct, 0:PU], ident)
                mm = pe.transpose(ps[0:SR, 6, ct * P:(ct + 1) * P], u_last[:, ct, PU:], ident)
            mm.then_inc(ut_ps, 1)
            pe.wait_ge(cst_ready, 2)
            NA = NH * (S // P)

            def query_transposes(i):
                pe.wait_ge(q_in[i % 2], 16 * (i // 2 + 1))
                if i > 1:
                    pe.wait_ge(mixa_hi, i - 1)
                    pe.wait_ge(mixa_lo, i - 1)
                r = rows_of(i)
                for j in range(4):
                    mm = pe.transpose(ps[:, 7, j * P:j * P + r], q_ld[0:r, i % 2, j * P:(j + 1) * P], ident[0:r, 0:r])
                mm.then_inc(qt_ps, 1)

            def head(h):
                g = h // 2
                return g % 2, g // 2, (g // 2) * 2 + h % 2

            def scores(n):
                i, h = divmod(n, NH)
                if n == 0:
                    pe.wait_ge(kt_ready, 3)
                if h == 0:
                    pe.wait_ge(qt_ready, i + 1)
                if n >= 2:
                    pe.wait_ge(sm_done, n - 1)
                kh, pair, j = head(h)
                half = slice(kh * HD, (kh + 1) * HD)
                keys = (i + 1) * P
                for a in range(0, keys, 512):
                    w = min(512, keys - a)
                    mm = pe.matmul(ps[:, 2 * (n % 2) + a // 512, 0:w], q_t[half, i % 2, j, :],
                                   k_t[half, pair, a:a + w], start=True, stop=True)
                mm.then_inc(qk_done, 1)

            def turn(n):
                i = n // NH
                pe.wait_ge(exp_done, n + 1)
                if n > 0:
                    pe.wait_ge(pt_act, n)
                if dve_parts(n - 1) > 0:
                    pe.wait_ge(pt_dve, dve_parts(n - 1))
                for s in range(i + 1):
                    mm = pe.transpose(ps[:, 4 + s // 4, (s % 4) * P:(s % 4 + 1) * P],
                                      sm[:, n % 4, s * P:(s + 1) * P], ident)
                mm.then_inc(pt_ps, 1)

            def values(n):
                i, h = divmod(n, NH)
                pe.wait_ge(pt_act, n + 1)
                if dve_parts(n) > 0:
                    pe.wait_ge(pt_dve, dve_parts(n))
                if h == 0 and i > 0:
                    pe.wait_ge(o_ready, i)
                for s in range(i + 1):
                    mm = pe.matmul(ps[:, 6, h * HD:(h + 1) * HD], pt[:, n % 2, s * P:(s + 1) * P],
                                   v_tok[:, s, (h // 2) * HD:(h // 2 + 1) * HD], start=(s == 0), stop=(s == i))
                mm.then_inc(pv_done, 1)

            def output_transposes(i):
                pe.wait_ge(o_ready, i + 1)
                pe.wait_ge(qt_ready, min(i + 2, S // P + 1))
                if sum(v < NH * (i + 1) + 3 for v in LN_AT) // 3 > 0:
                    pe.wait_ge(yn_ready, sum(v < NH * (i + 1) + 3 for v in LN_AT) // 3)
                for j in range(4):
                    mm = pe.transpose(ps[:, 7, j * P:(j + 1) * P], o_tok[:, j * P:(j + 1) * P], ident)
                mm.then_inc(ot_ps, 1)

            def layer_norm_sum(v):
                k = v // 3
                a, z = BLOCKS[k]
                if v == 0:
                    pe.wait_ge(tap_done, 2 * CT * W)
                    pe.wait_ge(consts_made, 2)
                if v % 3 == 0:
                    pe.wait_ge(qt_ready, min(S // P + 1, (LN_AT[v] - 5) // NH + 2))
                    pe.wait_ge(mixa_hi, (LN_AT[v] - 3) // NH)
                    pe.wait_ge(mixa_lo, (LN_AT[v] - 3) // NH)
                    if k > 0:
                        pe.wait_ge(yn_ready, k)
                    for ct in range(CT):
                        mm = pe.matmul(ps[:, 7, 0:z - a], ones[:, :], y[:, ct, a:z], start=(ct == 0), stop=(ct == CT - 1))
                    mm.then_inc(mean_mm, 1)
                elif v % 3 == 1:
                    pe.wait_ge(ysq_ready, k + 1)
                    for t in range(3 * k, 3 * k + 3):
                        r = rows_of(t)
                        for ct in range(CT):
                            mm = pe.matmul(ps[0:r, 7, t:t + 1], ysq[:, ct, t * P - a:t * P - a + r], ones[:, 0:1],
                                           start=(ct == 0), stop=(ct == CT - 1))
                    mm.then_inc(var_mm, 1)
                else:
                    pe.wait_ge(lnd_ready, k + 1)
                    for t in range(3 * k, 3 * k + 3):
                        r = rows_of(t)
                        mm = pe.matmul(ps[:, 7, t * P - a:t * P - a + r], ones[0:r, :], lnd[0:r, t % 3, 0:r],
                                       start=True, stop=True)
                    mm.then_inc(lnb_mm, 1)

            query_transposes(0)
            for n in range(NA + 4):
                if n < NA:
                    scores(n)
                if n >= 2 and n - 2 < NA:
                    turn(n - 2)
                if n >= 3 and n - 3 < NA:
                    values(n - 3)
                if n % NH == 5 and n < NA:
                    query_transposes(n // NH + 1)
                if n % NH == 3 and NH < n < NA:
                    output_transposes(n // NH - 1)
                if n in LN_AT:
                    layer_norm_sum(LN_AT.index(n))
            output_transposes(S // P - 1)
            def sample_scores(pr):
                for par in range(2):
                    b = 2 * pr + par
                    pe.wait_ge(sk_in[par], 16 * NPG * (pr + 1))
                    pe.wait_ge(ktn_ready, b + 1)
                    if par == 0:
                        pe.wait_ge(qblk_ready, 1)
                        if pr > 0:
                            pe.wait_ge(sexp_done, pr)
                    rows = slice(par * SR, (par + 1) * SR)
                    for j, (a, z) in enumerate(KB):
                        out = ps[rows, j, 0:z - a]
                        pe.matmul(out, q_blk[:, b, 0, :], kt_b[par][:, 0, a:z], start=True, stop=False)
                        pe.matmul(out, q_blk[:, b, 1, :], kt_b[par][:, 1, a:z], start=False, stop=False)
                        mm = pe.matmul(out, kb[0:SR, P + b * SR:P + (b + 1) * SR], smneg[:, a:z],
                                       start=False, stop=True)
                mm.then_inc(sqk_done, 1)

            def turn_outputs(pr):
                pe.wait_ge(so_ready, pr + 1)
                if pr > 0:
                    pe.wait_ge(sot_ready, pr)
                else:
                    pe.wait_ge(mixa_hi, S // P)
                    pe.wait_ge(mixa_lo, S // P)
                for p in range(2):
                    mm = pe.transpose(ps[:, 7, p * P:(p + 1) * P], o_s[:, p * P:(p + 1) * P], ident)
                mm.then_inc(sot_ps, 1)

            sample_scores(0)
            for pr in range(NS // 2):
                pe.wait_ge(sexp_done, pr + 1)
                if pr > 0:
                    pe.wait_ge(spt_ready, 2 * pr)
                for s in range(NPG + 1):
                    w = P if s < NPG else TS
                    mm = pe.transpose(ps[0:w, 3 + s // 4, (s % 4) * P:(s % 4 + 1) * P],
                                      p_s[:, s * P:s * P + w], ident)
                mm.then_inc(spt_ps, 1)
                if pr > 0:
                    turn_outputs(pr - 1)
                pe.wait_ge(spt_ready, 2 * pr + 2)
                pe.wait_ge(vn_in, 16)
                for par in range(2):
                    b = 2 * pr + par
                    pe.wait_ge(sv_in[par], 16 * NPG * (pr + 1))
                    rows = slice(par * SR, (par + 1) * SR)
                    for s in range(NPG + 1):
                        k = P if s < NPG else TS
                        v = v_b[par][:, s, :] if s < NPG else v_new[:, b, :]
                        mm = pe.matmul(ps[rows, 6, 0:NKV * HD], pt_s[0:k, s, rows], v, start=(s == 0), stop=(s == NPG))
                    mm.then_inc(spv_done, 1)
                if pr + 1 < NS // 2:
                    sample_scores(pr + 1)
            turn_outputs(NS // 2 - 1)
            pe.wait_ge(sot_ready, NS // 2)
            pe.wait_ge(mixs_hi, 1)
            pe.wait_ge(mixs_lo, 1)
            project(5, N_OUT, 512, x1_ready)
            project(6, N_OUT + 4, 512, x1_ready)
            pe.wait_ge(x1_ready, 2 * NT)
            for o in range(NT):
                transpose_rows(NT + o, xn1[0:rows_of(ALL[o]), o % NX1, :], rows_of(ALL[o]))
            pe.wait_ge(hi_ready, 2 * NT)
            pe.wait_ge(lo_ready, 2 * NT)
            pe.sem_inc(down_mm, 1)
            with pe.Fori(0, FG) as g:
                for c in range(2):
                    for gu in range(2):
                        n = N_FFN + 2 * c + gu
                        pe.wait_ge(split_lo, g * 6 + (n + 1))
                        for j, (a, z) in enumerate(BLOCKS):
                            done = 3 * c + j
                            pe.wait_ge(f_ready if gu else silu_f, g * 6 + (1 + max(0, done - 2)))
                            for k in range(KT):
                                w = unit(n, k, P)
                                mm = three(ps[:, 3 * gu + j, 0:z - a], *w, hi_t[:, k, a:z], lo_t[:, k, a:z],
                                           k == 0, k == KT - 1)
                            mm.then_inc(up_mm if gu else gate_mm, 1)
                pe.wait_ge(split_lo, g * 6 + (N_FFN + 6))
                for t in range(NT):
                    if t % 3 == 0:
                        pe.wait_ge(f_hi_ready, g * 6 + (4 + t // 3))
                        pe.wait_ge(f_lo_ready, g * 6 + (4 + t // 3))
                    r = rows_of(t)
                    for nh in range(2):
                        pe.wait_ge(y_added, g * (2 * NT) + (1 + max(0, 2 * t + nh - 1)))
                        for c in range(2):
                            n = N_FFN + 4 + c
                            mm = three(ps[0:r, 6 + nh, :], f_hi[:, c, cols_of(t)], f_lo[:, c, cols_of(t)],
                                       *unit(n, nh, 512), c == 0, c == 1)
                            if t == SAMPLE and nh == 1 and c == 0:
                                mm.then_inc(w_used, 1)
                        mm.then_inc(down_mm, 1)

        @block.scalar
        def _(act):
            steps = [0]

            def link(ins):
                steps[0] += 1
                ins.then_inc(act_step, 1)
                act.wait_ge(act_step, steps[0])

            def square_rows(q, src, junk, r):
                if q > 0:
                    act.wait_ge(ms_ready, q)
                act.activation(junk[0:r, :], src, ACT.Square, accum_out=ms[0:r, q:q + 1]).then_inc(ms_ready, 1)

            def take_hi(q):
                t = ALL[q % NT]
                r = rows_of(t)
                act.wait_ge(xt_done, q + 1)
                for half in range(2):
                    b = 2 * (q % NT % 4) + half
                    ins = act.activation(hi_t[:, 4 * half:4 * half + 4, cols_of(t)],
                                         ps[:, b, :].rearrange("p (k c) -> p k c", k=4)[:, :, 0:r], ACT.Copy)
                ins.then_inc(hi_ready, 1)

            for o in range(NT + 1):
                if o < NT:
                    t = ALL[o]
                    act.wait_ge(x_in[o % 3], 16 * (o // 3 + 1))
                    square_rows(o, xin[0:rows_of(t), o % 3, :], sq, rows_of(t))
                if o > 0:
                    take_hi(o - 1)
            act.wait_ge(lo_ready, NT)
            for j, (a, z) in enumerate(BLOCKS):
                act.wait_ge(kiw_mm, j + 1)
                act.activation(kiw_t[:, a:z], ps[0:KIW, j, 0:z - a], ACT.Copy).then_inc(kiw_left, 1)
            act.wait_ge(kiw_ps, 1)
            act.activation(kiw[:, 0:6, :], ps[:, 0, 0:6 * KIW].rearrange("p (t n) -> p t n", t=6), ACT.Copy)
            act.activation(kiw[:, 6:SAMPLE, :], ps[:, 1, 0:2 * KIW].rearrange("p (t n) -> p t n", t=2), ACT.Copy)
            act.activation(kiw[0:SR, SAMPLE, :], ps[0:SR, 1, 2 * KIW:3 * KIW], ACT.Copy).then_inc(kiw_evac, 1)
            act.wait_ge(kiw_ready, 1)
            act.dma_start(O["ki_prompt"].rearrange("(t p) d -> p t d", p=P), kiw[:, 0:SAMPLE, 0:ID]).then_inc(stores, 16)
            act.dma_start(O["ki_sample"], kiw[0:SR, SAMPLE, 0:ID]).then_inc(stores, 16)
            for c in (1, 2):
                for o, t in enumerate(CHUNKS[c]):
                    r = rows_of(t)
                    act.wait_ge(proj_done, BASE[c] + o + 1)
                    act.activation(qi_tok[0:r, t - FIRST, (c - 1) * 512:c * 512],
                                   ps[0:r, 4 if t == SAMPLE else t, :], ACT.Copy).then_inc(proj_evac, 1)
            act.wait_ge(kit_ps, 1)
            for b in range(2):
                for half in range(2):
                    act.activation(ki_hh[half * ID:(half + 1) * ID, b * 512:(b + 1) * 512], ps[0:ID, 6 + b, :],
                                   ACT.Copy).then_inc(kit_ready, 1)
            act.activation(kin_t[:, :], ps[0:ID, 5, 0:SR], ACT.Copy).then_inc(kit_ready, 1)
            act.activation(wts[:, :], ps[0:NI, 5, SR:2 * SR], ACT.Copy).then_inc(kit_ready, 1)

            link(act.activation(ident_r[:, :], ident, ACT.Copy))

            def split_index_queries(i):
                act.wait_ge(qi_ready, 2 * (NSEL + 1))
                if i > 0:
                    act.wait_ge(qit_ps, 2 * i)
                act.activation(qs_tok[:, :, 0:ID], qi_tok[:, i, :].rearrange("p (h d) -> p h d", d=ID), ACT.Copy
                               ).then_inc(qs_hi, 1)

            def take_index_queries(i, part):
                act.wait_ge(qit_ps, 2 * i + part + 1)
                act.activation(qs_t[i % 2][:, 8 * part:8 * part + 8, :],
                               wide(6, 1024).rearrange("p (j c) -> p j c", j=8), ACT.Copy).then_inc(qit_ready, 1)

            split_index_queries(0)
            take_index_queries(0, 0)
            take_index_queries(0, 1)
            for i in range(NSEL):
                keys = (FIRST + i + 1) * P
                for h in range(NI):
                    n = i * NI + h
                    act.wait_ge(idx_mm, n + 1)
                    if n >= 3:
                        act.wait_ge(acc_done, 2 * (n - 2))
                    act.activation(rl3[n % 3][:, 0:keys], wide(2 * (n % 3), keys), ACT.Relu).then_inc(relu_done, 1)
                    if i + 1 < NSEL:
                        if h == 0:
                            split_index_queries(i + 1)
                        if h in (6, 11):
                            take_index_queries(i + 1, h // 11)
            act.wait_ge(qist_ps, 1)
            for b in range(2):
                for hh in range(2):
                    ins = act.activation(
                        qis_t[:, :, 8 * b + 4 * hh:8 * b + 4 * hh + 4, :].rearrange("p b h t -> p h b t"),
                        ps[0:ID, 6 + b, hh * 256:(hh + 1) * 256].rearrange("p (h b t) -> p h b t", h=4, b=NS), ACT.Copy)
                ins.then_inc(qist_ready, 1)
            act.wait_ge(acc_done, 2 * nsteps)
            for b in range(NS):
                if b >= AHEAD:
                    act.wait_ge(sidx_mm, b - AHEAD + 1)
                act.activation(kis_t[b % AHEAD][:, PAST:SKEYS], kin_t[:, b * TS:(b + 1) * TS], ACT.Copy).then_inc(kin_done, 1)
                act.wait_ge(sidx_mm, b + 1)
                if b >= 2:
                    act.wait_ge(sw_mm, b - 1)
                act.activation(rl[:, b % 2, :], wide(0, SKEYS), ACT.Relu).then_inc(srelu_done, 1)

            def take_keys_values(o):
                t = CHUNKS[3][o]
                r = rows_of(t)
                src = ps[0:r, 4 if t == SAMPLE else t, :]
                act.wait_ge(proj_done, BASE[3] + o + 1)
                act.activation(v_tok[0:r, t, :], src[:, 256:512], ACT.Copy)
                act.activation(k_tok[0:r, t, :], src[:, 0:256], ACT.Copy).then_inc(proj_evac, 1)

            act.wait_ge(masks_ready, 1)
            for i in range(HALVINGS):
                act.wait_ge(sel_mid, i + 1)
                for k in COUNT_ACT:
                    work, place, r = select_tile(k)
                    act.activation(place, work, ACT.Sign, bias=s_mid[0:r, k:k + 1], scale=-1.0,
                                   accum_out=s_cnt[0:r, k:k + 1]).then_inc(sel_cnt, 1)
                if i == 2:
                    take_keys_values(0)
                if i == 7:
                    for o in range(1, 5):
                        take_keys_values(o)
            for o in range(5, NT):
                take_keys_values(o)
            act.wait_ge(proj_evac, BASE[4])
            act.activation(hsq_k[:, 0:SAMPLE, :], k_tok[:, 0:SAMPLE, :], ACT.Square)
            act.activation(hsq_k[0:SR, SAMPLE, :], k_tok[0:SR, SAMPLE, :], ACT.Square).then_inc(head_sq, 1)

            for o in range(NT + 1):
                if o < NT:
                    t = ALL[o]
                    r = rows_of(t)
                    src = ps[0:r, 4 if t == SAMPLE else t, :]
                    act.wait_ge(proj_done, BASE[4] + o + 1)
                    if o >= 3:
                        act.wait_ge(q_out[o % 3], 16 * (o // 3))
                    qs = qst[0:r, o % 3, :]
                    for a in range(2):
                        ins = act.activation(
                            qs[:, a * 256:(a + 1) * 256].rearrange("p (r k d) -> p k r d", r=2, k=2),
                            src[:, a * 256:(a + 1) * 256].rearrange("p (k r d) -> p k r d", k=2, r=2), ACT.Copy)
                    link(ins)
                    if o > 0:
                        act.wait_ge(head_ms, o + 1)
                    act.activation(hsq[0:r, :], qs, ACT.Square).then_inc(proj_evac, 1)
                if o > 0:
                    r = rows_of(ALL[o - 1])
                    act.wait_ge(q_ready, o)
                    act.dma_start(q_scr[ALL[o - 1], 0:r, :], qst[0:r, (o - 1) % 3, :]).then_inc(q_out[(o - 1) % 3], 16)
                if o == 1:
                    act.wait_ge(k_ready, 1)
                    act.dma_start(O["k_prompt"].rearrange("(t p) d -> p t d", p=P), k_tok[:, 0:SAMPLE, :]).then_inc(stores, 16)
                    act.dma_start(O["k_sample"], k_tok[0:SR, SAMPLE, :]).then_inc(stores, 16)
                    act.dma_start(O["v_prompt"].rearrange("(t p) d -> p t d", p=P), v_tok[:, 0:SAMPLE, :]).then_inc(stores, 16)
                    act.dma_start(O["v_sample"].rearrange("b t c -> (b t) c"), v_tok[0:SR, SAMPLE, :]).then_inc(stores, 16)
            act.wait_ge(bad_ready, 1)
            act.dma_start(s_row[0:1, 0:P], s_bad[:, :]).then_inc(flag_in, 16)
            for ct in range(CT):
                for j, (a, z) in enumerate(BLOCKS):
                    n = 3 * ct + j
                    s = (2 * ct + 1) * 3 + j
                    act.wait_ge(u_mm, s + 1)
                    if n >= 2:
                        act.wait_ge(glu_mul, n - 1)
                    act.activation(sig[:, n % 2, 0:z - a], ps[:, s % 8, 0:z - a], ACT.Sigmoid).then_inc(glu_sig, 1)
            act.wait_ge(kt_ps, 1)
            act.wait_ge(ut_ps, 1)
            for p in range(2):
                act.activation(k_t[:, p, 0:S], wide(2 * p, S), ACT.Copy).then_inc(kt_ready, 1)
            act.activation(k_t[:, :, S:ROWS], ps[:, 4, 0:2 * SR].rearrange("p (a c) -> p a c", a=2), ACT.Copy
                           ).then_inc(kt_ready, 1)
            act.wait_ge(stores, 16 * 6)
            act.activation(cst[0:PU, 0, :], ps[0:PU, 5, :], ACT.Copy).then_inc(cst_ready, 1)
            act.activation(cst[:, 1, :], ps[0:SR, 6, :], ACT.Copy).then_inc(cst_ready, 1)
            act.wait_ge(cst_ready, 2)
            act.dma_start(O["conv_prompt"], cst[0:PU, 0, :]).then_inc(cst_out, 16)
            act.dma_start(O["conv_sample"][:, PU - TS:PU, :], cst[:, 1, :]).then_inc(cst_out, 16)
            NA = NH * (S // P)

            def take_queries(i):
                act.wait_ge(qt_ps, i + 1)
                r = rows_of(i)
                act.activation(q_t[:, i % 2, :, 0:r], ps[:, 7, :].rearrange("p (j c) -> p j c", j=4)[:, :, 0:r],
                               ACT.Copy).then_inc(qt_ready, 1)

            def exps(n):
                i = n // NH
                keys = (i + 1) * P
                act.wait_ge(nmax, n + 1)
                act.activation(sm[:, n % 4, 0:keys], sm[:, n % 4, 0:keys], ACT.Exp, bias=stat[:, 0, n % 16:n % 16 + 1],
                               scale=HD ** -0.5, accum_out=stat[:, 1, n % 16:n % 16 + 1]).then_inc(exp_done, 1)

            def take_weights(n):
                keys = (n // NH + 1) * P
                act.wait_ge(pt_ps, n + 1)
                if n >= 2:
                    act.wait_ge(pv_done, n - 1)
                act.activation(pt[:, n % 2, 0:min(keys, 512)], ps[:, 4, 0:min(keys, 512)], ACT.Copy
                               ).then_inc(pt_act, 1)

            def take_outputs(i):
                act.wait_ge(ot_ps, i + 1)
                act.activation(hi_t[:, CT:KT, cols_of(i)], ps[:, 7, :].rearrange("p (j c) -> p j c", j=4), ACT.Copy
                               ).then_inc(mixa_hi, 1)

            def layer_norm_step(v):
                k = v // 3
                a, z = BLOCKS[k]
                if v % 3 == 0:
                    act.wait_ge(yc_ready, k + 1)
                    if k > 0:
                        act.wait_ge(var_mm, k)
                    act.activation(ysq[:, :, 0:z - a], y[:, :, a:z], ACT.Square).then_inc(ysq_ready, 1)
                elif v % 3 == 2:
                    act.wait_ge(yn_ready, k + 1)
                    for ct in range(CT):
                        ins = act.activation(y[:, ct, a:z], y[:, ct, a:z], ACT.Silu,
                                             bias=kf[:, K_LB + ct:K_LB + ct + 1], scale=kf[:, K_LG + ct:K_LG + ct + 1])
                    link(ins)
                    act.activation(hi_t[:, 0:CT, a:z], y[:, :, a:z], ACT.Copy).then_inc(mixc_hi, 1)

            take_queries(0)
            for n in range(NA + 4):
                if n < NA:
                    if n % NH == 0 and n >= 2 * NH:
                        act.wait_ge(o_ready, n // NH - 1)
                    exps(n)
                if n >= 2 and n - 2 < NA:
                    take_weights(n - 2)
                if n % NH == 6 and n < NA:
                    take_queries(n // NH + 1)
                if n % NH == 4 and n > NH:
                    take_outputs(n // NH - 1)
                if n - 1 in LN_AT:
                    layer_norm_step(LN_AT.index(n - 1))
            take_outputs(S // P - 1)
            def take_sample_outputs(pr):
                act.wait_ge(sot_ps, pr + 1)
                act.activation(o_st[:, :, pr, :], ps[:, 7, 0:2 * P].rearrange("p (a c) -> p a c", a=2), ACT.Copy
                               ).then_inc(sot_ready, 1)

            def new_sample_keys(b):
                if b >= 2:
                    act.wait_ge(sqk_done, b // 2)
                act.activation(kt_b[b % 2][:, :, PAST:SKEYS], k_t[:, :, S + b * TS:S + (b + 1) * TS], ACT.Copy
                               ).then_inc(ktn_ready, 1)

            new_sample_keys(0)
            act.wait_ge(mixc_lo, len(BLOCKS))
            new_sample_keys(1)
            act.wait_ge(mixa_lo, S // P)
            act.wait_ge(cst_out, 16 * 3)
            for pr in range(NS // 2):
                act.wait_ge(smax, pr + 1)
                if pr > 0:
                    act.wait_ge(spt_ps, pr)
                    act.wait_ge(so_ready, pr)
                act.activation(p_s[:, :], wide(0, SKEYS), ACT.Exp, bias=stat[:, 0, 0:1], scale=HD ** -0.5,
                               accum_out=stat[:, 1, 0:1]).then_inc(sexp_done, 1)
                act.wait_ge(spt_ps, pr + 1)
                if pr > 0:
                    act.wait_ge(spv_done, 2 * pr)
                act.activation(pt_s[:, 0:NPG, :], wide(3, NPG * P).rearrange("p (s c) -> p s c", s=NPG), ACT.Copy
                               ).then_inc(spt_ready, 1)
                act.activation(pt_s[0:TS, NPG, :], ps[0:TS, 5, 0:P], ACT.Copy).then_inc(spt_ready, 1)
                if pr > 0:
                    take_sample_outputs(pr - 1)
                if pr + 1 < NS // 2:
                    b = 2 * pr + 2
                    new_sample_keys(b)
                    new_sample_keys(b + 1)
                    load_values(act, b + 1, page_numbers(act, b + 1))
            take_sample_outputs(NS // 2 - 1)
            act.wait_ge(mixs_ready, 1)
            act.activation(hi_t[:, CT:KT, cols_of(SAMPLE)], mix_s[:, :, :], ACT.Copy).then_inc(mixs_hi, 1)
            for o in range(NT + 1):
                if o < NT:
                    t = ALL[o]
                    act.wait_ge(x1_ready, NT + o + 1)
                    square_rows(NT + o, x1[0:rows_of(t), t, :], sq1, rows_of(t))
            for o in range(NT):
                take_hi(NT + o)
            act.wait_ge(lo_ready, 2 * NT)
            act.sem_inc(silu_f, 1)
            with act.Fori(0, FG) as g:
                for m in range(7):
                    if m < 6:
                        a, z = BLOCKS[m % 3]
                        act.wait_ge(gate_mm, g * 6 + (m + 1))
                        act.wait_ge(f_ready, g * 6 + (1 + max(0, m - 1)))
                        act.activation(sg[:, m % 2, 0:z - a], ps[:, m % 3, 0:z - a], ACT.Silu).then_inc(silu_f, 1)
                    if m > 0:
                        c, j = divmod(m - 1, 3)
                        a, z = BLOCKS[j]
                        if m == 1:
                            act.wait_ge(down_mm, g * (2 * NT) + 1)
                        act.wait_ge(f_ready, g * 6 + (1 + m))
                        act.activation(f_hi[:, c, a:z], ff[:, (m - 1) % 2, 0:z - a], ACT.Copy).then_inc(f_hi_ready, 1)

        @block.vector
        def _(dve):
            steps = [0]

            def link(ins):
                steps[0] += 1
                ins.then_inc(dve_step, 1)
                dve.wait_ge(dve_step, steps[0])

            def norm_rows(q, src, dst, g_tile, r, places):
                dve.wait_ge(rs_ready, q + 1)
                if q % NT >= places:
                    dve.wait_ge(xt_done, q - places + 1)
                dve.scalar_tensor_tensor(dst, src, rs[0:r, q:q + 1], g_tile[0:r, :], ALU.mult, ALU.mult
                                         ).then_inc(xn_ready, 1)

            def take_lo(q):
                t = ALL[q % NT]
                r = rows_of(t)
                dve.wait_ge(hi_ready, q + 1)
                for half in range(2):
                    b = 2 * (q % NT % 4) + half
                    ks = slice(4 * half, 4 * half + 4)
                    ins = dve.tensor_tensor(lo_t[:, ks, cols_of(t)],
                                            ps[:, b, :].rearrange("p (k c) -> p k c", k=4)[:, :, 0:r],
                                            hi_t[:, ks, cols_of(t)].bitcast(F32), ALU.subtract)
                ins.then_inc(lo_ready, 1)

            def rope(x, cos, sin, t1, t2):
                dve.tensor_tensor(t1, x[:, :, 0:16], cos, ALU.mult)
                dve.tensor_tensor(t2[:, :, 0:8], x[:, :, 8:16], sin[:, :, 0:8], ALU.mult)
                link(dve.tensor_tensor(t2[:, :, 8:16], x[:, :, 0:8], sin[:, :, 8:16], ALU.mult))
                return dve.tensor_tensor(x[:, :, 0:16], t1, t2, ALU.add)

            def rope_tile(x, t, heads):
                r = rows_of(t)
                cos = kf[0:r, K_COS + 16 * t:K_COS + 16 * t + 16].unsqueeze(1).broadcast_to([r, heads, 16])
                sin = kf[0:r, K_SIN + 16 * t:K_SIN + 16 * t + 16].unsqueeze(1).broadcast_to([r, heads, 16])
                t1, t2 = (rt[0:r, i, 0:heads * 16].rearrange("p (h d) -> p h d", h=heads) for i in range(2))
                return rope(x, cos, sin, t1, t2)

            dve.memset(lnr[:, :], 1.0)
            link(dve.memset(rt[:, :, :], 0.0))
            dve.wait_ge(g_in, 16)
            for o in range(NT + 1):
                if o < NT:
                    r = rows_of(ALL[o])
                    norm_rows(o, xin[0:r, o % 3, :], xn[0:r, o % 2, :], gbc, r, 2)
                if o > 0:
                    take_lo(o - 1)
            dve.wait_ge(consts_in, 48)
            dve.wait_ge(kiw_evac, 1)
            for t0, t1, r in ((0, SAMPLE, P), (SAMPLE, NT, SR)):
                cos = kf[0:r, K_COS + 16 * t0:K_COS + 16 * t1].rearrange("p (t d) -> p t d", d=16)
                sin = kf[0:r, K_SIN + 16 * t0:K_SIN + 16 * t1].rearrange("p (t d) -> p t d", d=16)
                ta, tb = (rt[0:r, i, 0:(t1 - t0) * 16].rearrange("p (h d) -> p h d", d=16) for i in range(2))
                link(rope(kiw[0:r, t0:t1, 0:ID], cos, sin, ta, tb))
                ins = dve.tensor_scalar(wi_tok[0:r, t0:t1, :], kiw[0:r, t0:t1, ID:KIW], (NI * ID) ** -0.5, None, ALU.mult)
            ins.then_inc(kiw_ready, 1)
            for c in (1, 2):
                for o, t in enumerate(CHUNKS[c]):
                    r = rows_of(t)
                    dve.wait_ge(proj_evac, BASE[c] + o + 1)
                    if BASE[c] + o > 0:
                        dve.wait_ge(qi_ready, BASE[c] + o)
                    x = qi_tok[0:r, t - FIRST, (c - 1) * 512:c * 512].rearrange("p (h d) -> p h d", d=ID)
                    rope_tile(x, t, 8).then_inc(qi_ready, 1)
            dve.wait_ge(kit_ready, 4)
            dve.tensor_tensor(ki_lo[:, :], wide(6, S, slice(0, ID)), ki_hh[0:ID, :].bitcast(F32), ALU.subtract
                              ).then_inc(ki_lo_ready, 1)
            dve.wait_ge(wx_done, 1)
            dve.wait_ge(consts_made, 1)
            for b in range(NS):
                s = slice(b * TS, (b + 1) * TS)
                ins = dve.tensor_tensor(w_all[:, b, s], ps[:, 5, s], kf[:, K_M + b * TS:K_M + (b + 1) * TS], ALU.mult)
            ins.then_inc(wall_ready, 1)
            for i in range(NSEL):
                t = FIRST + i
                a0, keys = acc_at(t), (t + 1) * P
                for h in range(NI):
                    n = i * NI + h
                    dve.wait_ge(relu_done, n + 1)
                    w = wi_tok[:, t, h:h + 1]
                    src = rl3[n % 3]
                    m = keys // 2
                    if h == 0:
                        dve.tensor_scalar(acc[:, a0:a0 + m], src[:, 0:m], w, None, ALU.mult).then_inc(acc_done, 1)
                        dve.tensor_scalar(acc[:, a0 + m:a0 + t * P], src[:, m:t * P], w, None, ALU.mult)
                        dve.scalar_tensor_tensor(acc[:, a0 + t * P:a0 + keys], src[:, t * P:keys], w,
                                                 kf[:, K_TRI:K_TRI + P], ALU.mult, ALU.add).then_inc(acc_done, 1)
                    else:
                        for j, (a, z) in enumerate(((0, m), (m, keys))):
                            dve.wait_ge(acc_done, 2 * n - 1 + j)
                            dve.scalar_tensor_tensor(acc[:, a0 + a:a0 + z], src[:, a:z], w, acc[:, a0 + a:a0 + z],
                                                     ALU.mult, ALU.add).then_inc(acc_done, 1)
            dve.wait_ge(sw_mm, NS)
            dve.tensor_copy(sacc[:, 0:PAST], wide(3, PAST, slice(0, SR)))
            dve.tensor_tensor(sacc[:, PAST:SKEYS], ps[0:SR, 5, 0:TS], kf[0:SR, K_NEW:K_NEW + TS], ALU.add
                              ).then_inc(masks_ready, 1)

            dve.memset(s_lo[:, :], 0.0)
            dve.memset(s_hi[:, :], 0.0)
            dve.memset(s_cnt[:, :], 0.0)
            link(dve.tensor_scalar(s_m8[:, :, :], kf[:, K_IOTA:K_IOTA + 8].unsqueeze(1).broadcast_to([P, NSEL + 1, 8]),
                                   -1.0, None, ALU.mult))
            dve.wait_ge(masks_ready, 1)
            for k in range(NSEL + 1):
                work, place, r = select_tile(k)
                dve.tensor_reduce(s_lo[0:r, k:k + 1], work[:, 0:TOPK], AX_X, ALU.min)
                ins = dve.reduce_max(s_hi[0:r, k:k + 1], work, AX_X)
            link(ins)
            link(dve.tensor_tensor(s_up[:, :], s_hi[:, :], s_lo[:, :], ALU.subtract))
            for i in range(HALVINGS):
                ins = dve.tensor_scalar(s_w[:, i, :], s_up[:, :], 0.5 ** (i + 1), None, ALU.mult)
            link(ins)
            dve.tensor_tensor(s_mid[:, :], s_lo[:, :], s_w[:, 0, :], ALU.add).then_inc(sel_mid, 1)
            dve.wait_ge(sel_mid, 1)
            for i in range(HALVINGS):
                for k in COUNT_DVE:
                    work, place, r = select_tile(k)
                    ins = dve.tensor_scalar(place, work, s_mid[0:r, k:k + 1], None, ALU.is_lt, ALU.add,
                                            accum_out=s_cnt[0:r, k:k + 1])
                link(ins)
                dve.wait_ge(sel_cnt, len(COUNT_ACT) * (i + 1))
                link(dve.tensor_tensor(s_few[:, :], s_cnt[:, :], kf[:, K_FEW:K_FEW + NSEL + 1], ALU.is_le))
                dve.scalar_tensor_tensor(s_up[:, :], s_few[:, :], 3.0e38, s_mid[:, :], ALU.mult, ALU.add)
                link(dve.tensor_tensor(s_add[:, :], s_few[:, :], s_w[:, i, :], ALU.mult))
                ins = dve.tensor_tensor(s_hi[:, :], s_hi[:, :], s_up[:, :], ALU.min)
                if i < HALVINGS - 1:
                    link(dve.tensor_tensor(s_lo[:, :], s_lo[:, :], s_add[:, :], ALU.add))
                    dve.tensor_tensor(s_mid[:, :], s_lo[:, :], s_w[:, i + 1, :], ALU.add).then_inc(sel_mid, 1)
                    dve.wait_ge(sel_mid, i + 2)
                else:
                    link(ins)

            dve.wait_ge(head_sq, 1)
            parts = ((slice(0, P), slice(0, SAMPLE)), (slice(0, SR), slice(SAMPLE, NT)))
            for r, t in parts:
                n = (t.stop - t.start) * NKV
                ins = dve.tensor_reduce(hk[r, 0, t.start * NKV:t.stop * NKV],
                                        hsq_k[r, t, :].rearrange("p t (h d) -> p (t h) d", d=HD), AX_X, ALU.add)
            link(ins)
            for r, t in parts:
                h = hk[r, 0, t.start * NKV:t.stop * NKV]
                ins = dve.tensor_scalar(h, h, 1.0 / HD, RMS_EPS, ALU.mult, ALU.add)
            ins.then_inc(head_ms, 1)
            dve.wait_ge(head_rs, 1)
            for r, t in parts:
                n = (t.stop - t.start) * NKV
                x = k_tok[r, t, :].rearrange("p t (h d) -> p (t h) d", d=HD)
                ins = dve.tensor_tensor(x, x, hk[r, 1, t.start * NKV:t.stop * NKV].unsqueeze(2).broadcast_to(
                    [r.stop, n, HD]), ALU.mult)
            link(ins)
            for r, t in parts:
                n = (t.stop - t.start) * NKV
                x = k_tok[r, t, :].rearrange("p t (h d) -> p (t h) d", d=HD)
                ins = dve.tensor_tensor(x, x, kf[r, K_GK:K_GK + HD].unsqueeze(1).broadcast_to([r.stop, n, HD]), ALU.mult)
            link(ins)
            for r, t in parts:
                nt = t.stop - t.start
                cos, sin = (kf[r, c + 16 * t.start:c + 16 * t.stop].rearrange("p (t d) -> p t d", d=16)
                            for c in (K_COS, K_SIN))
                x = k_tok[r, t, :].rearrange("p t (h d) -> p t h d", d=HD)
                t1, t2 = (rt_k[r, i, t.start * NKV * 16:t.stop * NKV * 16].rearrange("p (t h d) -> p t h d", t=nt, h=NKV)
                          for i in range(2))
                for h in range(NKV):
                    dve.tensor_tensor(t1[:, :, h, :], x[:, :, h, 0:16], cos, ALU.mult)
                    dve.tensor_tensor(t2[:, :, h, 0:8], x[:, :, h, 8:16], sin[:, :, 0:8], ALU.mult)
                    ins = dve.tensor_tensor(t2[:, :, h, 8:16], x[:, :, h, 0:8], sin[:, :, 8:16], ALU.mult)
                link(ins)
                for h in range(NKV):
                    ins = dve.tensor_tensor(x[:, :, h, 0:16], t1[:, :, h, :], t2[:, :, h, :], ALU.add)
            ins.then_inc(k_ready, 1)

            def largest_left(k):
                work, place, r = select_tile(k)
                keys = work.shape[1]
                link(dve.tensor_scalar(place, work, s_hi[0:r, k:k + 1], None, ALU.is_gt, ALU.add,
                                       accum_out=s_cnt[0:r, k:k + 1]))
                link(dve.scalar_tensor_tensor(left[0:r, k % 2, 0:keys], place, TAKEN, work, ALU.mult, ALU.add))
                dve.max(s_m8[0:r, k, :], left[0:r, k % 2, 0:keys])

            for o in range(NT):
                t = ALL[o]
                r = rows_of(t)
                x = qst[0:r, o % 3, :].rearrange("p (h d) -> p h d", d=HD)
                dve.wait_ge(proj_evac, BASE[4] + o + 1)
                link(dve.tensor_reduce(hs[0:r, o % 2, :], hsq[0:r, :].rearrange("p (h d) -> p h d", d=HD), AX_X, ALU.add))
                dve.tensor_scalar(hs[0:r, o % 2, :], hs[0:r, o % 2, :], 1.0 / HD, RMS_EPS,
                                  ALU.mult, ALU.add).then_inc(head_ms, 1)
                if o <= NSEL:
                    if o == 0:
                        link(dve.memset(s_cnt[:, :], float(TOPK - 1)))
                        dve.wait_ge(k_ready, 1)
                    largest_left(o)
                dve.wait_ge(head_rs, o + 2)
                link(dve.tensor_tensor(x, x, hs[0:r, 2 + o % 2, :].unsqueeze(2).broadcast_to([r, NH, HD]), ALU.mult))
                link(dve.tensor_tensor(x, x, kf[0:r, K_GQ:K_GQ + HD].unsqueeze(1).broadcast_to([r, NH, HD]), ALU.mult))
                if o > 0:
                    dve.wait_ge(q_ready, o)
                rope_tile(x, t, NH).then_inc(q_ready, 1)

            rank, iota = s_up, kf[:, K_IOTA:K_IOTA + 8].unsqueeze(1).broadcast_to([P, NSEL + 1, 8])
            link(dve.tensor_scalar(rank[:, :], s_cnt[:, :], -1.0, float(TOPK), ALU.mult, ALU.add))
            link(dve.tensor_scalar(s_add[:, :], rank[:, :], -1.0, None, ALU.add))
            dve.tensor_tensor(s_eq[:, 0], iota, s_add[:, :].unsqueeze(2).broadcast_to([P, NSEL + 1, 8]), ALU.is_equal)
            link(dve.tensor_tensor(s_eq[:, 1], iota, rank[:, :].unsqueeze(2).broadcast_to([P, NSEL + 1, 8]), ALU.is_equal))
            for i in range(2):
                ins = dve.tensor_tensor(s_eq[:, i], s_eq[:, i], s_m8[:, :, :], ALU.mult)
            link(ins)
            for i in range(2):
                ins = dve.tensor_reduce(s_thr[:, i], s_eq[:, i], AX_X, ALU.add)
            link(ins)
            dve.tensor_tensor(s_few[:, :], s_thr[:, 1], s_thr[:, 0], ALU.is_ge)
            link(dve.tensor_scalar(s_lo[:, :], rank[:, :], 8.0, None, ALU.is_ge))
            link(dve.tensor_tensor(s_few[:, :], s_few[:, :], s_lo[:, :], ALU.max))
            dve.reduce_max(s_bad[:, :], s_few[:, :], AX_X).then_inc(bad_ready, 1)
            for k in range(NSEL + 1):
                work, place, r = select_tile(k)
                ins = dve.tensor_scalar(place, work, s_thr[0:r, 0, k:k + 1], DROP, ALU.is_lt, ALU.mult)
            link(ins)
            dve.wait_ge(flag_in, 16)
            link(dve.reduce_max(s_row[:, P:P + 1], s_row[:, 0:P], AX_X))
            link(dve.tensor_copy(s_flag[:, :], s_row[:, P:P + 1]))
            again = dve.value_load(s_flag[0:1, 0:1], min_val=0, max_val=1)
            with dve.If(again > 0):
                base = 0
                for k in range(NSEL + 1):
                    work, place, r = select_tile(k)
                    with dve.Fori(0, TOPK // 8) as i:
                        dve.max(m8[0:r, :], work).then_inc(round_done, 1)
                        dve.wait_ge(round_done, 2 * i + (base + 1))
                        dve.sem_inc(fence_dve, 1)
                        dve.match_replace(work, m8[0:r, :], work, TAKEN).then_inc(round_done, 1)
                        dve.wait_ge(round_done, 2 * i + (base + 2))
                    base += 2 * (TOPK // 8) + 1
                    dve.tensor_scalar(place, work, TAKEN, DROP, ALU.not_equal, ALU.mult).then_inc(round_done, 1)
                dve.wait_ge(round_done, base)
            for t in range(FIRST):
                if t > 0:
                    dve.memset(mneg[:, mask_at(t):mask_at(t) + t * P], 0.0)
                dve.tensor_copy(mneg[:, mask_at(t) + t * P:mask_at(t + 1)], kb[:, 0:P]).then_inc(masks_ready, 1)
            link(dve.memset(s_lo[:, :], 0.0))
            dve.sem_inc(masks_ready, 1)

            def conv_taps(first, last):
                for q in range(first, last):
                    ct, j = divmod(q, W)
                    if q == 0:
                        dve.wait_ge(u_state, 16 * CT)
                    if q == 2 * W:
                        dve.wait_ge(kt_ps, 1)
                        dve.wait_ge(stores, 16 * 6)
                    w = kf[:, K_CW + q:K_CW + q + 1]
                    up = u[:, ct, j:j + S]
                    un = u[:, ct, PU + S:].rearrange("p (b w) -> p b w", b=NS)[:, :, j:j + TS]
                    yp, ys = y[:, ct, 0:S], y[:, ct, S:ROWS].rearrange("p (b t) -> p b t", b=NS)
                    if j == 0:
                        bias = kf[:, K_CB + ct:K_CB + ct + 1]
                        dve.tensor_scalar(yp, up, w, bias, ALU.mult, ALU.add).then_inc(tap_done, 1)
                        dve.tensor_scalar(ys, un, w, bias, ALU.mult, ALU.add).then_inc(tap_done, 1)
                    else:
                        dve.wait_ge(tap_done, 2 * q - 1)
                        dve.scalar_tensor_tensor(yp, up, w, yp, ALU.mult, ALU.add).then_inc(tap_done, 1)
                        dve.wait_ge(tap_done, 2 * q)
                        dve.scalar_tensor_tensor(ys, un, w, ys, ALU.mult, ALU.add).then_inc(tap_done, 1)

            for r in range(3):
                dve.wait_ge(q_out[r], 48)
            dve.memset(u[:, :, 0:PU], 0.0)
            for ct in range(CT):
                new = u[:, ct, PU + S:].rearrange("p (b w) -> p b w", b=NS)[:, :, PU:]
                for j, (a, z) in enumerate(BLOCKS):
                    n = 3 * ct + j
                    s = 2 * ct * 3 + j
                    dve.wait_ge(glu_sig, n + 1)
                    if z <= S:
                        ins = dve.tensor_tensor(u[:, ct, PU + a:PU + z], ps[:, s % 8, 0:z - a], sig[:, n % 2, 0:z - a],
                                                ALU.mult)
                    else:
                        dve.tensor_tensor(u[:, ct, PU + a:PU + S], ps[:, s % 8, 0:S - a], sig[:, n % 2, 0:S - a],
                                          ALU.mult)
                        ins = dve.tensor_tensor(new, ps[:, s % 8, S - a:z - a].rearrange("p (b t) -> p b t", b=NS),
                                                sig[:, n % 2, S - a:z - a].rearrange("p (b t) -> p b t", b=NS), ALU.mult)
                    ins.then_inc(glu_mul, 1)
                dve.wait_ge(glu_mul, 3 * ct + 3)
                dve.tensor_copy(u_last[:, ct, 0:PU], u[:, ct, S:S + PU])
                dve.tensor_copy(u_last[:, ct, PU:].rearrange("p (b t) -> p b t", b=NS), new).then_inc(ulast_ready, 1)
                conv_taps(TAP_STOPS[ct], TAP_STOPS[ct + 1])
            NA = NH * (S // P)

            def mask_scores(n):
                i = n // NH
                keys = (i + 1) * P
                dve.wait_ge(qk_done, n + 1)
                if n >= 4:
                    dve.wait_ge(pt_ps, n - 3)
                if n == 0:
                    dve.wait_ge(u_mm, 3 * 2 * CT)
                dve.tensor_tensor_reduce(sm[:, n % 4, 0:keys], wide(2 * (n % 2), keys),
                                         mneg[:, mask_at(i):mask_at(i) + keys], 1.0, -3.0e38, ALU.add, ALU.max,
                                         mx[:, n % 2:n % 2 + 1]).then_inc(sm_done, 1)
                dve.wait_ge(sm_done, n + 1)
                if n >= 16:
                    dve.wait_ge(exp_done, n - 15)
                dve.tensor_scalar(stat[:, 0, n % 16:n % 16 + 1], mx[:, n % 2:n % 2 + 1], -(HD ** -0.5), None, ALU.mult
                                  ).then_inc(nmax, 1)

            def take_weights(n):
                keys = (n // NH + 1) * P
                if keys <= 512:
                    return
                dve.wait_ge(pt_ps, n + 1)
                dve.wait_ge(pv_done, n - 1)
                dve.tensor_copy(pt[:, n % 2, 512:keys], ps[:, 5, 0:keys - 512]).then_inc(pt_dve, 1)

            def outputs(i):
                dve.wait_ge(exp_done, NH * (i + 1))
                link(dve.reciprocal(rinv[:, :], stat[:, 1, i % 2 * NH:(i % 2 + 1) * NH]))
                dve.wait_ge(pv_done, NH * (i + 1))
                if i > 0:
                    dve.wait_ge(ot_ps, i)
                dve.tensor_tensor(o_tok[:, :].rearrange("p (h d) -> p h d", d=HD),
                                  ps[:, 6, :].rearrange("p (h d) -> p h d", d=HD),
                                  rinv[:, :].unsqueeze(2).broadcast_to([P, NH, HD]), ALU.mult).then_inc(o_ready, 1)

            def lows(i):
                dve.wait_ge(mixa_hi, i + 1)
                dve.tensor_tensor(lo_t[:, CT:KT, cols_of(i)], ps[:, 7, :].rearrange("p (j c) -> p j c", j=4),
                                  hi_t[:, CT:KT, cols_of(i)].bitcast(F32), ALU.subtract).then_inc(mixa_lo, 1)

            def layer_norm_step(v):
                k = v // 3
                a, z = BLOCKS[k]
                if v % 3 == 0:
                    dve.wait_ge(mean_mm, k + 1)
                    for ct in range(CT):
                        ins = dve.tensor_tensor(y[:, ct, a:z], y[:, ct, a:z], ps[:, 7, 0:z - a], ALU.subtract)
                    ins.then_inc(yc_ready, 1)
                elif v % 3 == 1:
                    dve.wait_ge(var_mm, k + 1)
                    if k == len(BLOCKS) - 1:
                        dve.tensor_scalar(lnr[0:SR, SAMPLE:NT], ps[0:SR, 7, SAMPLE:NT], LN_EPS, None, ALU.add)
                    full = slice(3 * k, min(3 * k + 3, SAMPLE))
                    dve.tensor_scalar(lnr[:, full], ps[:, 7, full], LN_EPS, None, ALU.add).then_inc(lnv_ready, 1)
                    dve.wait_ge(lnr_ready, k + 1)
                    if k > 0:
                        dve.wait_ge(lnb_mm, k)
                    for t in range(3 * k, 3 * k + 3):
                        r = rows_of(t)
                        ins = dve.tensor_scalar(lnd[0:r, t % 3, 0:r], ident[0:r, 0:r], lnr[0:r, t:t + 1], float(C),
                                                ALU.mult, ALU.mult)
                    ins.then_inc(lnd_ready, 1)
                else:
                    dve.wait_ge(lnb_mm, k + 1)
                    for ct in range(CT):
                        ins = dve.tensor_tensor(y[:, ct, a:z], y[:, ct, a:z], ps[:, 7, 0:z - a], ALU.mult)
                    ins.then_inc(yn_ready, 1)

            def conv_lows(k):
                a, z = BLOCKS[k]
                dve.wait_ge(mixc_hi, k + 1)
                dve.tensor_tensor(lo_t[:, 0:CT, a:z], y[:, :, a:z], hi_t[:, 0:CT, a:z].bitcast(F32), ALU.subtract
                                  ).then_inc(mixc_lo, 1)

            taken = TAP_STOPS[-1]
            weight = [n // NH + 1 if n < CONV_HEADS else 0 for n in range(NA)]
            for n in range(NA + 4):
                if n < NA:
                    mask_scores(n)
                if n >= 2 and n - 2 < NA:
                    take_weights(n - 2)
                if n < NA:
                    until = TAP_STOPS[-1] + -(-(CT * W - TAP_STOPS[-1]) * sum(weight[:n + 1]) // sum(weight))
                    conv_taps(taken, until)
                    taken = until
                if n % NH == 2 and n > NH:
                    outputs(n // NH - 1)
                if n % NH == 4 and n > NH:
                    lows(n // NH - 1)
                if n - 1 in LN_AT:
                    layer_norm_step(LN_AT.index(n - 1))
                if n - 2 in LN_AT[2::3]:
                    conv_lows(LN_AT.index(n - 2) // 3)
            link(dve.memset(q_blk[:, :, :, :], 0.0))
            dve.wait_ge(qt_ready, S // P + 1)
            for h in range(NH):
                kh, pair, j = (h // 2) % 2, h // 4, (h // 4) * 2 + h % 2
                half = slice(kh * HD, (kh + 1) * HD)
                ins = dve.tensor_copy(q_blk[half, :, pair, h * TS:(h + 1) * TS],
                                      q_t[half, 0, j, 0:SR].rearrange("p (b t) -> p b t", b=NS))
            ins.then_inc(qblk_ready, 1)
            if LN_AT[-1] + 2 >= NA + 4:
                conv_lows(len(BLOCKS) - 1)
            lows(S // P - 1)
            for pr in range(NS // 2):
                dve.wait_ge(sqk_done, pr + 1)
                link(dve.reduce_max(mx[:, 0:1], wide(0, SKEYS), AX_X))
                dve.tensor_scalar(stat[:, 0, 0:1], mx[:, 0:1], -(HD ** -0.5), None, ALU.mult).then_inc(smax, 1)
                dve.wait_ge(sexp_done, pr + 1)
                link(dve.reciprocal(rinv[:, 0:1], stat[:, 1, 0:1]))
                dve.wait_ge(spv_done, 2 * pr + 2)
                if pr > 0:
                    dve.wait_ge(sot_ps, pr)
                dve.tensor_scalar(o_s[:, :], ps[:, 6, 0:NKV * HD], rinv[:, 0:1], None, ALU.mult).then_inc(so_ready, 1)
            dve.wait_ge(sot_ready, NS // 2)
            for h in range(NH):
                kh, pair = (h // 2) % 2, h // 4
                src = o_st[kh * HD:(kh + 1) * HD, pair, :, :].rearrange("p a (b c) -> p (a b) c", b=2)
                dst = mix_s[(h % 2) * HD:(h % 2 + 1) * HD, h // 2, :].rearrange("p (b t) -> p b t", b=NS)
                ins = dve.tensor_copy(dst, src[:, :, h * TS:(h + 1) * TS])
            ins.then_inc(mixs_ready, 1)
            dve.wait_ge(mixs_hi, 1)
            dve.tensor_tensor(lo_t[:, CT:KT, cols_of(SAMPLE)], mix_s[:, :, :],
                              hi_t[:, CT:KT, cols_of(SAMPLE)].bitcast(F32), ALU.subtract).then_inc(mixs_lo, 1)
            def norm_x1(o):
                t = ALL[o]
                r = rows_of(t)
                norm_rows(NT + o, x1[0:r, t, :], xn1[0:r, o % NX1, :], gbc1, r, NX1)

            dve.wait_ge(x1_in, 32)
            for n in range(2 * NT):
                t, c = ALL[n % NT], n // NT
                r = rows_of(t)
                dve.wait_ge(proj_done, BASE[5] + n + 1)
                xs = x1[0:r, t, c * 512:(c + 1) * 512]
                dve.tensor_tensor(xs, xs, ps[0:r, 4 if t == SAMPLE else t, :], ALU.add).then_inc(x1_ready, 1)
                if n == NT + 4:
                    dve.wait_ge(g_in, 32)
                    for o in range(5):
                        norm_x1(o)
            for o in range(NT):
                if 5 <= o + 3 < NT:
                    norm_x1(o + 3)
                take_lo(NT + o)
            dve.sem_inc(f_ready, 1)
            dve.sem_inc(y_added, 1)
            with dve.Fori(0, FG) as g:
                for m in range(7):
                    if m < 6:
                        a, z = BLOCKS[m % 3]
                        dve.wait_ge(up_mm, g * 6 + (m + 1))
                        dve.wait_ge(silu_f, g * 6 + (m + 2))
                        if m >= 2:
                            dve.wait_ge(f_hi_ready, g * 6 + (m - 1))
                            dve.wait_ge(f_lo_ready, g * 6 + (m - 1))
                        dve.tensor_tensor(ff[:, m % 2, 0:z - a], ps[:, 3 + m % 3, 0:z - a], sg[:, m % 2, 0:z - a],
                                          ALU.mult).then_inc(f_ready, 1)
                    if m > 0:
                        c, j = divmod(m - 1, 3)
                        a, z = BLOCKS[j]
                        dve.wait_ge(f_hi_ready, g * 6 + m)
                        dve.tensor_tensor(f_lo[:, c, a:z], ff[:, (m - 1) % 2, 0:z - a], f_hi[:, c, a:z].bitcast(F32),
                                          ALU.subtract).then_inc(f_lo_ready, 1)
                dve.wait_ge(y_added, g * (2 * NT) + 1)
                for t in range(NT):
                    r = rows_of(t)
                    for nh in range(2):
                        dve.wait_ge(down_mm, g * (2 * NT) + (2 * t + nh + 2))
                        xs = x1[0:r, t, nh * 512:(nh + 1) * 512]
                        dve.tensor_tensor(xs, xs, ps[0:r, 6 + nh, :], ALU.add).then_inc(y_added, 1)

_OUTS = [
    ("y_prompt", (S, D), (1, S, D)), ("y_sample", (SR, D), (NS, TS, D)),
    ("k_prompt", (S, NKV * HD), (1, 1, S, NKV, HD)), ("v_prompt", (S, NKV * HD), (1, 1, S, NKV, HD)),
    ("ki_prompt", (S, ID), (1, 1, S, ID)), ("conv_prompt", (W - 1, C), (1, 1, W - 1, C)),
    ("k_sample", (SR, NKV * HD), (1, NS, TS, NKV, HD)), ("v_sample", (NS, TS, NKV * HD), (1, NS, TS, NKV, HD)),
    ("ki_sample", (SR, ID), (1, NS, TS, ID)), ("conv_sample", (NS, W - 1, C), (1, NS, W - 1, C)),
]

def kernel(**inputs):
    import ml_dtypes
    import concourse.bacc as bacc
    from concourse.bass_utils import run_bass_kernel_spmd

    a = {k: np.asarray(v) for k, v in inputs.items()}
    pool = a["cache_k"].shape[1]
    f, b = shape_constants()

    def spread(row, at, kf):
        kf[:, at:at + row.size] = row.reshape(1, -1)

    def by_channel(x):
        return x.reshape(-1, CT, P).transpose(2, 1, 0).reshape(P, -1)

    spread(a["q_norm_g"][0], K_GQ, f)
    spread(a["k_norm_g"][0], K_GK, f)
    f[:, K_CW:K_CB] = by_channel(a["conv_dw_w"][0])
    f[:, K_CB:K_LG] = by_channel(a["conv_dw_b"][0])
    f[:, K_LG:K_LB] = by_channel(a["conv_ln_g"][0])
    f[:, K_LB:K_IOTA] = by_channel(a["conv_ln_b"][0])
    arrays = {
        "x_prompt": a["x_prompt"][0], "x_sample": a["x_sample"].reshape(SR, D),
        "cache_kt": a["cache_k"][0].reshape(pool, PAGE, NKV * HD).transpose(0, 2, 1),
        "cache_v": a["cache_v"][0].reshape(pool, PAGE, NKV * HD),
        "cache_it": a["cache_idx_k"][0].transpose(0, 2, 1),
        "state_t": a["state_conv"][0].transpose(2, 0, 1), "state": a["state_conv"][0],
        "page_table": a["page_table"].reshape(1, -1),
        "attn_norm_g": a["attn_norm_g"], "ffn_norm_g": a["ffn_norm_g"],
        "w_in": a["w_in"][0], "w_out": a["w_out"][0], "w_gate": a["w_gate"][0], "w_up": a["w_up"][0],
        "w_down": a["w_down"][0], "kf": f, "kb": b.astype(ml_dtypes.bfloat16),
    }
    arrays = {k: np.ascontiguousarray(v) for k, v in arrays.items()}
    nc = bacc.Bacc("TRN2", target_bir_lowering=False, num_devices=1)
    A = {k: nc.dram_tensor(f"in_{k}", v.shape, mybir.dt.from_np(v.dtype), kind="ExternalInput").ap()
         for k, v in arrays.items()}
    O = {k: nc.dram_tensor(f"out_{k}", s, F32, kind="ExternalOutput").ap() for k, s, _ in _OUTS}
    decoder_program(nc, A, O)
    r = run_bass_kernel_spmd(nc, [{f"in_{k}": v for k, v in arrays.items()}], core_ids=[0])
    return tuple(r.results[0][f"out_{k}"].reshape(shape) for k, _, shape in _OUTS)
```
